# Optimizing a Trainium2 kernel written in Bass

```python
import jax, jax.numpy as jnp
from jax import lax
import numpy as np

D_MODEL = 1024
BATCH = 1
SEQ = 512
DEPTH = 1
DEC_BATCH = 1
DEC_SEQ = 64
PAST_LEN = 512

CHUNK = 64
N_META = 16
RET_HEADS = 4
RET_DK = 64
RET_DV = 128
SWA_HEADS = 8
SWA_KV_HEADS = 2
SWA_HD = 64
WINDOW = 128
ROPE_THETA = 10000.0
N_GROUPS = 4
EXPERTS_PER_GROUP = 8
N_EXPERTS = N_GROUPS * EXPERTS_PER_GROUP
TOP_K_IN_GROUP = 2
EXPERT_FF = 256
EPS = 1e-6
NEG_INF = -1e30
RET_Q = RET_HEADS * RET_DK
RET_V = RET_HEADS * RET_DV
SWA_Q = SWA_HEADS * SWA_HD
SWA_KV = SWA_KV_HEADS * SWA_HD
MIX_WIDTH = RET_V + SWA_Q
IN_WIDTH = 2 * RET_Q + 2 * RET_V + SWA_Q + 2 * SWA_KV
SPLIT_POINTS = (RET_Q, 2 * RET_Q, 2 * RET_Q + RET_V, 2 * RET_Q + 2 * RET_V,
                2 * RET_Q + 2 * RET_V + SWA_Q, 2 * RET_Q + 2 * RET_V + SWA_Q + SWA_KV)

kernel_name = "hymba_retention_swa_hmoe_stream_step"

def rmsnorm(x, g):
    xf = x.astype(jnp.float32)
    y = xf * lax.rsqrt(jnp.mean(xf * xf, axis=-1, keepdims=True) + EPS)
    return (y * g.astype(jnp.float32)).astype(x.dtype)

def rope(x, pos):
    half = x.shape[-1] // 2
    inv = ROPE_THETA ** (-jnp.arange(half, dtype=jnp.float32) / half)
    ang = pos.astype(jnp.float32)[:, None] * inv[None, :]
    cos = jnp.cos(ang)[:, None, :]
    sin = jnp.sin(ang)[:, None, :]
    xf = x.astype(jnp.float32)
    x1, x2 = xf[..., :half], xf[..., half:]
    return jnp.concatenate([x1 * cos - x2 * sin, x2 * cos + x1 * sin], axis=-1).astype(x.dtype)

def ret_log_decay():
    return jnp.log1p(-jnp.exp2(-5.0 - jnp.arange(RET_HEADS, dtype=jnp.float32)))

def retention_output(q, k, v, S):
    c = q.shape[1]
    log_g = ret_log_decay()
    i = jnp.arange(c, dtype=jnp.float32)
    diff = i[:, None] - i[None, :]
    decay = jnp.where(diff[None] >= 0, jnp.exp(jnp.maximum(diff, 0.0)[None] * log_g[:, None, None]), 0.0)
    intra = jnp.einsum('bihd,bjhd->bhij', q, k) * decay.astype(q.dtype)[None]
    o = jnp.einsum('bhij,bjhe->bihe', intra, v)
    cross_scale = jnp.exp((i + 1.0)[:, None] * log_g[None, :]).astype(q.dtype)
    cross = jnp.einsum('bihd,bhde->bihe', q, S.astype(q.dtype)) * cross_scale[None, :, :, None]
    return o + cross

def retention_update(k, v, S):
    c = k.shape[1]
    log_g = ret_log_decay()
    i = jnp.arange(c, dtype=jnp.float32)
    w = jnp.exp((c - 1.0 - i)[:, None] * log_g[None, :]).astype(k.dtype)
    kw = k * w[None, :, :, None]
    full = jnp.exp(c * log_g)[None, :, None, None]
    S_new = full * S.astype(jnp.float32) + jnp.einsum('bjhd,bjhe->bhde', kw, v).astype(jnp.float32)
    return S_new.astype(S.dtype)

def to_chunks(t, n, c):
    return jnp.moveaxis(t.reshape((t.shape[0], n, c) + t.shape[2:]), 1, 0)

def project(xn, w_in, q_norm_g, k_norm_g, pos):
    b, l, _ = xn.shape
    h = xn @ w_in
    rq, rk, rv, rg, sq, sk, sv = jnp.split(h, SPLIT_POINTS, axis=-1)
    rq = rope(rq.reshape(b, l, RET_HEADS, RET_DK), pos)
    rk = rope(rk.reshape(b, l, RET_HEADS, RET_DK), pos) * (RET_DK ** -0.5)
    rv = rv.reshape(b, l, RET_HEADS, RET_DV)
    sq = rope(rmsnorm(sq.reshape(b, l, SWA_HEADS, SWA_HD), q_norm_g), pos)
    sk = rope(rmsnorm(sk.reshape(b, l, SWA_KV_HEADS, SWA_HD), k_norm_g), pos)
    sv = sv.reshape(b, l, SWA_KV_HEADS, SWA_HD)
    return rq, rk, rv, rg, sq, sk, sv

def swa_attention(q, k_full, v_full, valid, meta_k, meta_v, has_meta, sinks, c):
    b, l, h, d = q.shape
    n = l // c
    s = WINDOW + c
    g = h // SWA_KV_HEADS
    idx = jnp.arange(n)[:, None] * c + jnp.arange(s)[None, :]
    kb = k_full[:, idx]
    vb = v_full[:, idx]
    band_ok = valid[idx]
    meta_ok = jnp.full((N_META,), has_meta)
    qb = q.reshape(b, n, c, SWA_KV_HEADS, g, d)
    scale = d ** -0.5
    s_meta = jnp.einsum('bnqkgd,mkd->bnkgqm', qb, meta_k).astype(jnp.float32) * scale
    s_band = jnp.einsum('bnqkgd,bnskd->bnkgqs', qb, kb).astype(jnp.float32) * scale
    s_meta = jnp.where(meta_ok[None, None, None, None, None, :], s_meta, NEG_INF)
    s_band = jnp.where(band_ok[None, :, None, None, None, :], s_band, NEG_INF)
    sink = jnp.broadcast_to(sinks.astype(jnp.float32).reshape(SWA_KV_HEADS, g)[None, None, :, :, None, None],
                            (b, n, SWA_KV_HEADS, g, c, 1))
    p = jax.nn.softmax(jnp.concatenate([s_meta, s_band, sink], axis=-1), axis=-1)
    p_meta = p[..., :N_META].astype(v_full.dtype)
    p_band = p[..., N_META:N_META + s].astype(v_full.dtype)
    o = (jnp.einsum('bnkgqm,mkd->bnqkgd', p_meta, meta_v)
         + jnp.einsum('bnkgqs,bnskd->bnqkgd', p_band, vb))
    return o.reshape(b, l, h * d)

def hier_moe(hn, w_group, w_expert, w_gate, w_up, w_down):
    b, l, d = hn.shape
    t = hn.reshape(-1, d)
    pg = jax.nn.softmax((t @ w_group).astype(jnp.float32), axis=-1)
    g_sel = jnp.argmax(pg, axis=-1)
    p_sel = jnp.take_along_axis(pg, g_sel[:, None], axis=-1)
    el = (t @ w_expert).astype(jnp.float32).reshape(-1, N_GROUPS, EXPERTS_PER_GROUP)
    el_sel = jnp.take_along_axis(el, g_sel[:, None, None], axis=1)[:, 0]
    top_p, top_i = lax.top_k(jax.nn.softmax(el_sel, axis=-1), TOP_K_IN_GROUP)
    w = p_sel * top_p / jnp.sum(top_p, axis=-1, keepdims=True)
    eid = g_sel[:, None] * EXPERTS_PER_GROUP + top_i
    comb = jnp.sum(jax.nn.one_hot(eid, N_EXPERTS, dtype=jnp.float32) * w[..., None], axis=1)
    out = jnp.zeros(t.shape, jnp.float32)
    for e in range(N_EXPERTS):
        a = jax.nn.silu(t @ w_gate[e]) * (t @ w_up[e])
        out = out + comb[:, e:e + 1] * (a @ w_down[e]).astype(jnp.float32)
    return out.astype(hn.dtype).reshape(b, l, d)

def layer_forward(x, pos, ret_s0, hist_k, hist_v, has_hist, meta_k, meta_v, has_meta,
                  norm1_g, w_in, q_norm_g, k_norm_g, ret_norm_g, attn_sinks, w_out,
                  norm2_g, w_group, w_expert, w_gate, w_up, w_down):
    b, l, _ = x.shape
    rq, rk, rv, rg, sq, sk, sv = project(rmsnorm(x, norm1_g), w_in, q_norm_g, k_norm_g, pos)
    c = min(CHUNK, l)
    n = l // c
    def body(S, qkv):
        q_c, k_c, v_c = qkv
        return retention_update(k_c, v_c, S), retention_output(q_c, k_c, v_c, S)
    ret_s, o_r = lax.scan(body, ret_s0, (to_chunks(rq, n, c), to_chunks(rk, n, c), to_chunks(rv, n, c)))
    o_r = jnp.moveaxis(o_r, 0, 1).reshape(b, l, RET_HEADS, RET_DV)
    o_r = rmsnorm(o_r, ret_norm_g.reshape(RET_HEADS, RET_DV)).reshape(b, l, RET_V) * jax.nn.silu(rg)
    k_full = jnp.concatenate([hist_k, sk], axis=1)
    v_full = jnp.concatenate([hist_v, sv], axis=1)
    valid = jnp.concatenate([jnp.full((WINDOW,), has_hist), jnp.ones((l,), dtype=bool)])
    o_s = swa_attention(sq, k_full, v_full, valid, meta_k, meta_v, has_meta, attn_sinks, c)
    x = x + jnp.concatenate([o_r, o_s], axis=-1) @ w_out
    x = x + hier_moe(rmsnorm(x, norm2_g), w_group, w_expert, w_gate, w_up, w_down)
    return x, ret_s, k_full[:, -WINDOW:], v_full[:, -WINDOW:]

def setup_inputs(seed: int = 0) -> dict:
    key = jax.random.key(seed)
    ks = jax.random.split(key, 20)

    def nrm(k, shape, scale):
        return jax.random.normal(k, shape, jnp.float32) * scale

    return {
        "x_prompt": nrm(ks[0], (BATCH, SEQ, D_MODEL), 1.0),
        "x_sample": nrm(ks[1], (DEC_BATCH, DEC_SEQ, D_MODEL), 1.0),
        "cache_ret_state": nrm(ks[2], (DEPTH, DEC_BATCH, RET_HEADS, RET_DK, RET_DV), 0.1),
        "cache_swa_k": nrm(ks[3], (DEPTH, DEC_BATCH, WINDOW, SWA_KV_HEADS, SWA_HD), 1.0),
        "cache_swa_v": nrm(ks[4], (DEPTH, DEC_BATCH, WINDOW, SWA_KV_HEADS, SWA_HD), 1.0),
        "meta_tokens": nrm(ks[5], (N_META, D_MODEL), 1.0),
        "norm1_g": 1.0 + nrm(ks[6], (DEPTH, D_MODEL), 0.01),
        "w_in": nrm(ks[7], (DEPTH, D_MODEL, IN_WIDTH), D_MODEL ** -0.5),
        "q_norm_g": 1.0 + nrm(ks[8], (DEPTH, SWA_HD), 0.01),
        "k_norm_g": 1.0 + nrm(ks[9], (DEPTH, SWA_HD), 0.01),
        "ret_norm_g": 1.0 + nrm(ks[10], (DEPTH, RET_V), 0.01),
        "attn_sinks": nrm(ks[11], (DEPTH, SWA_HEADS), 0.5),
        "w_out": nrm(ks[12], (DEPTH, MIX_WIDTH, D_MODEL), MIX_WIDTH ** -0.5),
        "norm2_g": 1.0 + nrm(ks[13], (DEPTH, D_MODEL), 0.01),
        "w_group": nrm(ks[14], (DEPTH, D_MODEL, N_GROUPS), D_MODEL ** -0.5),
        "w_expert": nrm(ks[15], (DEPTH, D_MODEL, N_EXPERTS), D_MODEL ** -0.5),
        "w_gate": nrm(ks[16], (DEPTH, N_EXPERTS, D_MODEL, EXPERT_FF), D_MODEL ** -0.5),
        "w_up": nrm(ks[17], (DEPTH, N_EXPERTS, D_MODEL, EXPERT_FF), D_MODEL ** -0.5),
        "w_down": nrm(ks[18], (DEPTH, N_EXPERTS, EXPERT_FF, D_MODEL), EXPERT_FF ** -0.5),
    }

def reference(x_prompt, x_sample, cache_ret_state, cache_swa_k, cache_swa_v, meta_tokens,
              norm1_g, w_in, q_norm_g, k_norm_g, ret_norm_g, attn_sinks, w_out, norm2_g,
              w_group, w_expert, w_gate, w_up, w_down):
    b = x_prompt.shape[0]
    meta_pos = jnp.arange(N_META, dtype=jnp.int32)
    prompt_pos = N_META + jnp.arange(x_prompt.shape[1], dtype=jnp.int32)
    sample_pos = N_META + PAST_LEN + jnp.arange(x_sample.shape[1], dtype=jnp.int32)
    xp, xs, m = x_prompt, x_sample, meta_tokens[None]
    rs_p, k_p, v_p, rs_s, k_s, v_s = [], [], [], [], [], []
    for layer in range(DEPTH):
        lw = (norm1_g[layer], w_in[layer], q_norm_g[layer], k_norm_g[layer], ret_norm_g[layer],
              attn_sinks[layer], w_out[layer], norm2_g[layer], w_group[layer], w_expert[layer],
              w_gate[layer], w_up[layer], w_down[layer])
        ret_zero = jnp.zeros((1, RET_HEADS, RET_DK, RET_DV), m.dtype)
        _, m_rk, m_rv, _, _, m_sk, m_sv = project(rmsnorm(m, lw[0]), lw[1], lw[2], lw[3], meta_pos)
        s_meta = retention_update(m_rk, m_rv, ret_zero)
        meta_k, meta_v = m_sk[0], m_sv[0]
        hist0 = jnp.zeros((b, WINDOW, SWA_KV_HEADS, SWA_HD), xp.dtype)
        s0 = jnp.broadcast_to(s_meta, (b,) + s_meta.shape[1:])
        xp, sp, kp, vp = layer_forward(xp, prompt_pos, s0, hist0, hist0, False,
                                       meta_k, meta_v, True, *lw)
        xs, ss, ksn, vsn = layer_forward(xs, sample_pos, cache_ret_state[layer], cache_swa_k[layer],
                                         cache_swa_v[layer], True, meta_k, meta_v, True, *lw)
        if layer + 1 < DEPTH:
            mz = jnp.zeros((1, WINDOW, SWA_KV_HEADS, SWA_HD), m.dtype)
            m = layer_forward(m, meta_pos, ret_zero, mz, mz, False, jnp.zeros_like(meta_k),
                              jnp.zeros_like(meta_v), False, *lw)[0]
        rs_p.append(sp)
        k_p.append(kp)
        v_p.append(vp)
        rs_s.append(ss)
        k_s.append(ksn)
        v_s.append(vsn)
    return (xp, xs, jnp.stack(rs_p), jnp.stack(k_p), jnp.stack(v_p),
            jnp.stack(rs_s), jnp.stack(k_s), jnp.stack(v_s))


_drawn_inputs = setup_inputs


def setup_inputs(seed=0):
    import zlib

    import numpy as np

    out = dict(_drawn_inputs(seed))
    spreads = {}
    factors = {'norm1_g': 3.028,
     'q_norm_g': 8.0,
     'k_norm_g': 5.223,
     'ret_norm_g': 2.754,
     'attn_sinks': 8.0,
     'norm2_g': 3.124}
    for name, (base, spread) in spreads.items():
        noise = np.random.default_rng([zlib.crc32(name.encode()), seed]).standard_normal(out[name].shape)
        drawn = base * np.exp(spread * noise) if base else spread * noise
        out[name] = __import__('jax').numpy.asarray(drawn.astype(out[name].dtype))
    for name, factor in factors.items():
        out[name] = (out[name] * factor).astype(out[name].dtype)
    return out
```

```python
from contextlib import ExitStack

import numpy as np

import concourse.bass as bass
from concourse import mybir

ALU = mybir.AluOpType
ACT = mybir.ActivationFunctionType
F32 = mybir.dt.float32
F32R = mybir.dt.float32r
I32 = mybir.dt.int32
AX_X = mybir.AxisListType.X

P = 128
D = 1024
KD = D // P
SEQ, DEC, NMETA = 512, 64, 16
T_TOK = SEQ + DEC
T_ALL = T_TOK + NMETA
NT = 5
TAIL = 4
CH = 64
PAST = 512
RH, RDK, RDV = 4, 64, 128
QH, HD = 8, 64
WINDOW = 128
BAND = WINDOW + CH
KEYS = BAND + NMETA
CACHE0 = T_ALL
NG, EPG = 4, 8
NE = NG * EPG
NPAIR = NE // 2
FF = 256
CAP = 64
LEVELS = T_TOK // CAP
PER_LEVEL = 17
EPS = 1e-6
NEG = -1e30
OFF = 64.0

C_RQK, C_RV, C_RG, C_SQ, C_SKV = 0, 512, 1024, 1536, 2048
CHUNKS = [(C_SKV, 256), (C_SQ, 512), (C_RQK, 512), (C_RV, 512), (C_RG, 512)]
SKV, SQ, RQK, RV, RG = range(5)
RING = 4
OUT_K = [4, 5, 6, 7, 0, 1, 2, 3]


def rows_of(t):
    return P if t < TAIL else DEC + NMETA


def out_rows(t):
    return P if t < TAIL else DEC


def constants():
    p = np.arange(P)
    at, cols = {}, []

    def put(name, a):
        a = np.asarray(a, np.float32).reshape(P, -1)
        lo = sum(c.shape[1] for c in cols)
        at[name] = (lo, lo + a.shape[1])
        cols.append(a)

    put("ident", np.eye(P))
    put("causal", p[None, :] >= p[:, None])
    put("before", p[:, None] < p[None, :])
    put("ones", np.ones((P, P)))
    put("iota", np.tile(p, (P, 1)))
    pos = np.zeros((NT, P), np.float32)
    for t in range(TAIL):
        pos[t] = NMETA + P * t + p
    pos[TAIL, :DEC] = NMETA + PAST + np.arange(DEC)
    pos[TAIL, DEC:DEC + NMETA] = np.arange(NMETA)
    half = HD // 2
    inv = np.float32(10000.0) ** (-np.arange(half, dtype=np.float32) / np.float32(half))
    ang = pos[:, :, None] * inv
    cos, sin = np.cos(ang), np.sin(ang)
    put("cos", np.concatenate([cos, cos], -1).transpose(1, 0, 2))
    put("sin", np.concatenate([-sin, sin], -1).transpose(1, 0, 2))
    gamma = 1.0 - 2.0 ** (-5.0 - np.arange(RH))
    step = np.stack([p, np.where(p < DEC, p, p - DEC)], 0)[..., None] + 1.0
    q_scale = gamma ** step
    k_scale = gamma ** -step * RDK ** -0.5
    put("ret_scale", np.concatenate([q_scale, k_scale], -1).transpose(1, 0, 2))
    head = 2 * np.arange(2)[None, :] + (p[:, None] >= 64)
    put("decay", np.stack([gamma[head] ** n for n in (P, DEC, NMETA)], 1))
    tok = np.arange(NT)[None, :] * P + p[:, None]
    put("token", np.where(tok < T_TOK, tok, 0))
    put("expert_row0", np.tile(np.arange(NE) * CAP, (P, 1)))
    put("pair_row0", np.tile(np.arange(NE) % 2 * CAP, (P, 1)))
    return np.ascontiguousarray(np.concatenate(cols, 1)), at


def stream_step(nc, consts, x_prompt, x_sample, cache_ret_state, cache_swa_k, cache_swa_v,
                meta_tokens, norm1_g, w_in, q_norm_g, k_norm_g, ret_norm_g, attn_sinks, w_out,
                norm2_g, w_group, w_expert, w_gate, w_up, w_down,
                y_prompt, y_sample, ret_prompt, k_prompt, v_prompt, ret_sample, k_sample,
                v_sample):
    _, at = constants()
    NCONST = consts.shape[1]

    hn_d = nc.dram_tensor("hn_d", [T_TOK, D], F32, kind="Internal").ap()
    y_d = nc.dram_tensor("y_d", [LEVELS * NE * CAP, D], F32, kind="Internal").ap()
    y_pairs = y_d.rearrange("(q r) d -> q r d", r=2 * CAP)

    w_in_v = w_in.rearrange("o (p k) n -> p (o k) n", p=P)
    w_out_v = w_out.rearrange("o (k p) n -> p (o k) n", p=P)
    gate_v = w_gate.rearrange("o e (p k) f -> (o e) p (k f)", p=P)
    up_v = w_up.rearrange("o e (p k) f -> (o e) p (k f)", p=P)
    down_v = w_down.rearrange("o e (p j) n -> (o e) p (j n)", p=P)

    with ExitStack() as ctx:
        def sb(name, shape, dt=F32):
            return ctx.enter_context(nc.sbuf_tensor(name, shape, dt))

        def sem(name):
            return ctx.enter_context(nc.semaphore(name))

        cst = sb("cst", [P, NCONST])

        def const(name, rows=P):
            return cst[0:rows, at[name][0]:at[name][1]]

        ident, iota, ones = const("ident"), const("iota"), const("ones")
        cos_t = const("cos").rearrange("p (t d) -> p t d", t=NT)
        sin_t = const("sin").rearrange("p (t d) -> p t d", t=NT)
        ret_scale = const("ret_scale").rearrange("p (a h) -> p a h", a=2)
        decay = const("decay").rearrange("p (a h) -> p a h", a=3)
        x_sb = sb("x_sb", [P, NT, D])
        g1T = sb("g1T", [P, KD])
        g2T = sb("g2T", [P, KD])
        retgT = sb("retgT", [P, RH])
        qk_g = sb("qk_g", [P, 2, HD])
        sinks = sb("sinks", [P, QH])
        w_router = sb("w_router", [P, KD, NG + NE])
        small = sb("small", [P, 160])
        ms = sb("ms", [P, 8])
        root = sb("root", [P, 4, 8])
        rstd = sb("rstd", [P, 8])
        rstd1 = sb("rstd1", [P, NT])
        ssq = sb("ssq", [P, 8])
        state_p = sb("state_p", [P, 2, RDV])
        state_s = sb("state_s", [P, 2, RDV])
        state_tmp = sb("state_tmp", [P, 2, RDV])

        attn = ExitStack()

        def sba(name, shape, dt=F32):
            return attn.enter_context(nc.sbuf_tensor(name, shape, dt))

        rope_g = sba("rope_g", [P, 2, 2, NT, HD])
        rqk = sba("rqk", [P, NT, 512])
        rv = sba("rv", [P, NT, 512])
        gate = sba("gate", [P, NT, 512])
        sq = sba("sq", [P, NT, 4, 2, HD])
        sk = sba("sk", [P, NT, P])
        sv = sba("sv", [P, NT, P])
        rT = sba("rT", [P, 4, T_ALL])
        sqT = sba("sqT", [P, 4, T_ALL])
        skT = sba("skT", [P, T_ALL + WINDOW])
        cache_k = sba("cache_k", [P, P])
        cache_v = sba("cache_v", [P, P])
        v_shift = sba("v_shift", [P, 4, P])
        v_own = sba("v_own", [P, 8, P])
        h_raw = sba("h_raw", [P, NT, 512])
        h_a = sba("h_a", [P, 512])
        h_b = sba("h_b", [P, 512])
        h_sq = sba("h_sq", [P, 512])
        probs = sba("probs", [P, 4, KEYS])
        probsT = sba("probsT", [P, 2, 4, P])
        ret_aT = sba("ret_aT", [P, 4, P])
        o_rows = sba("o_rows", [P, 4, P])
        xT_hi = sba("xT_hi", [P, KD, T_ALL], F32R)
        xT_lo = sba("xT_lo", [P, KD, T_ALL], F32R)
        w_raw = sba("w_raw", [P, RING, 512])
        w_hi = sba("w_hi", [P, RING, 512], F32R)
        w_lo = sba("w_lo", [P, RING, 512], F32R)
        part = sba("part", [P, 2, 4, P])
        attn.close()

        w_moe = sb("w_moe", [P, 2, 2, 3, KD * FF])
        rows = sb("rows", [P, 2, D])
        xg = rows
        hnT = sb("hnT", [P, KD, P])
        logits = sb("logits", [P, NT, NG + NE])
        r4 = sb("r4", [P, NT, NG])
        r4b = sb("r4b", [P, NT, NG])
        oh_g = sb("oh_g", [P, NT, NG])
        r32 = sb("r32", [P, NT, NG, EPG])
        el = sb("el", [P, NT, EPG])
        el2 = sb("el2", [P, NT, EPG])
        cand = sb("cand", [P, NT, EPG])
        oh_e = sb("oh_e", [P, 2, NT, EPG])
        oh = sb("oh", [P, 2, NT, NE])
        chosen = sb("chosen", [P, NT, NE])
        rank = sb("rank", [P, NT, NE])
        tmp_k = sb("tmp_k", [P, 2, NT, NE])
        rank_k = sb("rank_k", [P, 2 * NT])
        row_k = sb("row_k", [P, 2 * NT])
        row_l = sb("row_l", [P, 2 * NT])
        lvl_a = sb("lvl_a", [P, 2 * NT])
        lvl_b = sb("lvl_b", [P, 2 * NT])
        level0 = sb("level0", [P, 1])
        slot_f = sb("slot_f", [P, 2 * NT])
        slot_i = sb("slot_i", [P, 2 * NT], I32)
        pair_tok = sb("pair_tok", [P, 2 * NT, NPAIR])
        row_oh = sb("row_oh", [P, 2 * NT, P])
        idx = sb("idx", [P, NPAIR], I32)
        idx_now = sb("idx_now", [P, 2, 1], I32)
        most = sb("most", [P, 1])
        most_i = sb("most_i", [P, 1], I32)
        w_k = sb("w_k", [P, 2, NT])
        xgT = sb("xgT", [P, 2, KD, P])
        glu = sb("glu", [P, 3, FF])
        actv = sb("actv", [P, FF])
        actT = sb("actT", [P, 2, P])
        y_sb = sb("y_sb", [P, 2, D])
        y_tok = w_moe[:, 0].rearrange("p e m n -> p (e m n)")[:, 0:2 * NT * D].rearrange(
            "p (t k d) -> p t k d", t=NT, k=2)

        acc = ctx.enter_context(nc.psum_tensor("acc", [P, NT, 512], F32))
        side = ctx.enter_context(nc.psum_tensor("side", [P, 2, 2, 256], F32))
        side3 = ctx.enter_context(nc.psum_tensor("side3", [P, 512], F32))
        side4 = side[:, :, :, :].rearrange("p b h n -> p (b h) n")
        sideb = side[:, :, :, :].rearrange("p b h n -> p b (h n)")

        c_in = sem("c_in")
        x_in = [sem(f"x_in{t}") for t in range(NT)]
        g_in = sem("g_in")
        kv_in = sem("kv_in")
        raw_in = [sem(f"raw_in{s}") for s in range(RING)]
        hi_done = sem("hi_done")
        split = sem("split")
        piece_used = sem("piece_used")
        xt_ps = sem("xt_ps")
        xt_part = sem("xt_part")
        xt_hi = sem("xt_hi")
        xt_lo = sem("xt_lo")
        pool_pass = sem("pool_pass")
        ssq_clear = sem("ssq_clear")
        acc_done = sem("acc_done")
        acc_free = sem("acc_free")
        ms_ready = sem("ms_ready")
        root_ready = sem("root_ready")
        rstd_ready = sem("rstd_ready")
        act_step = sem("act_step")
        dve_step = sem("dve_step")
        raw_q = sem("raw_q")
        raw_sq = sem("raw_sq")
        raw_sq_used = sem("raw_sq_used")
        raw_q_used = sem("raw_q_used")
        v_rows = sem("v_rows")
        qk_rows = sem("qk_rows")
        gate_z = sem("gate_z")
        gate_rows = sem("gate_rows")
        shift_in = sem("shift_in")
        vmeta = sem("vmeta")
        t_ps = sem("t_ps")
        qT_ev = sem("qT_ev")
        kT_ev = sem("kT_ev")
        rT_ev = sem("rT_ev")
        s_ps = sem("s_ps")
        s_max = sem("s_max")
        s_exp = sem("s_exp")
        s_prob = sem("s_prob")
        pT_ps = sem("pT_ps")
        pT_a = sem("pT_a")
        pT_c = sem("pT_c")
        o_ps = sem("o_ps")
        o_hi = sem("o_hi")
        o_lo = sem("o_lo")
        st_ps = sem("st_ps")
        st_new = sem("st_new")
        ra_ps = sem("ra_ps")
        ra_ev = sem("ra_ev")
        ro_part = sem("ro_part")
        ro_cross = sem("ro_cross")
        ro_ps = sem("ro_ps")
        ro_sq = sem("ro_sq")
        ro_rows = sem("ro_rows")
        rm_ps = sem("rm_ps")
        rm_part = sem("rm_part")
        rm_hi = sem("rm_hi")
        rm_lo = sem("rm_lo")
        x2_done = sem("x2_done")
        sq2 = sem("sq2")
        rstd2 = sem("rstd2")
        hn_rows = sem("hn_rows")
        hn_out = [sem(f"hn_out{b}") for b in range(2)]
        hT_ps = sem("hT_ps")
        hT_ev = sem("hT_ev")
        lg_ps = sem("lg_ps")
        lg_ev = sem("lg_ev")
        r_exp = sem("r_exp")
        r_expd = sem("r_expd")
        m_ready = sem("m_ready")
        rank_ps = sem("rank_ps")
        oh_ready = sem("oh_ready")
        idx_ps = sem("idx_ps")
        idx_ready = sem("idx_ready")
        slots_ready = sem("slots_ready")
        gu_in = [sem(f"gu_in{u}") for u in range(2)]
        dn_in = [sem(f"dn_in{u}") for u in range(2)]
        idx_c = sem("idx_c")
        xg_in = [sem(f"xg_in{u}") for u in range(2)]
        xg_ps = sem("xg_ps")
        xg_ev = sem("xg_ev")
        gu_ps = sem("gu_ps")
        e_exp = sem("e_exp")
        e_act = sem("e_act")
        aT_ps = sem("aT_ps")
        aT_ev = sem("aT_ev")
        y_ps = sem("y_ps")
        y_ev = sem("y_ev")
        y_out = [sem(f"y_out{u}") for u in range(2)]
        L_idx = sem("L_idx")
        L_col = sem("L_col")
        L_w = sem("L_w")
        L_xg = sem("L_xg")
        L_xt = sem("L_xt")
        L_xe = sem("L_xe")
        L_gu = sem("L_gu")
        L_ex = sem("L_ex")
        L_act = sem("L_act")
        L_at = sem("L_at")
        L_ae = sem("L_ae")
        L_y = sem("L_y")
        L_ye = sem("L_ye")
        L_out = sem("L_out")
        L_step = sem("L_step")
        glu_step = sem("glu_step")
        L_oh = sem("L_oh")
        L_ips = sem("L_ips")
        yg_in = [sem(f"yg_in{t}") for t in range(NT)]
        y_fin = sem("y_fin")
        fin_out = sem("fin_out")
        st_out = sem("st_out")
        kv_out = sem("kv_out")

        ORDER = [TAIL, 0, 1, 2, 3]
        HALVES = [(t, hh) for t in ORDER for hh in range(2)]

        def bcast(ap, *pattern):
            return ap.unsqueeze(pattern[0]).to_broadcast(pattern[1])

        block = ctx.enter_context(nc.Block())

        @block.sync
        def _(sp):
            xp = x_prompt.rearrange("o (t p) d -> p (o t) d", p=P)
            for t in range(TAIL):
                sp.dma_start(x_sb[:, t, :], xp[:, t, :]).then_inc(x_in[t], 16)
                if t == 0:
                    sp.dma_start(cst[:, :], consts).then_inc(c_in, 16)
                    sp.dma_start(g1T[:, :], norm1_g.rearrange("o (p k) -> p (o k)", k=KD)).then_inc(c_in, 16)
            sp.dma_start(x_sb[0:DEC, TAIL, :], x_sample.rearrange("o s d -> (o s) d")).then_inc(x_in[TAIL], 16)
            sp.dma_start(x_sb[DEC:DEC + NMETA, TAIL, :], meta_tokens).then_inc(x_in[TAIL], 16)

            def load_piece(src, width, i, s, first):
                if not first:
                    sp.wait_ge(split, i - RING + 1)
                sp.dma_start(w_raw[:, s, 0:width], src).then_inc(raw_in[s], 16)

            for c, (col, width) in enumerate(CHUNKS):
                if c == 0:
                    for k in range(KD):
                        load_piece(w_in_v[:, k, col:col + width], width, k, k % RING, k < RING)
                    continue
                with sp.Fori(0, KD // RING) as r:
                    for s in range(RING):
                        k = r * RING + s
                        load_piece(w_in_v[:, bass.ds(k, 1), col:col + width].rearrange("p o n -> p (o n)"),
                                   width, k + KD * c, s, False)
            for n in range(2):
                for j, k in enumerate(OUT_K):
                    load_piece(w_out_v[:, k, n * 512:n * 512 + 512], 512, KD * (len(CHUNKS) + n) + j,
                               j % RING, False)

            sp.wait_ge(o_lo, len(HALVES))
            sp.wait_ge(o_hi, len(HALVES))
            sp.wait_ge(rm_lo, NT)
            sp.wait_ge(rm_hi, NT)
            sp.wait_ge(kv_out, 16 * 6)
            sp.wait_ge(shift_in, 16 * 4)

            def load_pair(p, u, first):
                if not first:
                    sp.wait_ge(gu_ps, p - 1)
                for e in range(2):
                    for m, v in enumerate((gate_v, up_v)):
                        sp.dma_start(w_moe[:, u, e, m, :], v[bass.ds(p * 2 + e, 1)].rearrange("o p n -> p (o n)")
                                     ).then_inc(gu_in[u], 16)
                if not first:
                    sp.wait_ge(y_ps, p - 1)
                for e in range(2):
                    sp.dma_start(w_moe[:, u, e, 2, :], down_v[bass.ds(p * 2 + e, 1)].rearrange("o p n -> p (o n)")
                                 ).then_inc(dn_in[u], 16)

            for u in range(2):
                load_pair(u, u, True)
            with sp.Fori(1, NPAIR // 2) as i:
                for u in range(2):
                    load_pair(i * 2 + u, u, False)

            sp.wait_ge(slots_ready, 1)
            n_most = sp.value_load(most_i[0:1, 0:1], min_val=0, max_val=T_TOK)
            with sp.If(n_most > CAP):
                sp.wait_ge(y_ps, NPAIR)
                with sp.Fori(1, LEVELS) as lv:
                    with sp.Fori(0, NPAIR) as p:
                        it = (lv - 1) * NPAIR + p
                        sp.wait_ge(L_y, it)
                        for e in range(2):
                            for m, v in enumerate((gate_v, up_v, down_v)):
                                sp.dma_start(w_moe[:, 0, e, m, :],
                                             v[bass.ds(p * 2 + e, 1)].rearrange("o p n -> p (o n)")
                                             ).then_inc(L_w, 16)
            yp = y_prompt.rearrange("o (t p) d -> p (o t) d", p=P)
            ys = y_sample.rearrange("o s d -> (o s) d")
            for t in range(NT):
                sp.wait_ge(y_fin, t + 1)
                if t < TAIL:
                    sp.dma_start(yp[:, t, :], x_sb[:, t, :]).then_inc(fin_out, 16)
                else:
                    sp.dma_start(ys, x_sb[0:DEC, t, :]).then_inc(fin_out, 16)
            sp.wait_ge(fin_out, 16 * NT)
            sp.wait_ge(st_out, 16 * 4)

        @block.gpsimd
        def _(pool):
            rt = w_router[:, :, :]

            def alone():
                pool.sem_inc(pool_pass, 1)

            pool.dma_start(g2T[:, :], norm2_g.rearrange("o (p k) -> p (o k)", k=KD)).then_inc(g_in, 16)
            pool.dma_start(retgT[:, :], ret_norm_g).then_inc(g_in, 16)
            pool.dma_start(qk_g[:, 0, :], q_norm_g.to_broadcast([P, HD])).then_inc(g_in, 16)
            pool.dma_start(qk_g[:, 1, :], k_norm_g.to_broadcast([P, HD])).then_inc(g_in, 16)
            pool.dma_start(sinks[:, :], attn_sinks.to_broadcast([P, QH])).then_inc(g_in, 16)
            pool.dma_start(rt[:, :, 0:NG], w_group.rearrange("o (p k) n -> p (o k) n", p=P)).then_inc(g_in, 16)
            pool.dma_start(rt[:, :, NG:], w_expert.rearrange("o (p k) n -> p (o k) n", p=P)).then_inc(g_in, 16)

            def split_piece(i, s, rnd, width, first):
                pool.wait_ge(raw_in[s], (rnd + 1) * 16)
                if not first:
                    pool.wait_ge(piece_used, i - RING + 1)
                    alone()
                nc.gpsimd.tensor_copy(w_hi[:, s, 0:width], w_raw[:, s, 0:width]).then_inc(hi_done, 1)
                pool.wait_ge(hi_done, i + 1)
                nc.gpsimd.tensor_tensor(w_lo[:, s, 0:width], w_raw[:, s, 0:width],
                                        w_hi[:, s, 0:width].bitcast(F32), ALU.subtract).then_inc(split, 1)

            for k in range(KD):
                split_piece(k, k % RING, k // RING, CHUNKS[0][1], k < RING)
            with pool.Fori(2, 2 * (len(CHUNKS) + 2)) as r:
                for s in range(RING):
                    split_piece(r * RING + s, s, r, 512, False)

            def gather(p, u, first):
                if not first:
                    pool.wait_ge(xg_ps, p - 1)
                    alone()
                nc.gpsimd.tensor_copy(idx_now[:, u, :], idx[:, bass.ds(p, 1)]).then_inc(idx_c, 1)
                pool.wait_ge(idx_c, p + 1)
                if not first:
                    alone()
                pool.indirect_dma_start(out=xg[:, u, :], out_offset=None, in_=hn_d,
                                        in_offset=bass.IndirectOffsetOnAxis(ap=idx_now[:, u, 0:1], axis=0)
                                        ).then_inc(xg_in[u], 16)

            pool.wait_ge(hn_out[0], 16 * 3)
            pool.wait_ge(hn_out[1], 16 * 2)
            pool.wait_ge(hT_ps, NT)
            pool.wait_ge(idx_ready, 1)
            for u in range(2):
                gather(u, u, True)
            with pool.Fori(1, NPAIR // 2) as i:
                for u in range(2):
                    gather(i * 2 + u, u, False)
            pool.wait_ge(slots_ready, 1)
            n_most = pool.value_load(most_i[0:1, 0:1], min_val=0, max_val=T_TOK)
            with pool.If(n_most > CAP):
                pool.wait_ge(xg_ps, NPAIR)
                with pool.Fori(1, LEVELS) as lv:
                    pool.wait_ge(L_idx, lv)
                    alone()
                    with pool.Fori(0, NPAIR) as p:
                        it = (lv - 1) * NPAIR + p
                        pool.wait_ge(L_xt, it)
                        alone()
                        nc.gpsimd.tensor_copy(idx_now[:, 0, :], idx[:, bass.ds(p, 1)]).then_inc(L_col, 1)
                        pool.wait_ge(L_col, it + 1)
                        alone()
                        pool.indirect_dma_start(out=xg[:, 0, :], out_offset=None, in_=hn_d,
                                                in_offset=bass.IndirectOffsetOnAxis(ap=idx_now[:, 0, 0:1], axis=0)
                                                ).then_inc(L_xg, 16)

            def fetch(levels):
                for t in range(NT):
                    for k in range(2):
                        n = out_rows(t)
                        pool.indirect_dma_start(out=y_tok[0:n, t, k, :], out_offset=None,
                                                in_=y_d[0:levels * NE * CAP, :],
                                                in_offset=bass.IndirectOffsetOnAxis(
                                                    ap=slot_i[0:n, k * NT + t:k * NT + t + 1], axis=0)
                                                ).then_inc(yg_in[t], 16)

            for u in range(2):
                pool.wait_ge(y_out[u], 8 * NPAIR)
            pool.wait_ge(y_ps, NPAIR)
            with pool.If(n_most > CAP):
                pool.wait_ge(L_out, 16 * NPAIR * (LEVELS - 1))
                fetch(LEVELS)
            with pool.If(n_most <= CAP):
                fetch(1)

        @block.tensor
        def _(pe):
            mm = nc.tensor.matmul
            busy = {5: None, 6: None, 7: None}

            def take(*banks):
                for b in banks:
                    if busy[b]:
                        for s, n in busy[b]:
                            pe.wait_ge(s, n)

            n_t = [0]

            pe.wait_ge(c_in, 32)
            n = 0
            for t in range(NT):
                pe.wait_ge(x_in[t], 16 if t < TAIL else 32)
                R = rows_of(t)
                xv = x_sb[0:R, t, :].rearrange("p (q k) -> p k q", k=KD)
                for half in range(2):
                    b = n % 2
                    take(5 + b)
                    for j in range(4):
                        l = nc.tensor.transpose(sideb[:, b, j * P:j * P + R], xv[:, 4 * half + j, :],
                                                ident[0:R, 0:R])
                    l.then_inc(xt_ps, 1)
                    n += 1
                    busy[5 + b] = [(xt_part, n)]

            n_piece = [0]

            def dense(tiles, width, order, chunk):
                for kk, k in enumerate(order):
                    s = n_piece[0] % RING
                    pe.wait_ge(split, n_piece[0] + 1)
                    for t, R in tiles:
                        if kk == 0 and chunk > 0:
                            pe.wait_ge(acc_free, NT * (chunk - 1) + t + 1)
                        lo, hi = P * t, P * t + R
                        for j, (a, w) in enumerate(((xT_hi, w_hi), (xT_hi, w_lo), (xT_lo, w_hi))):
                            l = mm(acc[0:R, t, 0:width], a[:, k, lo:hi], w[:, s, 0:width],
                                   start=(kk == 0 and j == 0), stop=(kk == KD - 1 and j == 2))
                        if kk == KD - 1:
                            l.then_inc(acc_done, 1)
                        elif t == tiles[-1][0]:
                            l.then_inc(piece_used, 1)
                    if kk == KD - 1:
                        pe.wait_ge(acc_done, NT * (chunk + 1))
                        pe.sem_inc(piece_used, 1)
                    n_piece[0] += 1

            pe.wait_ge(xt_lo, 2 * NT)
            pe.wait_ge(xt_hi, 2 * NT)
            for c, (col, width) in enumerate(CHUNKS):
                dense([(t, rows_of(t)) for t in range(NT)], width, range(KD), c)

            pe.wait_ge(kv_in, 16 * 4)
            for i, t in enumerate(ORDER):
                R = rows_of(t)
                take(5, 6)
                pe.wait_ge(qk_rows, NT * (SQ + 1))
                for h in range(4):
                    nc.tensor.transpose(sideb[:, 0, h * P:h * P + R],
                                        sq[0:R, t, h, :, :].rearrange("p g d -> p (g d)"), ident[0:R, 0:R])
                l = nc.tensor.transpose(sideb[:, 1, 0:R], sk[0:R, t, :], ident[0:R, 0:R])
                if i == 0:
                    l = nc.tensor.transpose(sideb[:, 1, P:2 * P], cache_k[:, :], ident[:, :])
                l.then_inc(t_ps, 1)
                busy[5], busy[6] = [(qT_ev, i + 1)], [(kT_ev, i + 1)]
                take(7)
                pe.wait_ge(qk_rows, NT * 3)
                for j in range(4):
                    l = nc.tensor.transpose(side3[:, j * P:j * P + R], rqk[0:R, t, j * P:j * P + P],
                                            ident[0:R, 0:R])
                l.then_inc(t_ps, 1)
                busy[7] = [(rT_ev, i + 1)]

            def scores(i, t, hh):
                take(5, 6)
                pe.wait_ge(qT_ev, NT)
                pe.wait_ge(kT_ev, NT)
                for c2 in range(2 if t < TAIL else 1):
                    c = 2 * t + c2
                    if t == TAIL:
                        keys = [(CACHE0, WINDOW, 0), (SEQ, CH, WINDOW)]
                    elif c < 2:
                        keys = [(0, CH * (c + 1), WINDOW - CH * c)]
                    else:
                        keys = [(CH * c - WINDOW, BAND, 0)]
                    keys.append((T_TOK, NMETA, BAND))
                    for hl in range(2):
                        for col, n, dst in keys:
                            for g in range(2):
                                l = mm(side[64 * c2:64 * c2 + 64, g, hl, dst:dst + n],
                                       sqT[64 * g:64 * g + 64, 2 * hh + hl, CH * c:CH * c + CH],
                                       skT[64 * g:64 * g + 64, col:col + n], start=True, stop=True)
                l.then_inc(s_ps, 1)
                busy[5] = busy[6] = [(s_exp, i + 1)]

            def probs_T(i, t):
                R = out_rows(t)
                take(5, 6)
                pe.wait_ge(s_prob, i + 1)
                for j in range(4):
                    nc.tensor.transpose(sideb[:, 0, j * P:j * P + R], probs[0:R, j, 0:P], ident[0:R, 0:R])
                for j in range(4):
                    l = nc.tensor.transpose(sideb[0:CH + NMETA, 1, j * P:j * P + R], probs[0:R, j, P:KEYS],
                                            ident[0:R, 0:R])
                l.then_inc(pT_ps, 1)
                busy[5], busy[6] = [(pT_a, i + 1)], [(pT_c, i + 1)]

            def values(i, t):
                take(7)
                pe.wait_ge(pT_a, i + 1)
                pe.wait_ge(pT_c, i + 1)
                n = CH + NMETA
                for g in range(2):
                    gc = slice(64 * g, 64 * g + 64)
                    for c2 in range(2 if t < TAIL else 1):
                        if t == TAIL:
                            lots = [(cache_v[:, gc], 0, P), (sv[0:n, t, gc], 1, n)]
                        else:
                            before = v_shift[:, t, gc] if c2 else (sv[:, t - 1, gc] if t else None)
                            lots = [(before, 0, P)] if before is not None else []
                            lots.append((v_own[0:n, 2 * t + c2, gc], 1, n))
                        q = slice(64 * c2, 64 * c2 + 64)
                        for j, (v, blk, kn) in enumerate(lots):
                            for hl in range(2):
                                l = mm(side3[64 * hl:64 * hl + 64, P * g + 64 * c2:P * g + 64 * c2 + 64], v,
                                       probsT[0:kn, blk, 2 * g + hl, q], start=(j == 0),
                                       stop=(j == len(lots) - 1))
                l.then_inc(o_ps, 1)
                busy[7] = [(o_hi, i + 1), (o_lo, i + 1)]

            pe.wait_ge(shift_in, 16 * 4)
            pe.wait_ge(vmeta, 1)
            for i, (t, hh) in enumerate(HALVES):
                scores(i, t, hh)
                probs_T(i, t)
                values(i, t)

            def outer(lo, n, t):
                take(7)
                for h in range(RH):
                    l = mm(side3[64 * (h % 2):64 * (h % 2) + 64, P * (h // 2):P * (h // 2) + P],
                           rqk[lo:lo + n, t, 256 + 64 * h:256 + 64 * h + 64],
                           rv[lo:lo + n, t, P * h:P * h + P], start=True, stop=True)
                l.then_inc(st_ps, 1)

            pe.wait_ge(v_rows, NT * 2)
            pe.wait_ge(rT_ev, NT)
            outer(DEC, NMETA, TAIL)
            busy[7] = [(st_new, 1)]
            for i, t in enumerate(ORDER):
                R = out_rows(t)
                state = state_s if t == TAIL else state_p
                tok = slice(P * t, P * t + R)
                take(5, 6)
                for h in range(RH):
                    hs = slice(64 * (h % 2), 64 * (h % 2) + 64)
                    l = mm(side[0:R, h % 2, h // 2, 0:R], rT[hs, 2 + h // 2, tok], rT[hs, h // 2, tok],
                           start=True, stop=True)
                l.then_inc(ra_ps, 1)
                busy[5] = busy[6] = [(ra_ev, i + 1)]
                take(5, 6)
                for h in range(RH):
                    hs = slice(64 * (h % 2), 64 * (h % 2) + 64)
                    out = side[0:R, h % 2, h // 2, 0:P]
                    l = mm(out, ret_aT[0:R, 2 * (h % 2) + h // 2, 0:R], rv[0:R, t, P * h:P * h + P],
                           start=True, stop=False)
                    if R < P:
                        l.then_inc(ro_part, 1)
                        pe.wait_ge(ro_part, h + 1)
                    if h == 0:
                        pe.wait_ge(st_new, max(1, i + 1))
                    l = mm(out, rT[hs, h // 2, tok], state[hs, h // 2, :], start=False, stop=True)
                    if R < P and h < RH - 1:
                        l.then_inc(ro_cross, 1)
                        pe.wait_ge(ro_cross, h + 1)
                l.then_inc(ro_ps, 1)
                busy[5] = busy[6] = [(ro_rows, i + 1)]
                outer(0, R, t)
                busy[7] = [(st_new, i + 2)]
                take(7)
                pe.wait_ge(ro_rows, i + 1)
                for h in range(RH):
                    l = nc.tensor.transpose(side3[:, P * h:P * h + R], o_rows[0:R, h, :], ident[0:R, 0:R])
                l.then_inc(rm_ps, 1)
                busy[7] = [(rm_part, i + 1)]

            pe.wait_ge(o_hi, len(HALVES))
            pe.wait_ge(o_lo, len(HALVES))
            pe.wait_ge(rm_hi, NT)
            pe.wait_ge(rm_lo, NT)
            for n in range(2):
                dense([(t, rows_of(t)) for t in range(NT)], 512, OUT_K, len(CHUNKS) + n)

            for t in range(NT):
                R = out_rows(t)
                pe.wait_ge(hn_rows, t + 1)
                take(5, 6)
                hv = rows[0:R, t % 2, :].rearrange("p (q k) -> p k q", k=KD)
                for k in range(KD):
                    l = nc.tensor.transpose(sideb[:, k // 4, (k % 4) * P:(k % 4) * P + R], hv[:, k, :],
                                            ident[0:R, 0:R])
                l.then_inc(hT_ps, 1)
                busy[5] = busy[6] = [(hT_ev, t + 1)]
                take(7)
                pe.wait_ge(hT_ev, t + 1)
                for k in range(KD):
                    l = mm(side3[0:R, 0:NG + NE], hnT[:, k, 0:R], w_router[:, k, :], start=(k == 0),
                           stop=(k == KD - 1))
                l.then_inc(lg_ps, 1)
                busy[7] = [(lg_ev, t + 1)]

            pe.wait_ge(m_ready, 1)
            take(7)
            for t in range(NT):
                for t2 in range(t + 1):
                    mm(side3[:, NE * t:NE * t + NE], const("before") if t2 == t else ones, chosen[:, t2, :],
                       start=(t2 == 0), stop=(t2 == t))
            for t in range(NT):
                l = mm(side3[:, NE * NT:NE * NT + NE], ones, chosen[:, t, :], start=(t == 0), stop=(t == NT - 1))
            l.then_inc(rank_ps, 1)
            pe.wait_ge(oh_ready, 1)

            def find_rows():
                for j in range(2 * NT):
                    l = mm(side3[:, 256:256 + NPAIR], row_oh[:, j, :], pair_tok[:, j, :], start=(j == 0),
                           stop=(j == 2 * NT - 1))
                return l

            find_rows().then_inc(idx_ps, 1)

            def rows_T(p, u, wait):
                pe.wait_ge(xg_in[u], wait)
                gv = xg[:, u, :].rearrange("p (q k) -> p k q", k=KD)
                for k in range(KD):
                    l = nc.tensor.transpose(sideb[:, k // 4, (k % 4) * P:(k % 4) * P + P], gv[:, k, :], ident)
                return l

            def gate_up(u, slot, xu):
                for k in range(KD):
                    for e in range(2):
                        l = mm(acc[64 * e:64 * e + 64, u, :].rearrange("p (m f) -> p m f", m=2),
                               xgT[:, xu, k, 64 * e:64 * e + 64], w_moe[:, slot, e, 0:2, k * FF:k * FF + FF],
                               start=(k == 0), stop=(k == KD - 1))
                return l

            def act_T():
                av = actv[:, :].rearrange("p (q j) -> p j q", j=2)
                for j in range(2):
                    l = nc.tensor.transpose(side3[:, P * j:P * j + P], av[:, j, :], ident)
                return l

            def down(slot):
                for n in range(2):
                    for j in range(2):
                        for e in range(2):
                            l = mm(acc[64 * e:64 * e + 64, 2 + n, :], actT[:, j, 64 * e:64 * e + 64],
                                   w_moe[:, slot, e, 2, j * D + n * 512:j * D + n * 512 + 512],
                                   start=(j == 0), stop=(j == 1))
                return l

            def first_half(p, u, rnd, first):
                if not first:
                    pe.wait_ge(xg_ev, p)
                rows_T(p, u, rnd * 16 + 16).then_inc(xg_ps, 1)
                pe.wait_ge(xg_ev, p + 1)
                pe.wait_ge(gu_in[u], rnd * 64 + 64)
                gate_up(u, u, u).then_inc(gu_ps, 1)

            def second_half(p, u, rnd, first):
                pe.wait_ge(e_act, p + 1)
                act_T().then_inc(aT_ps, 1)
                pe.wait_ge(aT_ev, p + 1)
                pe.wait_ge(dn_in[u], rnd * 32 + 32)
                if not first:
                    pe.wait_ge(y_ev, p)
                down(u).then_inc(y_ps, 1)

            pe.wait_ge(idx_ready, 1)
            pe.wait_ge(acc_free, NT * (len(CHUNKS) + 2))
            first_half(0, 0, 0, True)
            first_half(1, 1, 0, False)
            second_half(0, 0, 0, True)
            with pe.Fori(1, NPAIR // 2) as i:
                first_half(i * 2, 0, i, False)
                second_half(i * 2 - 1, 1, i - 1, False)
                first_half(i * 2 + 1, 1, i, False)
                second_half(i * 2, 0, i, False)
            second_half(NPAIR - 1, 1, NPAIR // 2 - 1, False)

            pe.wait_ge(slots_ready, 1)
            n_most = pe.value_load(most_i[0:1, 0:1], min_val=0, max_val=T_TOK)
            with pe.If(n_most > CAP):
                pe.wait_ge(y_ev, NPAIR)
                with pe.Fori(1, LEVELS) as lv:
                    pe.wait_ge(L_oh, lv)
                    find_rows().then_inc(L_ips, 1)
                    with pe.Fori(0, NPAIR) as p:
                        it = (lv - 1) * NPAIR + p
                        pe.wait_ge(L_xg, it * 16 + 16)
                        rows_T(0, 0, 16).then_inc(L_xt, 1)
                        pe.wait_ge(L_xe, it + 1)
                        pe.wait_ge(L_w, it * 96 + 96)
                        gate_up(0, 0, 0).then_inc(L_gu, 1)
                        pe.wait_ge(L_act, it + 1)
                        act_T().then_inc(L_at, 1)
                        pe.wait_ge(L_ae, it + 1)
                        pe.wait_ge(L_ye, it)
                        down(0).then_inc(L_y, 1)

        @block.scalar
        def _(act):
            af = nc.scalar.activation
            steps = [0]

            def step(ins):
                ins.then_inc(act_step, 1)
                steps[0] += 1
                act.wait_ge(act_step, steps[0])

            roots = [0]

            def guess(n, R=P):
                roots[0] += 1
                act.wait_ge(ms_ready, roots[0])
                step(af(root[0:R, 0, 0:n], ms[0:R, 0:n], ACT.Ln))
                af(root[0:R, 1, 0:n], root[0:R, 0, 0:n], ACT.Exp, scale=-0.5).then_inc(root_ready, 1)

            ck = cache_swa_k.rearrange("o b w g d -> (o b w) (g d)")
            cv = cache_swa_v.rearrange("o b w g d -> (o b w) (g d)")
            act.dma_start(cache_k[:, :], ck).then_inc(kv_in, 16)
            act.dma_start(cache_v[:, :], cv).then_inc(kv_in, 16)
            cs = cache_ret_state.rearrange("o b (i h) k v -> (h k) (o b i) v", h=2)
            for i in range(2):
                act.dma_start(state_s[:, i, :], cs[:, i, :]).then_inc(kv_in, 16)

            n = 0
            for t in range(NT):
                R = rows_of(t)
                act.wait_ge(x_in[t], 16 if t < TAIL else 32)
                if t == 0:
                    act.wait_ge(ssq_clear, 1)
                else:
                    act.wait_ge(act_step, steps[0])
                step(af(h_raw[0:R, 0:2, :].rearrange("p a n -> p (a n)"), x_sb[0:R, t, :], ACT.Square,
                        accum_out=ssq[0:R, t:t + 1]))
                for half in range(2):
                    n += 1
                    act.wait_ge(xt_part, n)
                    nc.scalar.copy(xT_hi[:, 4 * half:4 * half + 4, P * t:P * t + R],
                                   part[:, half, :, 0:R]).then_inc(xt_hi, 1)
            guess(NT)

            act.wait_ge(rstd_ready, 1)
            n_raw = n_sq = 0
            for c in range(len(CHUNKS)):
                for t in range(NT):
                    R = rows_of(t)
                    r1 = rstd1[0:R, t:t + 1]
                    act.wait_ge(acc_done, NT * c + t + 1)
                    if c in (SKV, SQ, RQK):
                        if n_raw >= NT:
                            act.wait_ge(raw_q_used, n_raw - NT + 1)
                        width = P if c == SKV else 512
                        step(af(h_raw[0:R, t, 0:width], acc[0:R, t, 0:width], ACT.Copy, scale=r1))
                        if c == SKV:
                            step(af(sv[0:R, t, :], acc[0:R, t, P:2 * P], ACT.Copy, scale=r1))
                            act.sem_inc(v_rows, 1)
                        act.sem_inc(acc_free, 1)
                        act.sem_inc(raw_q, 1)
                        n_raw += 1
                    else:
                        step(af((rv if c == RV else gate)[0:R, t, :], acc[0:R, t, :], ACT.Copy, scale=r1))
                        act.sem_inc(acc_free, 1)
                        if c == RV:
                            act.sem_inc(v_rows, 1)
                for t in range(NT):
                    R = rows_of(t)
                    if c in (SKV, SQ):
                        if n_sq:
                            act.wait_ge(raw_sq_used, n_sq)
                        n_sq += 1
                        width = P if c == SKV else 512
                        af(h_sq[0:R, 0:width], h_raw[0:R, t, 0:width], ACT.Square).then_inc(raw_sq, 1)
                        guess(2 if c == SKV else QH, R)
                    elif c == RG:
                        if t:
                            act.wait_ge(gate_rows, t)
                        af(h_sq[0:R, :], gate[0:R, t, :], ACT.Exp, scale=-1.0).then_inc(gate_z, 1)

            act.wait_ge(qk_rows, NT)
            own = v_own[:, :, :].rearrange("p (t c) d -> p t c d", c=2)
            act.dma_start(v_shift[64:128, :, :], sv[0:64, 0:4, :]).then_inc(shift_in, 16)
            act.dma_start(v_shift[0:64, 1:4, :], sv[64:128, 0:3, :]).then_inc(shift_in, 16)
            act.dma_start(own[0:64, :, 0, :], sv[0:64, 0:4, :]).then_inc(shift_in, 16)
            act.dma_start(own[0:64, :, 1, :], sv[64:128, 0:4, :]).then_inc(shift_in, 16)
            for out_p, out_s, rows_, old in ((k_prompt, k_sample, sk, ck), (v_prompt, v_sample, sv, cv)):
                op = out_p.rearrange("o b w g d -> (o b w) (g d)")
                os = out_s.rearrange("o b w g d -> (o b w) (g d)")
                act.dma_start(op, rows_[:, 3, :]).then_inc(kv_out, 16)
                act.dma_start(os[DEC:, :], rows_[0:DEC, TAIL, :]).then_inc(kv_out, 16)
                act.dma_start(os[0:WINDOW - DEC, :], old[DEC:, :]).then_inc(kv_out, 16)

            for i, t in enumerate(ORDER):
                R = rows_of(t)
                act.wait_ge(t_ps, 2 * i + 1)
                if i == 0:
                    step(nc.scalar.copy(skT[:, CACHE0:CACHE0 + P], sideb[:, 1, P:2 * P]))
                nc.scalar.copy(skT[:, P * t:P * t + R], sideb[:, 1, 0:R]).then_inc(kT_ev, 1)
                act.wait_ge(t_ps, 2 * i + 2)
                nc.scalar.copy(rT[:, :, P * t:P * t + R],
                               side3[:, :].rearrange("p (j n) -> p j n", j=4)[:, :, 0:R]).then_inc(rT_ev, 1)

            for i, (t, hh) in enumerate(HALVES):
                R = out_rows(t)
                act.wait_ge(s_max, i + 1)
                for j in range(4):
                    step(af(probs[0:R, j, 0:KEYS], side4[0:R, j, 0:KEYS], ACT.Exp, scale=HD ** -0.5,
                            bias=small[0:R, 4 + j:5 + j], accum_out=small[0:R, 8 + j:9 + j]))
                af(small[0:R, 16:20], small[0:R, 12:16], ACT.Exp).then_inc(s_exp, 1)
                act.wait_ge(pT_ps, i + 1)
                nc.scalar.copy(probsT[0:CH + NMETA, 1, :, 0:R],
                               sideb[0:CH + NMETA, 1, :].rearrange("p (j n) -> p j n", j=4)[:, :, 0:R]
                               ).then_inc(pT_c, 1)
                act.wait_ge(o_ps, i + 1)
                nc.scalar.copy(xT_hi[:, 4 + hh:KD:2, P * t:P * t + R],
                               side3[:, 0:2 * P].rearrange("p (g n) -> p g n", g=2)[:, :, 0:R]).then_inc(o_hi, 1)

            for i, t in enumerate(ORDER):
                R = out_rows(t)
                act.wait_ge(ro_ps, i + 1)
                if i:
                    act.wait_ge(ro_rows, i)
                af(h_sq[0:R, :].rearrange("p (j n) -> p j n", j=4), side4[0:R, :, 0:P], ACT.Square
                   ).then_inc(ro_sq, 1)
                guess(RH, R)
                act.wait_ge(rm_part, i + 1)
                nc.scalar.copy(xT_hi[:, 0:4, P * t:P * t + R], part[:, 0, :, 0:R]).then_inc(rm_hi, 1)
                if t == TAIL or t == 3:
                    act.wait_ge(st_new, i + 2)
                    st = state_s if t == TAIL else state_p
                    dst = (ret_sample if t == TAIL else ret_prompt).rearrange("o b (i h) k v -> (h k) (o b i) v", h=2)
                    for j in range(2):
                        act.dma_start(dst[:, j, :], st[:, j, :]).then_inc(st_out, 16)

            for t in range(NT):
                R = out_rows(t)
                b = t % 2
                act.wait_ge(x2_done, NT + t + 1)
                if t >= 2:
                    act.wait_ge(hn_out[b], 16 * (t // 2))
                    act.wait_ge(hT_ps, t - 1)
                step(af(rows[0:R, b, :], x_sb[0:R, t, :], ACT.Square, accum_out=ssq[0:R, 0:1]))
                act.sem_inc(sq2, 1)
                guess(1, R)
                act.wait_ge(rstd2, t + 1)
                af(rows[0:R, b, :], x_sb[0:R, t, :], ACT.Copy, scale=rstd[0:R, 0:1]).then_inc(hn_rows, 1)
                act.wait_ge(hn_rows, t + 1)
                act.dma_start(hn_d[P * t:P * t + R, :], rows[0:R, b, :]).then_inc(hn_out[b], 16)

            act.wait_ge(r_exp, 1)
            step(af(r4b[:, :, :], r4[:, :, :], ACT.Exp))
            act.sem_inc(r_expd, 1)
            act.wait_ge(r_exp, 2)
            af(small[:, 20:25], small[:, 25:30], ACT.Exp).then_inc(r_expd, 1)

            def pair_out(p, u, rnd, first):
                act.wait_ge(y_ps, p + 1)
                if not first:
                    act.wait_ge(y_out[u], rnd * 16)
                step_free(nc.scalar.copy(y_sb[:, u, :], acc[:, 2:4, :].rearrange("p b n -> p (b n)")), p)
                act.dma_start(y_pairs[bass.ds(p, 1)].rearrange("o r d -> (o r) d"), y_sb[:, u, :]
                              ).then_inc(y_out[u], 16)

            def step_free(ins, p):
                ins.then_inc(y_ev, 1)
                act.wait_ge(y_ev, p + 1)

            def pair_exp(p, u, first):
                act.wait_ge(gu_ps, p + 1)
                if not first:
                    act.wait_ge(e_act, p)
                af(glu[:, 0, :], acc[:, u, 0:FF], ACT.Exp, scale=-1.0).then_inc(e_exp, 1)

            pair_exp(0, 0, True)
            pair_exp(1, 1, False)
            pair_out(0, 0, 0, True)
            pair_exp(2, 0, False)
            pair_out(1, 1, 0, True)
            pair_exp(3, 1, False)
            with act.Fori(1, NPAIR // 2 - 1) as i:
                for u in range(2):
                    pair_out(i * 2 + u, u, i, False)
                    pair_exp(i * 2 + u + 2, u, False)
            pair_out(NPAIR - 2, 0, NPAIR // 2 - 1, False)
            pair_out(NPAIR - 1, 1, NPAIR // 2 - 1, False)

            act.wait_ge(slots_ready, 1)
            n_most = act.value_load(most_i[0:1, 0:1], min_val=0, max_val=T_TOK)
            with act.If(n_most > CAP):
                act.wait_ge(y_out[0], 8 * NPAIR)
                with act.Fori(1, LEVELS) as lv:
                    with act.Fori(0, NPAIR) as p:
                        it = (lv - 1) * NPAIR + p
                        act.wait_ge(L_gu, it + 1)
                        af(glu[:, 0, :], acc[:, 0, 0:FF], ACT.Exp, scale=-1.0).then_inc(L_ex, 1)
                        act.wait_ge(L_y, it + 1)
                        act.wait_ge(L_out, it * 16)
                        nc.scalar.copy(y_sb[:, 0, :], acc[:, 2:4, :].rearrange("p b n -> p (b n)")).then_inc(L_ye, 1)
                        act.wait_ge(L_ye, it + 1)
                        act.dma_start(y_pairs[bass.ds(lv * NPAIR + p, 1)].rearrange("o r d -> (o r) d"),
                                      y_sb[:, 0, :]).then_inc(L_out, 16)

        @block.vector
        def _(dve):
            tt = nc.vector.tensor_tensor
            ts = nc.vector.tensor_scalar
            stt = nc.vector.scalar_tensor_tensor
            red = nc.vector.tensor_reduce
            steps = [0]

            def step(ins):
                ins.then_inc(dve_step, 1)
                steps[0] += 1
                dve.wait_ge(dve_step, steps[0])

            roots = [0]

            def inv_root(dst, n, R=P):
                roots[0] += 1
                dve.sem_inc(ms_ready, 1)
                dve.wait_ge(root_ready, roots[0])
                a = root[0:R, 2, 0:n]
                g = root[0:R, 1, 0:n]
                step(tt(a, g, g, ALU.mult))
                step(tt(a, a, ms[0:R, 0:n], ALU.mult))
                step(ts(a, a, -0.5, 1.5, ALU.mult, ALU.add))
                step(tt(dst, a, g, ALU.mult))

            step(nc.vector.memset(ssq[:, :], 1.0))
            dve.sem_inc(ssq_clear, 1)
            dve.wait_ge(c_in, 32)
            n = 0
            for t in range(NT):
                R = rows_of(t)
                for half in range(2):
                    n += 1
                    dve.wait_ge(xt_ps, n)
                    if n > 2:
                        dve.wait_ge(xt_lo, n - 2)
                        dve.wait_ge(xt_hi, n - 2)
                    src = sideb[:, (n - 1) % 2, :].rearrange("p (j n) -> p j n", j=4)[:, :, 0:R]
                    tt(part[:, half, :, 0:R], src,
                       g1T[:, 4 * half:4 * half + 4].unsqueeze(2).to_broadcast([P, 4, R]), ALU.mult
                       ).then_inc(xt_part, 1)
                    dve.wait_ge(xt_hi, n)
                    dst = (slice(None), slice(4 * half, 4 * half + 4), slice(P * t, P * t + R))
                    tt(xT_lo[dst], part[:, half, :, 0:R], xT_hi[dst].bitcast(F32), ALU.subtract
                       ).then_inc(xt_lo, 1)
            dve.wait_ge(act_step, NT)
            step(ts(ms[:, 0:NT], ssq[:, 0:NT], 1.0 / D, EPS, ALU.mult, ALU.add))
            inv_root(rstd1[:, :], NT)
            dve.sem_inc(rstd_ready, 1)
            dve.wait_ge(g_in, 16 * 7)
            for a in range(2):
                g = qk_g[:, a:a + 1, :].to_broadcast([P, NT, HD])
                step(tt(rope_g[:, a, 0], cos_t, g, ALU.mult))
                h = HD // 2
                step(tt(rope_g[:, a, 1, :, 0:h], sin_t[:, :, 0:h], qk_g[:, a:a + 1, h:].to_broadcast([P, NT, h]),
                        ALU.mult))
                step(tt(rope_g[:, a, 1, :, h:], sin_t[:, :, h:], qk_g[:, a:a + 1, 0:h].to_broadcast([P, NT, h]),
                        ALU.mult))

            def rope(src, nh, R, cos, sin):
                h = HD // 2
                s = src.rearrange("p (n d) -> p n d", n=nh)
                a = h_a[0:R, 0:nh * HD].rearrange("p (n d) -> p n d", n=nh)
                b = h_b[0:R, 0:nh * HD].rearrange("p (n d) -> p n d", n=nh)
                step(tt(a, s, cos.unsqueeze(1).to_broadcast([R, nh, HD]), ALU.mult))
                step(tt(b[:, :, 0:h], s[:, :, h:], sin[:, 0:h].unsqueeze(1).to_broadcast([R, nh, h]), ALU.mult))
                step(tt(b[:, :, h:], s[:, :, 0:h], sin[:, h:].unsqueeze(1).to_broadcast([R, nh, h]), ALU.mult))
                step(tt(a, a, b, ALU.add))
                return a

            n_raw = 0
            for c in (SKV, SQ, RQK):
                for t in range(NT):
                    R = rows_of(t)
                    n_raw += 1
                    dve.wait_ge(raw_q, n_raw)
                    if c == RQK:
                        a = rope(h_raw[0:R, t, :], 8, R, cos_t[0:R, t], sin_t[0:R, t])
                        dve.sem_inc(raw_q_used, 1)
                        step(tt(rqk[0:R, t, :].rearrange("p (n d) -> p n d", n=8), a,
                                ret_scale[0:R, t // TAIL, :].unsqueeze(2).to_broadcast([R, 8, HD]), ALU.mult))
                    else:
                        nh, kind = (2, 1) if c == SKV else (QH, 0)
                        w = nh * HD
                        dve.wait_ge(raw_sq, n_raw)
                        step(red(ssq[0:R, 0:nh], h_sq[0:R, 0:w].rearrange("p (n d) -> p n d", n=nh), AX_X, ALU.add))
                        dve.sem_inc(raw_sq_used, 1)
                        step(ts(ms[0:R, 0:nh], ssq[0:R, 0:nh], 1.0 / HD, EPS, ALU.mult, ALU.add))
                        inv_root(rstd[0:R, 0:nh], nh, R)
                        a = rope(h_raw[0:R, t, 0:w], nh, R, rope_g[0:R, kind, 0, t], rope_g[0:R, kind, 1, t])
                        dve.sem_inc(raw_q_used, 1)
                        r = rstd[0:R, 0:nh].unsqueeze(2).to_broadcast([R, nh, HD])
                        if c == SKV:
                            step(tt(sk[0:R, t, :].rearrange("p (n d) -> p n d", n=2), a, r, ALU.mult))
                        else:
                            for g in range(2):
                                step(tt(sq[0:R, t, :, g, :], a[:, 4 * g:4 * g + 4, :],
                                        rstd[0:R, 4 * g:4 * g + 4].unsqueeze(2).to_broadcast([R, 4, HD]), ALU.mult))
                    dve.sem_inc(qk_rows, 1)
                if c == SKV:
                    dve.wait_ge(v_rows, NT)
                    step(nc.vector.tensor_copy(v_own[64:64 + NMETA, :, :], sv[64:64 + NMETA, TAIL:TAIL + 1, :]
                                               .to_broadcast([NMETA, 8, P])))
                    step(nc.vector.memset(v_shift[0:64, 0, :], 0.0))
                    dve.sem_inc(vmeta, 1)

            for t in range(NT):
                R = rows_of(t)
                dve.wait_ge(gate_z, t + 1)
                step(ts(h_a[0:R, :], h_sq[0:R, :], 1.0, None, ALU.add))
                step(nc.vector.reciprocal(h_b[0:R, :], h_a[0:R, :]))
                step(tt(gate[0:R, t, :], gate[0:R, t, :], h_b[0:R, :], ALU.mult))
                dve.sem_inc(gate_rows, 1)

            for i, t in enumerate(ORDER):
                R = rows_of(t)
                dve.wait_ge(t_ps, 2 * i + 1)
                nc.vector.tensor_copy(sqT[:, :, P * t:P * t + R],
                                      sideb[:, 0, :].rearrange("p (j n) -> p j n", j=4)[:, :, 0:R]
                                      ).then_inc(qT_ev, 1)

            sk_v = sinks[:, :].rearrange("p (g a b) -> p a g b", g=2, a=2)
            for i, (t, hh) in enumerate(HALVES):
                R = out_rows(t)
                dve.wait_ge(s_ps, i + 1)
                if t == 0:
                    step(nc.vector.memset(side4[0:64, :, 0:WINDOW], NEG))
                    step(nc.vector.memset(side4[64:128, :, 0:CH], NEG))
                step(red(small[0:R, 0:4], side4[0:R, :, 0:KEYS], AX_X, ALU.max))
                sink = sk_v[0:R, hh]
                v4 = lambda lo: small[0:R, lo:lo + 4].rearrange("p (g b) -> p g b", g=2)
                step(stt(out=v4(0), in0=v4(0), scalar=HD ** -0.5, in1=sink, op0=ALU.mult, op1=ALU.max))
                step(ts(small[0:R, 4:8], small[0:R, 0:4], -1.0, None, ALU.mult))
                step(tt(v4(12), v4(4), sink, ALU.add))
                if i:
                    dve.wait_ge(pT_ps, i)
                dve.sem_inc(s_max, 1)
                dve.wait_ge(s_exp, i + 1)
                step(tt(small[0:R, 20:24], small[0:R, 8:12], small[0:R, 16:20], ALU.add))
                step(nc.vector.reciprocal(small[0:R, 24:28], small[0:R, 20:24]))
                tt(probs[0:R, :, 0:KEYS], probs[0:R, :, 0:KEYS],
                   small[0:R, 24:28].unsqueeze(2).to_broadcast([R, 4, KEYS]), ALU.mult).then_inc(s_prob, 1)
                dve.wait_ge(pT_ps, i + 1)
                nc.vector.tensor_copy(probsT[:, 0, :, 0:R],
                                      sideb[:, 0, :].rearrange("p (j n) -> p j n", j=4)[:, :, 0:R]
                                      ).then_inc(pT_a, 1)
                dve.wait_ge(o_hi, i + 1)
                dst = (slice(None), slice(4 + hh, KD, 2), slice(P * t, P * t + R))
                tt(xT_lo[dst], side3[:, 0:2 * P].rearrange("p (g n) -> p g n", g=2)[:, :, 0:R],
                   xT_hi[dst].bitcast(F32), ALU.subtract).then_inc(o_lo, 1)

            dve.wait_ge(st_ps, 1)
            ps_state = side3[:, 0:2 * RDV].rearrange("p (i v) -> p i v", i=2)
            tt(state_p[:, :, :], ps_state, decay[:, 2, :].unsqueeze(2).to_broadcast([P, 2, RDV]), ALU.mult
               ).then_inc(st_new, 1)
            causal = const("causal")
            for i, t in enumerate(ORDER):
                R = out_rows(t)
                state = state_s if t == TAIL else state_p
                dve.wait_ge(ra_ps, i + 1)
                if i:
                    dve.wait_ge(ro_ps, i)
                tt(ret_aT[0:R, :, 0:R], side4[0:R, :, 0:R],
                   causal[0:R, 0:R].unsqueeze(1).to_broadcast([R, 4, R]), ALU.mult).then_inc(ra_ev, 1)
                dve.wait_ge(ro_sq, i + 1)
                step(red(ssq[0:R, 0:RH], h_sq[0:R, :].rearrange("p (j n) -> p j n", j=4), AX_X, ALU.add))
                step(ts(ms[0:R, 0:RH], ssq[0:R, 0:RH], 1.0 / RDV, EPS, ALU.mult, ALU.add))
                inv_root(rstd[0:R, 0:RH], RH, R)
                if i:
                    dve.wait_ge(rm_ps, i)
                a = h_a[0:R, :].rearrange("p (j n) -> p j n", j=4)
                step(tt(a, side4[0:R, :, 0:RDV], rstd[0:R, 0:RH].unsqueeze(2).to_broadcast([R, 4, RDV]), ALU.mult))
                step(tt(o_rows[0:R, 0:4:2, :], a[:, 0:2, :],
                        gate[0:R, t, :].rearrange("p (j n) -> p j n", j=4)[:, 0:4:2, :], ALU.mult))
                step(tt(o_rows[0:R, 1:4:2, :], a[:, 2:4, :],
                        gate[0:R, t, :].rearrange("p (j n) -> p j n", j=4)[:, 1:4:2, :], ALU.mult))
                dve.sem_inc(ro_rows, 1)
                dve.wait_ge(st_ps, i + 2)
                step(tt(state_tmp[:, :, :], ps_state, state[:, :, :], ALU.add))
                tt(state[:, :, :], state_tmp[:, :, :],
                   decay[:, 1 if t == TAIL else 0, :].unsqueeze(2).to_broadcast([P, 2, RDV]), ALU.mult
                   ).then_inc(st_new, 1)
                dve.wait_ge(rm_ps, i + 1)
                if i:
                    dve.wait_ge(rm_hi, i)
                tt(part[:, 0, :, 0:R], side3[:, :].rearrange("p (j n) -> p j n", j=4)[:, :, 0:R],
                   retgT[:, :].unsqueeze(2).to_broadcast([P, 4, R]), ALU.mult).then_inc(rm_part, 1)
                dve.wait_ge(rm_hi, i + 1)
                dst = (slice(None), slice(0, 4), slice(P * t, P * t + R))
                tt(xT_lo[dst], part[:, 0, :, 0:R], xT_hi[dst].bitcast(F32), ALU.subtract).then_inc(rm_lo, 1)

            for n in range(2):
                for t in range(NT):
                    R = out_rows(t)
                    dve.wait_ge(acc_done, NT * (len(CHUNKS) + n) + t + 1)
                    step(tt(x_sb[0:R, t, 512 * n:512 * n + 512], x_sb[0:R, t, 512 * n:512 * n + 512],
                            acc[0:R, t, :], ALU.add))
                    dve.sem_inc(acc_free, 1)
                    dve.sem_inc(x2_done, 1)
            step(nc.vector.memset(logits[:, :, :], 0.0))
            for t in range(NT):
                R = out_rows(t)
                dve.wait_ge(sq2, t + 1)
                step(ts(ms[0:R, 0:1], ssq[0:R, 0:1], 1.0 / D, EPS, ALU.mult, ALU.add))
                if t:
                    dve.wait_ge(hn_rows, t)
                inv_root(rstd[0:R, 0:1], 1, R)
                dve.sem_inc(rstd2, 1)
                dve.wait_ge(hT_ps, t + 1)
                if t:
                    dve.wait_ge(lg_ps, t)
                tt(hnT[:, :, 0:R], side[:, :, :, :].rearrange("p b h (m n) -> p (b h m) n", m=2)[:, :, 0:R],
                   g2T[:, :].unsqueeze(2).to_broadcast([P, KD, R]), ALU.mult).then_inc(hT_ev, 1)
                dve.wait_ge(lg_ps, t + 1)
                nc.vector.tensor_copy(logits[0:R, t, :], side3[0:R, 0:NG + NE]).then_inc(lg_ev, 1)

            dve.wait_ge(lg_ev, NT)
            gl = logits[:, :, 0:NG]
            col = lambda lo: small[:, lo:lo + NT]

            def wide(ap, n):
                return ap.unsqueeze(2).to_broadcast([P, NT, n])

            def first_of(oh_out, vals, top, n):
                c = cand[:, :, 0:n]
                step(tt(c, vals, wide(top, n), ALU.is_equal))
                step(ts(small[:, 100:100 + n], iota[:, 0:n], -OFF, None, ALU.add))
                step(tt(c, c, small[:, 100:100 + n].unsqueeze(1).to_broadcast([P, NT, n]), ALU.mult))
                step(red(col(120), c, AX_X, ALU.min))
                step(tt(oh_out, c, wide(col(120), n), ALU.is_equal))

            step(red(col(30), gl, AX_X, ALU.max))
            step(tt(r4[:, :, :], gl, wide(col(30), NG), ALU.subtract))
            dve.sem_inc(r_exp, 1)
            first_of(oh_g[:, :, :], gl, col(30), NG)
            e4 = logits[:, :, NG:].rearrange("p t (g e) -> p t g e", g=NG)
            for t in range(NT):
                step(tt(r32[:, t], e4[:, t], oh_g[:, t, :].unsqueeze(2).to_broadcast([P, NG, EPG]), ALU.mult))
            step(red(el[:, :, :], r32[:, :, :, :].rearrange("p t g e -> p t e g"), AX_X, ALU.add))
            step(red(col(35), el[:, :, :], AX_X, ALU.max))
            first_of(oh_e[:, 0], el[:, :, :], col(35), EPG)
            step(stt(out=el2[:, :, :], in0=oh_e[:, 0], scalar=NEG, in1=el[:, :, :], op0=ALU.mult, op1=ALU.add))
            step(red(col(40), el2[:, :, :], AX_X, ALU.max))
            first_of(oh_e[:, 1], el2[:, :, :], col(40), EPG)
            step(tt(col(25), col(40), col(35), ALU.subtract))
            dve.sem_inc(r_exp, 1)
            for k in range(2):
                for g in range(NG):
                    step(tt(oh[:, k, :, EPG * g:EPG * g + EPG], oh_e[:, k],
                            wide(oh_g[:, :, g], EPG), ALU.mult))
            step(tt(chosen[:, :, :], oh[:, 0], oh[:, 1], ALU.add))
            step(nc.vector.memset(chosen[DEC:, TAIL, :], 0.0))
            dve.sem_inc(m_ready, 1)
            dve.wait_ge(r_expd, 2)
            step(red(col(50), r4b[:, :, :], AX_X, ALU.add))
            step(ts(col(55), col(20), 1.0, None, ALU.add))
            step(tt(col(50), col(50), col(55), ALU.mult))
            step(nc.vector.reciprocal(w_k[:, 0, :], col(50)))
            step(tt(w_k[:, 1, :], w_k[:, 0, :], col(20), ALU.mult))
            for k in range(2):
                for t in range(NT):
                    o2 = oh[:, k, t, :].rearrange("p (a b) -> p a b", b=2)
                    j = k * NT + t
                    step(tt(pair_tok[:, j, :], o2[:, :, 0], o2[:, :, 1], ALU.add))
                    step(ts(pair_tok[:, j, :], pair_tok[:, j, :], const("token")[:, t:t + 1], None, ALU.mult))
            dve.wait_ge(rank_ps, 1)
            step(nc.vector.tensor_copy(rank[:, :, :], side3[:, 0:NE * NT].rearrange("p (t e) -> p t e", t=NT)))
            step(red(most[:, :], side3[:, NE * NT:NE * NT + NE], AX_X, ALU.max))
            step(nc.vector.tensor_copy(most_i[:, :], most[:, :]))
            e_row = const("expert_row0").unsqueeze(1).to_broadcast([P, NT, NE])
            p_row = const("pair_row0").unsqueeze(1).to_broadcast([P, NT, NE])

            def pick(dst, values):
                for k in range(2):
                    step(tt(tmp_k[:, k], oh[:, k], values, ALU.mult))
                step(red(dst, tmp_k[:, :, :, :].rearrange("p k t e -> p (k t) e"), AX_X, ALU.add))

            pick(rank_k[:, :], rank[:, :, :])
            pick(row_k[:, :], p_row)
            pick(slot_f[:, :], e_row)
            step(nc.vector.tensor_copy(slot_i[:, :], rank_k[:, :]))
            step(ts(slot_i[:, :], slot_i[:, :], CAP.bit_length() - 1, None, ALU.logical_shift_right))
            step(nc.vector.tensor_copy(lvl_a[:, :], slot_i[:, :]))
            step(tt(slot_f[:, :], slot_f[:, :], rank_k[:, :], ALU.add))
            step(stt(out=slot_f[:, :], in0=lvl_a[:, :], scalar=float((NE - 1) * CAP), in1=slot_f[:, :],
                     op0=ALU.mult, op1=ALU.add))
            step(nc.vector.tensor_copy(slot_i[:, :], slot_f[:, :]))
            step(tt(row_k[:, :], row_k[:, :], rank_k[:, :], ALU.add))
            step(nc.vector.memset(level0[:, :], 0.0))

            def rows_of_level(one):
                one(ts(lvl_a[:, :], rank_k[:, :], level0[:, 0:1], None, ALU.subtract))
                one(ts(lvl_b[:, :], lvl_a[:, :], float(CAP), 1000.0, ALU.is_ge, ALU.mult))
                one(ts(lvl_a[:, :], lvl_a[:, :], 0.0, 1000.0, ALU.is_lt, ALU.mult))
                one(tt(lvl_a[:, :], lvl_a[:, :], lvl_b[:, :], ALU.add))
                one(tt(lvl_a[:, :], lvl_a[:, :], row_k[:, :], ALU.add))
                one(ts(row_l[:, :], lvl_a[:, :], level0[:, 0:1], None, ALU.subtract))
                for j in range(2 * NT):
                    one(ts(row_oh[:, j, :], iota, row_l[:, j:j + 1], None, ALU.is_equal))

            rows_of_level(step)
            dve.sem_inc(oh_ready, 1)
            dve.wait_ge(idx_ps, 1)
            step(nc.vector.tensor_copy(idx[:, :], side3[:, 256:256 + NPAIR]))
            dve.sem_inc(slots_ready, 1)
            dve.sem_inc(idx_ready, 1)

            def rows_in(p, u, first):
                dve.wait_ge(xg_ps, p + 1)
                if not first:
                    dve.wait_ge(gu_ps, p - 1)
                tt(xgT[:, u], sideb[:, :, :].rearrange("p b (j n) -> p (b j) n", j=4),
                   g2T[:, :].unsqueeze(2).to_broadcast([P, KD, P]), ALU.mult).then_inc(xg_ev, 1)

            def glu_steps(u, wait):
                ts(glu[:, 1, :], glu[:, 0, :], 1.0, None, ALU.add).then_inc(glu_step, 1)
                dve.wait_ge(glu_step, wait + 1)
                nc.vector.reciprocal(glu[:, 2, :], glu[:, 1, :]).then_inc(glu_step, 1)
                dve.wait_ge(glu_step, wait + 2)
                tt(glu[:, 1, :], glu[:, 2, :], acc[:, u, 0:FF], ALU.mult).then_inc(glu_step, 1)
                dve.wait_ge(glu_step, wait + 3)
                return tt(actv[:, :], glu[:, 1, :], acc[:, u, FF:2 * FF], ALU.mult)

            def act_in(p, u, first):
                dve.wait_ge(e_exp, p + 1)
                if not first:
                    dve.wait_ge(aT_ps, p)
                glu_steps(u, p * 3).then_inc(e_act, 1)

            def actT_in(p, first):
                dve.wait_ge(aT_ps, p + 1)
                if not first:
                    dve.wait_ge(y_ps, p)
                nc.vector.tensor_copy(actT[:, :, :], side3[:, 0:2 * P].rearrange("p (j n) -> p j n", j=2)
                                      ).then_inc(aT_ev, 1)

            rows_in(0, 0, True)
            rows_in(1, 1, True)
            act_in(0, 0, True)
            actT_in(0, True)
            with dve.Fori(1, NPAIR // 2) as i:
                rows_in(i * 2, 0, False)
                act_in(i * 2 - 1, 1, False)
                actT_in(i * 2 - 1, False)
                rows_in(i * 2 + 1, 1, False)
                act_in(i * 2, 0, False)
                actT_in(i * 2, False)
            act_in(NPAIR - 1, 1, False)
            actT_in(NPAIR - 1, False)

            n_most = dve.value_load(most_i[0:1, 0:1], min_val=0, max_val=T_TOK)
            with dve.If(n_most > CAP):
                with dve.Fori(1, LEVELS) as lv:
                    seen = [0]

                    def one(ins):
                        ins.then_inc(L_step, 1)
                        seen[0] += 1
                        dve.wait_ge(L_step, (lv - 1) * PER_LEVEL + seen[0])

                    one(ts(level0[:, :], level0[:, :], float(CAP), None, ALU.add))
                    rows_of_level(one)
                    assert seen[0] == PER_LEVEL
                    dve.sem_inc(L_oh, 1)
                    dve.wait_ge(L_ips, lv)
                    dve.wait_ge(L_xt, (lv - 1) * NPAIR)
                    nc.vector.tensor_copy(idx[:, :], side3[:, 256:256 + NPAIR]).then_inc(L_idx, 1)
                    with dve.Fori(0, NPAIR) as p:
                        it = (lv - 1) * NPAIR + p
                        dve.wait_ge(L_xt, it + 1)
                        tt(xgT[:, 0], sideb[:, :, :].rearrange("p b (j n) -> p (b j) n", j=4),
                           g2T[:, :].unsqueeze(2).to_broadcast([P, KD, P]), ALU.mult).then_inc(L_xe, 1)
                        dve.wait_ge(L_ex, it + 1)
                        glu_steps(0, (NPAIR + it) * 3).then_inc(L_act, 1)
                        dve.wait_ge(L_at, it + 1)
                        nc.vector.tensor_copy(actT[:, :, :], side3[:, 0:2 * P].rearrange("p (j n) -> p j n", j=2)
                                              ).then_inc(L_ae, 1)

            for t in range(NT):
                R = out_rows(t)
                dve.wait_ge(yg_in[t], 32)
                for k in range(2):
                    step(stt(out=x_sb[0:R, t, :], in0=y_tok[0:R, t, k, :], scalar=w_k[0:R, k, t:t + 1],
                             in1=x_sb[0:R, t, :], op0=ALU.mult, op1=ALU.add))
                dve.sem_inc(y_fin, 1)


_INS = ["x_prompt", "x_sample", "cache_ret_state", "cache_swa_k", "cache_swa_v", "meta_tokens", "norm1_g",
        "w_in", "q_norm_g", "k_norm_g", "ret_norm_g", "attn_sinks", "w_out", "norm2_g", "w_group",
        "w_expert", "w_gate", "w_up", "w_down"]
_OUTS = [(1, SEQ, D), (1, DEC, D), (1, 1, RH, RDK, RDV), (1, 1, WINDOW, 2, HD), (1, 1, WINDOW, 2, HD),
         (1, 1, RH, RDK, RDV), (1, 1, WINDOW, 2, HD), (1, 1, WINDOW, 2, HD)]


def kernel(**inputs):
    import numpy as _np
    import concourse.bacc as _bacc
    from concourse import mybir as _mybir
    from concourse.bass_utils import run_bass_kernel_spmd as _run

    nc = _bacc.Bacc("TRN2", target_bir_lowering=False, num_devices=1)
    table, _ = constants()
    arrays, args = {"in_consts_dram": table}, []
    args.append(nc.dram_tensor("in_consts_dram", table.shape, _mybir.dt.float32, kind="ExternalInput").ap())
    for name in _INS:
        a = _np.ascontiguousarray(inputs[name])
        if name == "ret_norm_g":
            a = _np.ascontiguousarray(a.reshape(RH, RDV).T)
        arrays[f"in_{name}_dram"] = a
        args.append(nc.dram_tensor(f"in_{name}_dram", a.shape, _mybir.dt.from_np(a.dtype), kind="ExternalInput").ap())
    for i, shape in enumerate(_OUTS):
        args.append(nc.dram_tensor(f"out_{i}_dram", shape, _mybir.dt.float32, kind="ExternalOutput").ap())
    stream_step(nc, *args)
    r = _run(nc, [arrays], core_ids=[0])
    return tuple(r.results[0][f"out_{i}_dram"] for i in range(len(_OUTS)))
```

```python
from contextlib import ExitStack

import numpy as np

import concourse.bass as bass
from concourse import mybir

ALU = mybir.AluOpType
ACT = mybir.ActivationFunctionType
F32 = mybir.dt.float32
F32R = mybir.dt.float32r
I32 = mybir.dt.int32
AX_X = mybir.AxisListType.X

P = 128
D = 1024
KD = D // P
SEQ, DEC, NMETA = 512, 64, 16
T_TOK = SEQ + DEC
T_ALL = T_TOK + NMETA
NT = 5
TAIL = 4
CH = 64
PAST = 512
RH, RDK, RDV = 4, 64, 128
QH, HD = 8, 64
WINDOW = 128
BAND = WINDOW + CH
KEYS = BAND + NMETA
CACHE0 = T_ALL
NG, EPG = 4, 8
NE = NG * EPG
NPAIR = NE // 2
FF = 256
CAP = 64
LEVELS = T_TOK // CAP
PER_LEVEL = 17
EPS = 1e-6
NEG = -1e30
OFF = 64.0

C_RQK, C_RV, C_RG, C_SQ, C_SKV = 0, 512, 1024, 1536, 2048
CHUNKS = [(C_SKV, 256), (C_SQ, 512), (C_RQK, 512), (C_RV, 512), (C_RG, 512)]
SKV, SQ, RQK, RV, RG = range(5)
RING = 4
OUT_K = [4, 5, 6, 7, 0, 1, 2, 3]


ORDER = [TAIL, 0, 1, 2, 3]
UNITS = [(t, g, hh) for t in ORDER for g in range(2) for hh in range(2)]
RUNITS = [(t, par) for t in ORDER for par in range(2)]
OUT0 = len(CHUNKS)


def plan():
    slots = KD * (len(CHUNKS) + 2)
    before = [[] for _ in range(slots)]
    after = [[] for _ in range(slots)]
    for c in range(len(CHUNKS) + 1):
        after[KD * c + KD - 1] += [("evict", c, t) for t in range(NT)]
    for i, t in enumerate(ORDER):
        after[KD * SQ + i].append(("post", SKV, t))
        after[KD * SQ + i + 1].append(("kT", t))
        after[KD * RQK + i].append(("post", SQ, t))
        after[KD * RQK + i + 1].append(("qT", t))
        after[KD * RV + i].append(("post", RQK, t))
        after[KD * OUT0 + i // 2].append(("post", RG, t))
    after[KD * SQ - 1].append(("meta_v",))
    after[KD * RQK - 1].append(("kv_out",))
    u0 = KD * RQK + 4
    for n in range(len(UNITS)):
        s = u0 + n
        before[s + 1].append(("norm", n))
        before[s + 2].insert(0, ("pT", n))
        after[s + 2].append(("value", n))
        after[s].append(("score", n))
    tail = [[] for _ in range(len(RUNITS) + 3)]
    for m, (t, par) in enumerate(RUNITS):
        if par == 0:
            tail[m].append(("rT", t))
        if m < 2:
            tail[m].append(("meta_state", par))
        tail[m].append(("ra", m))
        if m:
            tail[m].append(("ro", m - 1))
        if m > 1:
            tail[m].append(("rm", m - 2))
        if m:
            tail[m].append(("rn", m - 1))
    n = len(RUNITS)
    tail[n] += [("ro", n - 1), ("rm", n - 2), ("rn", n - 1)]
    tail[n + 1] += [("rm", n - 1)]
    lone = KD * OUT0 + 4
    first = lone - 2
    for s in range(first, lone):
        after[s] += tail[s - first]
    tail[-1].append(("states_out",))
    for t in range(NT):
        s = KD * (OUT0 + 1) + t
        after[s].append(("square", 0, t))
        after[s].append(("hT", 0, t))
        after[s + 1].append(("logit", 0, t))
    order = []
    for s in range(slots):
        if s == lone:
            for x in tail[lone - first:]:
                order += x
        order += before[s] + [("piece", s // KD, s % KD)] + after[s]
    for t in range(NT):
        order += [("evict", OUT0 + 1, t), ("square", 1, t), ("hT", 1, t)]
        if t:
            order.append(("logit", 1, t - 1))
    order.append(("logit", 1, NT - 1))
    free, held, steps = [0, 1, 2], {}, []
    last = {"kT": "kT", "qT": "qT", "rT": "rT", "meta_state": "meta_state", "score": "value", "ra": "rm",
            "hT": "logit"}
    unit = {"score": "u", "norm": "u", "pT": "u", "value": "u", "ra": "r", "ro": "r", "rn": "r", "rm": "r"}
    for x in order:
        kind, key = x[0], (unit.get(x[0], "h" if x[0] in ("hT", "logit") else x[0]),) + x[1:]
        if kind in last:
            held[key] = free.pop(0)
        bank = held.get(key)
        steps.append(x + (bank,))
        if kind in last.values() and key in held:
            free.append(held.pop(key))
    return steps


def rows_of(t):
    return P if t < TAIL else DEC + NMETA


def out_rows(t):
    return P if t < TAIL else DEC


def constants():
    p = np.arange(P)
    at, cols = {}, []

    def put(name, a):
        a = np.asarray(a, np.float32).reshape(P, -1)
        lo = sum(c.shape[1] for c in cols)
        at[name] = (lo, lo + a.shape[1])
        cols.append(a)

    put("ident", np.eye(P))
    put("causal", p[None, :] >= p[:, None])
    put("before", p[:, None] < p[None, :])
    put("ones", np.ones((P, P)))
    put("iota", np.tile(p, (P, 1)))
    pos = np.zeros((NT, P), np.float32)
    for t in range(TAIL):
        pos[t] = NMETA + P * t + p
    pos[TAIL, :DEC] = NMETA + PAST + np.arange(DEC)
    pos[TAIL, DEC:DEC + NMETA] = np.arange(NMETA)
    half = HD // 2
    inv = np.float32(10000.0) ** (-np.arange(half, dtype=np.float32) / np.float32(half))
    ang = pos[:, :, None] * inv
    cos, sin = np.cos(ang), np.sin(ang)
    put("cos", np.concatenate([cos, cos], -1).transpose(1, 0, 2))
    put("sin", np.concatenate([-sin, sin], -1).transpose(1, 0, 2))
    gamma = 1.0 - 2.0 ** (-5.0 - np.arange(RH))
    step = np.stack([p, np.where(p < DEC, p, p - DEC)], 0)[..., None] + 1.0
    q_scale = gamma ** step
    k_scale = gamma ** -step * RDK ** -0.5
    put("ret_scale", np.concatenate([q_scale, k_scale], -1).transpose(1, 0, 2))
    head = 2 * np.arange(2)[None, :] + (p[:, None] >= 64)
    put("decay", np.stack([gamma[head] ** n for n in (P, DEC, NMETA)], 1))
    tok = np.arange(NT)[None, :] * P + p[:, None]
    put("token", np.where(tok < T_TOK, tok, 0))
    put("expert_row0", np.tile(np.arange(NE) * CAP, (P, 1)))
    put("pair_row0", np.tile(np.arange(NE) % 2 * CAP, (P, 1)))
    return np.ascontiguousarray(np.concatenate(cols, 1)), at


def stream_step(nc, consts, x_prompt, x_sample, cache_ret_state, cache_swa_k, cache_swa_v,
                meta_tokens, norm1_g, w_in, q_norm_g, k_norm_g, ret_norm_g, attn_sinks, w_out,
                norm2_g, w_group, w_gate, w_up, w_down,
                y_prompt, y_sample, ret_prompt, k_prompt, v_prompt, ret_sample, k_sample,
                v_sample):
    _, at = constants()
    NCONST = consts.shape[1]

    hn_d = nc.dram_tensor("hn_d", [T_TOK, D], F32, kind="Internal").ap()
    y_d = nc.dram_tensor("y_d", [LEVELS * NE * CAP, D], F32, kind="Internal").ap()
    y_pairs = y_d.rearrange("(q r) d -> q r d", r=2 * CAP)

    w_in_v = w_in.rearrange("o (p k) n -> p (o k) n", p=P)
    w_out_v = w_out.rearrange("o (k p) n -> p (o k) n", p=P)
    gate_v = w_gate.rearrange("o e (p k) f -> (o e) p (k f)", p=P)
    up_v = w_up.rearrange("o e (p k) f -> (o e) p (k f)", p=P)
    down_v = w_down.rearrange("o e (p j) n -> (o e) p (j n)", p=P)

    with ExitStack() as ctx:
        def sb(name, shape, dt=F32):
            return ctx.enter_context(nc.sbuf_tensor(name, shape, dt))

        def sem(name):
            return ctx.enter_context(nc.semaphore(name))

        cst = sb("cst", [P, NCONST])

        def const(name, rows=P):
            return cst[0:rows, at[name][0]:at[name][1]]

        ident, iota, ones = const("ident"), const("iota"), const("ones")
        cos_t = const("cos").rearrange("p (t d) -> p t d", t=NT)
        sin_t = const("sin").rearrange("p (t d) -> p t d", t=NT)
        ret_scale = const("ret_scale").rearrange("p (a h) -> p a h", a=2)
        decay = const("decay").rearrange("p (a h) -> p a h", a=3)
        x_sb = sb("x_sb", [P, NT, D])
        g1T = sb("g1T", [P, KD])
        g2_both = sb("g2_both", [P, 2, KD])
        g2T = g2_both[:, 0, :]
        retgT = sb("retgT", [P, RH])
        qk_g = sb("qk_g", [P, 2, HD])
        sinks = sb("sinks", [P, QH])
        w_router = sb("w_router", [P, KD, NG + NE])
        small = sb("small", [P, 160])
        soft = sb("soft", [P, 3, 16])
        ssq2 = sb("ssq2", [P, 2, NT])
        rstd2 = sb("rstd2", [P, NT])
        ms = sb("ms", [P, 8])
        xsq = sb("xsq", [P, 512])
        root = sb("root", [P, 4, 8])
        rstd = sb("rstd", [P, 8])
        rstd1 = sb("rstd1", [P, NT])
        ssq = sb("ssq", [P, 8])

        attn = ExitStack()

        def sba(name, shape, dt=F32):
            return attn.enter_context(nc.sbuf_tensor(name, shape, dt))

        state_p = sba("state_p", [P, 2, RDV])
        state_s = sba("state_s", [P, 2, RDV])
        rope_g = sba("rope_g", [P, 2, 2, NT, HD])
        rqk = sba("rqk", [P, NT, 512])
        rv = sba("rv", [P, NT, 512])
        gate = sba("gate", [P, NT, 512])
        sk = sba("sk", [P, NT, P])
        sv = sba("sv", [P, NT, P])
        rT = sba("rT", [P, 4, T_ALL])
        sqT = sba("sqT", [P, 4, T_ALL])
        skT = sba("skT", [P, T_ALL + WINDOW])
        cache_k = sba("cache_k", [P, P])
        cache_v = sba("cache_v", [P, P])
        v_shift = sba("v_shift", [P, 4, P])
        v_own = sba("v_own", [P, 8, P])
        h_a = sba("h_a", [P, 512])
        h_b = sba("h_b", [P, 512])
        squares = sba("squares", [P, 3, 256])
        h_sq = squares[:, :, :].rearrange("p a n -> p (a n)")[:, 0:512]
        probs = sba("probs", [P, 3, 2, KEYS])
        probsT = sba("probsT", [P, 3, 2, 2, P])
        ret_aT = sba("ret_aT", [P, 3, 2, P])
        o_rows = sba("o_rows", [P, 3, 2, P])
        part_r = sba("part_r", [P, 3, 2, P])
        part = rv[:, 0:2, :].rearrange("p a (j n) -> p a j n", j=4)
        mix_lo = sba("mix_lo", [P, 4, T_ALL], F32R)
        with nc.sbuf_tensor("sq", [P, NT, 4, 2, HD], F32) as sq:
            pass
        mix_hi = sba("mix_hi", [P, NT * 512], F32R)[:, 0:4 * T_ALL].rearrange("p (j n) -> p j n", j=4)
        xT_hi = sba("xT_hi", [P, KD, T_ALL], F32R)
        xT_lo = sba("xT_lo", [P, KD, T_ALL], F32R)
        w_raw = sba("w_raw", [P, RING, 512])
        w_hi = sba("w_hi", [P, RING, 512], F32R)
        w_lo = sba("w_lo", [P, RING, 512], F32R)
        attn.close()

        w_moe = sb("w_moe", [P, 2, 2, 3, KD * FF])
        rows = sb("rows", [P, 2, D])
        xg = rows
        y_sb = sb("y_sb", [P, 2, D])
        xgT = sb("xgT", [P, 2, KD, P])
        glu = sb("glu", [P, 3, FF])
        actv = sb("actv", [P, FF])
        actT = sb("actT", [P, 2, P])
        chosen = sb("chosen", [P, NT, NE])
        rank = sb("rank", [P, NT, NE])
        hnT = sb("hnT", [P, 3, 4, P])
        logits = sb("logits", [P, NT, NG + NE])
        r4 = sb("r4", [P, NT, NG])
        r4b = sb("r4b", [P, NT, NG])
        oh_g = sb("oh_g", [P, NT, NG])
        r32 = sb("r32", [P, NT, NG, EPG])
        el = sb("el", [P, NT, EPG])
        el2 = sb("el2", [P, NT, EPG])
        cand = sb("cand", [P, NT, EPG])
        oh_e = sb("oh_e", [P, 2, NT, EPG])
        oh = sb("oh", [P, 2, NT, NE])
        tmp_k = sb("tmp_k", [P, 2, NT, NE])
        rank_k = sb("rank_k", [P, 2 * NT])
        row_k = sb("row_k", [P, 2 * NT])
        row_l = sb("row_l", [P, 2 * NT])
        lvl_a = sb("lvl_a", [P, 2 * NT])
        lvl_b = sb("lvl_b", [P, 2 * NT])
        level0 = sb("level0", [P, 1])
        slot_f = sb("slot_f", [P, 2 * NT])
        slot_i = sb("slot_i", [P, 2 * NT], I32)
        pair_tok = sb("pair_tok", [P, 2 * NT, NPAIR])
        row_oh = sb("row_oh", [P, 2 * NT, P])
        idx = sb("idx", [P, NPAIR], I32)
        idx_now = sb("idx_now", [P, 2, 1], I32)
        most = sb("most", [P, 1])
        most_i = sb("most_i", [P, 1], I32)
        w_k = sb("w_k", [P, 2, NT])
        y_tok = w_moe[:, 0].rearrange("p e m n -> p (e m n)")[:, 0:2 * NT * D].rearrange(
            "p (t k d) -> p t k d", t=NT, k=2)

        acc = ctx.enter_context(nc.psum_tensor("acc", [P, NT, 512], F32))
        side = ctx.enter_context(nc.psum_tensor("side", [P, 3, 512], F32))
        side3 = side[:, 2, :]

        c_in = sem("c_in")
        x_in = [sem(f"x_in{t}") for t in range(NT)]
        g_in = sem("g_in")
        kv_in = sem("kv_in")
        raw_in = [sem(f"raw_in{s}") for s in range(RING)]
        hi_done = sem("hi_done")
        split = sem("split")
        piece_used = sem("piece_used")
        xt_ps = sem("xt_ps")
        xt_part = sem("xt_part")
        xt_hi = sem("xt_hi")
        xt_lo = sem("xt_lo")
        pool_pass = sem("pool_pass")
        ssq_clear = sem("ssq_clear")
        acc_done = sem("acc_done")
        acc_free = sem("acc_free")
        ms_ready = sem("ms_ready")
        root_ready = sem("root_ready")
        rstd_ready = sem("rstd_ready")
        act_step = sem("act_step")
        dve_step = sem("dve_step")
        raw_sq = sem("raw_sq")
        raw_sq_used = sem("raw_sq_used")
        posted = sem("posted")
        k_ps = sem("k_ps")
        q_ps = sem("q_ps")
        r_ps = sem("r_ps")
        mix_clear = sem("mix_clear")
        gate_z = sem("gate_z")
        gate_rows = sem("gate_rows")
        shift_in = sem("shift_in")
        vmeta = sem("vmeta")
        qT_ev = sem("qT_ev")
        kT_ev = sem("kT_ev")
        rT_ev = sem("rT_ev")
        s_ps = sem("s_ps")
        s_max = sem("s_max")
        s_exp = sem("s_exp")
        s_prob = sem("s_prob")
        pT_ps = sem("pT_ps")
        pT_ev = sem("pT_ev")
        o_ps = sem("o_ps")
        o_hi = sem("o_hi")
        o_lo = sem("o_lo")
        st_ps = sem("st_ps")
        st_new = sem("st_new")
        ra_ps = sem("ra_ps")
        ra_ev = sem("ra_ev")
        ro_part = sem("ro_part")
        ro_cross = sem("ro_cross")
        ro_ps = sem("ro_ps")
        ro_sq = sem("ro_sq")
        ro_rows = sem("ro_rows")
        rm_ps = sem("rm_ps")
        rm_part = sem("rm_part")
        rm_hi = sem("rm_hi")
        rm_lo = sem("rm_lo")
        x2_done = sem("x2_done")
        sq2 = sem("sq2")
        rstd2_rdy = sem("rstd2_rdy")
        hn_rows = sem("hn_rows")
        hn_out = [sem(f"hn_out{b}") for b in range(2)]
        hT_ps = sem("hT_ps")
        hT_ev = sem("hT_ev")
        lg_ps = sem("lg_ps")
        lg_ev = sem("lg_ev")
        r_exp = sem("r_exp")
        r_expd = sem("r_expd")
        m_ready = sem("m_ready")
        rank_ps = sem("rank_ps")
        oh_ready = sem("oh_ready")
        idx_ps = sem("idx_ps")
        idx_ready = sem("idx_ready")
        slots_ready = sem("slots_ready")
        gu_in = [sem(f"gu_in{u}") for u in range(2)]
        dn_in = [sem(f"dn_in{u}") for u in range(2)]
        idx_c = sem("idx_c")
        xg_in = [sem(f"xg_in{u}") for u in range(2)]
        xg_ps = sem("xg_ps")
        xg_ev = sem("xg_ev")
        gu_ps = sem("gu_ps")
        e_exp = sem("e_exp")
        e_act = sem("e_act")
        aT_ps = sem("aT_ps")
        aT_ev = sem("aT_ev")
        y_ps = sem("y_ps")
        y_ev = sem("y_ev")
        y_out = [sem(f"y_out{u}") for u in range(2)]
        L_idx = sem("L_idx")
        L_col = sem("L_col")
        L_w = sem("L_w")
        L_xg = sem("L_xg")
        L_xt = sem("L_xt")
        L_xe = sem("L_xe")
        L_gu = sem("L_gu")
        L_ex = sem("L_ex")
        L_act = sem("L_act")
        L_at = sem("L_at")
        L_ae = sem("L_ae")
        L_y = sem("L_y")
        L_ye = sem("L_ye")
        L_out = sem("L_out")
        L_step = sem("L_step")
        glu_step = sem("glu_step")
        L_oh = sem("L_oh")
        L_ips = sem("L_ips")
        yg_in = [sem(f"yg_in{t}") for t in range(NT)]
        y_fin = sem("y_fin")
        fin_out = sem("fin_out")
        st_out = sem("st_out")
        kv_out = sem("kv_out")

        STEPS = plan()
        nth = {}
        for kind in {x[0] for x in STEPS}:
            for i, x in enumerate(y for y in STEPS if y[0] == kind):
                nth[x[:-1]] = i + 1
        st_nth = {}
        for x in STEPS:
            if x[0] in ("meta_state", "ro"):
                st_nth[x[:-1]] = len(st_nth) + 1

        block = ctx.enter_context(nc.Block())

        @block.sync
        def _(sp):
            xp = x_prompt.rearrange("o (t p) d -> p (o t) d", p=P)
            for t in range(TAIL):
                sp.dma_start(x_sb[:, t, :], xp[:, t, :]).then_inc(x_in[t], 16)
                if t == 0:
                    sp.dma_start(cst[:, :], consts).then_inc(c_in, 16)
                    sp.dma_start(g1T[:, :], norm1_g.rearrange("o (p k) -> p (o k)", k=KD)).then_inc(c_in, 16)
            sp.dma_start(x_sb[0:DEC, TAIL, :], x_sample.rearrange("o s d -> (o s) d")).then_inc(x_in[TAIL], 16)
            sp.dma_start(x_sb[DEC:DEC + NMETA, TAIL, :], meta_tokens).then_inc(x_in[TAIL], 16)

            def load_piece(src, width, i, s, first):
                if not first:
                    sp.wait_ge(split, i - RING + 1)
                sp.dma_start(w_raw[:, s, 0:width], src).then_inc(raw_in[s], 16)

            for c, (col, width) in enumerate(CHUNKS):
                if c == 0:
                    for k in range(KD):
                        load_piece(w_in_v[:, k, col:col + width], width, k, k % RING, k < RING)
                    continue
                with sp.Fori(0, KD // RING) as r:
                    for s in range(RING):
                        k = r * RING + s
                        load_piece(w_in_v[:, bass.ds(k, 1), col:col + width].rearrange("p o n -> p (o n)"),
                                   width, k + KD * c, s, False)
            for n in range(2):
                for j, k in enumerate(OUT_K):
                    load_piece(w_out_v[:, k, n * 512:n * 512 + 512], 512, KD * (len(CHUNKS) + n) + j,
                               j % RING, False)

            sp.wait_ge(o_lo, len(UNITS))
            sp.wait_ge(o_hi, len(UNITS))
            sp.wait_ge(rm_lo, len(RUNITS))
            sp.wait_ge(rm_hi, len(RUNITS))
            sp.wait_ge(kv_out, 16 * 6)
            sp.wait_ge(st_out, 16 * 4)

            def load_pair(p, u, first):
                if not first:
                    sp.wait_ge(gu_ps, p - 1)
                for e in range(2):
                    for m, v in enumerate((gate_v, up_v)):
                        sp.dma_start(w_moe[:, u, e, m, :], v[bass.ds(p * 2 + e, 1)].rearrange("o p n -> p (o n)")
                                     ).then_inc(gu_in[u], 16)
                if not first:
                    sp.wait_ge(y_ps, p - 1)
                for e in range(2):
                    sp.dma_start(w_moe[:, u, e, 2, :], down_v[bass.ds(p * 2 + e, 1)].rearrange("o p n -> p (o n)")
                                 ).then_inc(dn_in[u], 16)

            for u in range(2):
                load_pair(u, u, True)
            with sp.Fori(1, NPAIR // 2) as i:
                for u in range(2):
                    load_pair(i * 2 + u, u, False)

            sp.wait_ge(slots_ready, 1)
            n_most = sp.value_load(most_i[0:1, 0:1], min_val=0, max_val=T_TOK)
            with sp.If(n_most > CAP):
                sp.wait_ge(y_ps, NPAIR)
                with sp.Fori(1, LEVELS) as lv:
                    with sp.Fori(0, NPAIR) as p:
                        it = (lv - 1) * NPAIR + p
                        sp.wait_ge(L_y, it + 1)
                        for e in range(2):
                            for m, v in enumerate((gate_v, up_v, down_v)):
                                sp.dma_start(w_moe[:, 0, e, m, :],
                                             v[bass.ds(p * 2 + e, 1)].rearrange("o p n -> p (o n)")
                                             ).then_inc(L_w, 16)
            yp = y_prompt.rearrange("o (t p) d -> p (o t) d", p=P)
            ys = y_sample.rearrange("o s d -> (o s) d")
            for t in range(NT):
                sp.wait_ge(y_fin, t + 1)
                if t < TAIL:
                    sp.dma_start(yp[:, t, :], x_sb[:, t, :]).then_inc(fin_out, 16)
                else:
                    sp.dma_start(ys, x_sb[0:DEC, t, :]).then_inc(fin_out, 16)
            sp.wait_ge(fin_out, 16 * NT)

        @block.gpsimd
        def _(pool):
            rt = w_router[:, :, :]

            def alone():
                pool.sem_inc(pool_pass, 1)

            pool.dma_start(g2_both[:, :, :], norm2_g).then_inc(g_in, 16)
            pool.dma_start(retgT[:, :], ret_norm_g).then_inc(g_in, 16)
            pool.dma_start(qk_g[:, 0, :], q_norm_g.to_broadcast([P, HD])).then_inc(g_in, 16)
            pool.dma_start(qk_g[:, 1, :], k_norm_g.to_broadcast([P, HD])).then_inc(g_in, 16)
            pool.dma_start(sinks[:, :], attn_sinks.to_broadcast([P, QH])).then_inc(g_in, 16)
            pool.dma_start(w_router[:, :, :], w_group).then_inc(g_in, 16)

            def split_piece(i, s, rnd, width, first):
                pool.wait_ge(raw_in[s], (rnd + 1) * 16)
                if not first:
                    pool.wait_ge(piece_used, i - RING + 1)
                    alone()
                nc.gpsimd.tensor_copy(w_hi[:, s, 0:width], w_raw[:, s, 0:width]).then_inc(hi_done, 1)
                pool.wait_ge(hi_done, i + 1)
                nc.gpsimd.tensor_tensor(w_lo[:, s, 0:width], w_raw[:, s, 0:width],
                                        w_hi[:, s, 0:width].bitcast(F32), ALU.subtract).then_inc(split, 1)

            for k in range(KD):
                split_piece(k, k % RING, k // RING, CHUNKS[0][1], k < RING)
            with pool.Fori(2, 2 * (len(CHUNKS) + 2)) as r:
                for s in range(RING):
                    split_piece(r * RING + s, s, r, 512, False)

            def gather(p, u, first):
                if not first:
                    pool.wait_ge(xg_ps, p - 1)
                    alone()
                nc.gpsimd.tensor_copy(idx_now[:, u, :], idx[:, bass.ds(p, 1)]).then_inc(idx_c, 1)
                pool.wait_ge(idx_c, p + 1)
                if not first:
                    alone()
                pool.indirect_dma_start(out=xg[:, u, :], out_offset=None, in_=hn_d,
                                        in_offset=bass.IndirectOffsetOnAxis(ap=idx_now[:, u, 0:1], axis=0)
                                        ).then_inc(xg_in[u], 16)

            pool.wait_ge(hn_out[0], 16 * 3)
            pool.wait_ge(hn_out[1], 16 * 2)
            pool.wait_ge(idx_ready, 1)
            for u in range(2):
                gather(u, u, True)
            with pool.Fori(1, NPAIR // 2) as i:
                for u in range(2):
                    gather(i * 2 + u, u, False)
            pool.wait_ge(slots_ready, 1)
            n_most = pool.value_load(most_i[0:1, 0:1], min_val=0, max_val=T_TOK)
            with pool.If(n_most > CAP):
                pool.wait_ge(xg_ps, NPAIR)
                with pool.Fori(1, LEVELS) as lv:
                    pool.wait_ge(L_idx, lv)
                    alone()
                    with pool.Fori(0, NPAIR) as p:
                        it = (lv - 1) * NPAIR + p
                        pool.wait_ge(L_xt, it + 1)
                        alone()
                        nc.gpsimd.tensor_copy(idx_now[:, 0, :], idx[:, bass.ds(p, 1)]).then_inc(L_col, 1)
                        pool.wait_ge(L_col, it + 1)
                        alone()
                        pool.indirect_dma_start(out=xg[:, 0, :], out_offset=None, in_=hn_d,
                                                in_offset=bass.IndirectOffsetOnAxis(ap=idx_now[:, 0, 0:1], axis=0)
                                                ).then_inc(L_xg, 16)

            def fetch(levels):
                for t in range(NT):
                    for k in range(2):
                        n = out_rows(t)
                        pool.indirect_dma_start(out=y_tok[0:n, t, k, :], out_offset=None,
                                                in_=y_d[0:levels * NE * CAP, :],
                                                in_offset=bass.IndirectOffsetOnAxis(
                                                    ap=slot_i[0:n, k * NT + t:k * NT + t + 1], axis=0)
                                                ).then_inc(yg_in[t], 16)

            for u in range(2):
                pool.wait_ge(y_out[u], 8 * NPAIR)
            pool.wait_ge(y_ps, NPAIR)
            with pool.If(n_most > CAP):
                pool.wait_ge(L_out, 16 * NPAIR * (LEVELS - 1) + 16)
                fetch(LEVELS)
            with pool.If(n_most <= CAP):
                fetch(1)

        @block.tensor
        def _(pe):
            mm = nc.tensor.matmul
            busy = {0: [], 1: [], 2: []}

            def take(b):
                for s, n in busy[b]:
                    pe.wait_ge(s, n)

            pe.wait_ge(c_in, 32)
            n = 0
            for t in range(NT):
                pe.wait_ge(x_in[t], 16 if t < TAIL else 32)
                R = rows_of(t)
                xv = x_sb[0:R, t, :].rearrange("p (q k) -> p k q", k=KD)
                for half in range(2):
                    b = n % 2
                    take(b)
                    for j in range(4):
                        l = nc.tensor.transpose(side[:, b, j * P:j * P + R], xv[:, 4 * half + j, :],
                                                ident[0:R, 0:R])
                    l.then_inc(xt_ps, 1)
                    n += 1
                    busy[b] = [(xt_part, n)]
            pe.wait_ge(xt_lo, 2 * NT)
            pe.wait_ge(xt_hi, 2 * NT)

            def piece(c, kk, b):
                n = KD * c + kk
                s = n % RING
                pe.wait_ge(split, n + 1)
                width = CHUNKS[c][1] if c < OUT0 else 512
                if c < OUT0:
                    a_hi, a_lo = xT_hi[:, kk, :], xT_lo[:, kk, :]
                elif kk < 4:
                    a_hi, a_lo = mix_hi[:, kk, :], mix_lo[:, kk, :]
                    if c == OUT0:
                        pe.wait_ge(mix_clear, 1)
                        pe.wait_ge(o_hi, len(UNITS) - 3 + kk)
                        pe.wait_ge(o_lo, len(UNITS) - 3 + kk)
                else:
                    a_hi, a_lo = xT_hi[:, kk - 4, :], xT_lo[:, kk - 4, :]
                    if c == OUT0 and kk == 4:
                        pe.wait_ge(rm_hi, len(RUNITS))
                        pe.wait_ge(rm_lo, len(RUNITS))
                for t in range(NT):
                    R = rows_of(t)
                    if kk == 0 and c > 0:
                        pe.wait_ge(acc_free, nth["evict", c - 1, t])
                    for j, (a, w) in enumerate(((a_hi, w_hi), (a_hi, w_lo), (a_lo, w_hi))):
                        l = mm(acc[0:R, t, 0:width], a[:, P * t:P * t + R], w[:, s, 0:width],
                               start=(kk == 0 and j == 0), stop=(kk == KD - 1 and j == 2))
                    if kk == KD - 1:
                        l.then_inc(acc_done, 1)
                    elif t == NT - 1:
                        l.then_inc(piece_used, 1)
                if kk == KD - 1:
                    pe.wait_ge(acc_done, NT * (c + 1))
                    pe.sem_inc(piece_used, 1)

            def kT(t, b):
                R = rows_of(t)
                take(b)
                pe.wait_ge(posted, nth["post", SKV, t])
                l = nc.tensor.transpose(side[:, b, 0:R], sk[0:R, t, :], ident[0:R, 0:R])
                if t == TAIL:
                    pe.wait_ge(kv_in, 16 * 4)
                    l = nc.tensor.transpose(side[:, b, P:2 * P], cache_k[:, :], ident)
                l.then_inc(k_ps, 1)
                busy[b] = [(kT_ev, nth["kT", t])]

            def qT(t, b):
                R = rows_of(t)
                take(b)
                pe.wait_ge(posted, nth["post", SQ, t])
                for h in range(4):
                    l = nc.tensor.transpose(side[:, b, h * P:h * P + R],
                                            sq[0:R, t, h, :, :].rearrange("p g d -> p (g d)"), ident[0:R, 0:R])
                l.then_inc(q_ps, 1)
                busy[b] = [(qT_ev, nth["qT", t])]

            def rT_(t, b):
                R = rows_of(t)
                take(b)
                pe.wait_ge(posted, nth["post", RQK, t])
                for j in range(4):
                    l = nc.tensor.transpose(side[:, b, j * P:j * P + R], rqk[0:R, t, j * P:j * P + P],
                                            ident[0:R, 0:R])
                l.then_inc(r_ps, 1)
                busy[b] = [(rT_ev, nth["rT", t])]

            def score(i, b):
                t, g, hh = UNITS[i]
                take(b)
                pe.wait_ge(qT_ev, nth["qT", t])
                pe.wait_ge(kT_ev, NT)
                gs = slice(64 * g, 64 * g + 64)
                keys = []
                for c2 in range(2 if t < TAIL else 1):
                    c = 2 * t + c2
                    if t == TAIL:
                        keys.append([(CACHE0, WINDOW, 0), (SEQ, CH, WINDOW), (T_TOK, NMETA, BAND)])
                    elif c < 2:
                        keys.append([(0, CH * (c + 1), WINDOW - CH * c), (T_TOK, NMETA, BAND)])
                    else:
                        keys.append([(CH * c - WINDOW, BAND, 0), (T_TOK, NMETA, BAND)])
                for hl in range(2):
                    for lots in zip(*keys):
                        for c2, (col, n, dst) in enumerate(lots):
                            c = 2 * t + c2
                            l = mm(side[64 * c2:64 * c2 + 64, b, 256 * hl + dst:256 * hl + dst + n],
                                   sqT[gs, 2 * hh + hl, CH * c:CH * c + CH], skT[gs, col:col + n],
                                   start=True, stop=True)
                l.then_inc(s_ps, 1)

            def probs_T(i, b):
                R = out_rows(UNITS[i][0])
                pe.wait_ge(s_prob, i + 1)
                for hl in range(2):
                    nc.tensor.transpose(side[:, b, hl * P:hl * P + R], probs[0:R, b, hl, 0:P], ident[0:R, 0:R])
                for hl in range(2):
                    l = nc.tensor.transpose(side[0:CH + NMETA, b, 2 * P + hl * P:2 * P + hl * P + R],
                                            probs[0:R, b, hl, P:KEYS], ident[0:R, 0:R])
                l.then_inc(pT_ps, 1)

            def value(i, b):
                t, g, hh = UNITS[i]
                if i == 0:
                    pe.wait_ge(shift_in, 16 * 4)
                    pe.wait_ge(vmeta, 1)
                pe.wait_ge(pT_ev, i + 1)
                n = CH + NMETA
                gc = slice(64 * g, 64 * g + 64)
                for c2 in range(2 if t < TAIL else 1):
                    if t == TAIL:
                        lots = [(cache_v[:, gc], 0, P), (sv[0:n, t, gc], 1, n)]
                    else:
                        before = v_shift[:, t, gc] if c2 else (sv[:, t - 1, gc] if t else None)
                        lots = [(before, 0, P)] if before is not None else []
                        lots.append((v_own[0:n, 2 * t + c2, gc], 1, n))
                    q = slice(64 * c2, 64 * c2 + 64)
                    for j, (v, blk, kn) in enumerate(lots):
                        for hl in range(2):
                            l = mm(side[64 * hl:64 * hl + 64, b, q], v, probsT[0:kn, b, blk, hl, q],
                                   start=(j == 0), stop=(j == len(lots) - 1))
                l.then_inc(o_ps, 1)
                busy[b] = [(o_hi, i + 1), (o_lo, i + 1)]

            def outer(lo, n, t, par, b):
                for hp in range(2):
                    h = 2 * hp + par
                    l = mm(side[64 * par:64 * par + 64, b, P * hp:P * hp + P],
                           rqk[lo:lo + n, t, 256 + 64 * h:256 + 64 * h + 64],
                           rv[lo:lo + n, t, P * h:P * h + P], start=True, stop=True)
                l.then_inc(st_ps, 1)

            def meta_state(par, b):
                take(b)
                pe.wait_ge(acc_free, nth["evict", RV, TAIL])
                pe.wait_ge(posted, nth["post", RQK, TAIL])
                outer(DEC, NMETA, TAIL, par, b)
                busy[b] = [(st_new, st_nth["meta_state", par])]

            def ret_scores(m, b):
                t, par = RUNITS[m]
                R = out_rows(t)
                hs, tok = slice(64 * par, 64 * par + 64), slice(P * t, P * t + R)
                take(b)
                pe.wait_ge(rT_ev, nth["rT", t])
                for hp in range(2):
                    l = mm(side[0:R, b, P * hp:P * hp + R], rT[hs, 2 + hp, tok], rT[hs, hp, tok],
                           start=True, stop=True)
                l.then_inc(ra_ps, 1)

            def ret_out(m, b):
                t, par = RUNITS[m]
                R = out_rows(t)
                state = state_s if t == TAIL else state_p
                hs, tok = slice(64 * par, 64 * par + 64), slice(P * t, P * t + R)
                pe.wait_ge(ra_ev, m + 1)
                outer(0, R, t, par, b)
                if t != TAIL:
                    pe.wait_ge(st_new, st_nth[("ro", m - 2) if t else ("meta_state", par)])
                for hp in range(2):
                    h = 2 * hp + par
                    out = side[0:R, b, 2 * P + P * hp:2 * P + P * hp + P]
                    l = mm(out, ret_aT[0:R, b, hp, 0:R], rv[0:R, t, P * h:P * h + P], start=True, stop=False)
                    if R < P:
                        l.then_inc(ro_part, 1)
                        pe.wait_ge(ro_part, 2 * m + hp + 1)
                    l = mm(out, rT[hs, hp, tok], state[hs, hp, :], start=False, stop=True)
                    if R < P and hp == 0:
                        l.then_inc(ro_cross, 1)
                        pe.wait_ge(ro_cross, m + 1)
                l.then_inc(ro_ps, 1)

            def ret_T(m, b):
                t, par = RUNITS[m]
                R = out_rows(t)
                pe.wait_ge(ro_rows, m + 1)
                pe.wait_ge(st_new, st_nth["ro", m])
                for hp in range(2):
                    l = nc.tensor.transpose(side[:, b, P * hp:P * hp + R], o_rows[0:R, b, hp, :],
                                            ident[0:R, 0:R])
                l.then_inc(rm_ps, 1)
                busy[b] = [(rm_part, m + 1)]

            def hid_T(n, t, b):
                R = out_rows(t)
                take(b)
                pe.wait_ge(acc_free, nth["evict", OUT0 + n, t])
                for j in range(4):
                    lo = 512 * n + P * j
                    l = nc.tensor.transpose(side[:, b, P * j:P * j + R], x_sb[0:R, t, lo:lo + P],
                                            ident[0:R, 0:R])
                l.then_inc(hT_ps, 1)

            def logit(n, t, b):
                R = out_rows(t)
                pe.wait_ge(hT_ev, nth["hT", n, t])
                for j in range(4):
                    l = mm(side[0:R, b, 0:NG + NE], hnT[:, b, j, 0:R], w_router[:, 4 * n + j, :],
                           start=(j == 0), stop=(j == 3))
                l.then_inc(lg_ps, 1)
                busy[b] = [(lg_ev, nth["logit", n, t])]

            does = {"piece": piece, "kT": kT, "qT": qT, "rT": rT_, "score": score, "pT": probs_T,
                    "value": value, "meta_state": meta_state, "ra": ret_scores, "ro": ret_out, "rm": ret_T,
                    "hT": hid_T, "logit": logit}
            for kind, *args in STEPS:
                if kind in does:
                    does[kind](*args)

            pe.wait_ge(m_ready, 1)
            for b in range(3):
                take(b)
            for t in range(NT):
                for t2 in range(t + 1):
                    mm(side3[:, NE * t:NE * t + NE], const("before") if t2 == t else ones, chosen[:, t2, :],
                       start=(t2 == 0), stop=(t2 == t))
            for t in range(NT):
                l = mm(side3[:, NE * NT:NE * NT + NE], ones, chosen[:, t, :], start=(t == 0), stop=(t == NT - 1))
            l.then_inc(rank_ps, 1)
            pe.wait_ge(oh_ready, 1)

            def find_rows():
                for j in range(2 * NT):
                    l = mm(side3[:, 256:256 + NPAIR], row_oh[:, j, :], pair_tok[:, j, :], start=(j == 0),
                           stop=(j == 2 * NT - 1))
                return l

            find_rows().then_inc(idx_ps, 1)

            def rows_T(p, u, wait):
                pe.wait_ge(xg_in[u], wait)
                gv = xg[:, u, :].rearrange("p (q k) -> p k q", k=KD)
                for k in range(KD):
                    l = nc.tensor.transpose(side[:, k // 4, (k % 4) * P:(k % 4) * P + P], gv[:, k, :], ident)
                return l

            def gate_up(u, slot, xu):
                for k in range(KD):
                    for e in range(2):
                        l = mm(acc[64 * e:64 * e + 64, u, :].rearrange("p (m f) -> p m f", m=2),
                               xgT[:, xu, k, 64 * e:64 * e + 64], w_moe[:, slot, e, 0:2, k * FF:k * FF + FF],
                               start=(k == 0), stop=(k == KD - 1))
                return l

            def act_T():
                av = actv[:, :].rearrange("p (q j) -> p j q", j=2)
                for j in range(2):
                    l = nc.tensor.transpose(side3[:, P * j:P * j + P], av[:, j, :], ident)
                return l

            def down(slot):
                for n in range(2):
                    for j in range(2):
                        for e in range(2):
                            l = mm(acc[64 * e:64 * e + 64, 2 + n, :], actT[:, j, 64 * e:64 * e + 64],
                                   w_moe[:, slot, e, 2, j * D + n * 512:j * D + n * 512 + 512],
                                   start=(j == 0), stop=(j == 1))
                return l

            def first_half(p, u, rnd, first):
                if not first:
                    pe.wait_ge(xg_ev, p)
                rows_T(p, u, rnd * 16 + 16).then_inc(xg_ps, 1)
                pe.wait_ge(xg_ev, p + 1)
                pe.wait_ge(gu_in[u], rnd * 64 + 64)
                gate_up(u, u, u).then_inc(gu_ps, 1)

            def second_half(p, u, rnd, first):
                pe.wait_ge(e_act, p + 1)
                act_T().then_inc(aT_ps, 1)
                pe.wait_ge(aT_ev, p + 1)
                pe.wait_ge(dn_in[u], rnd * 32 + 32)
                if not first:
                    pe.wait_ge(y_ev, p)
                down(u).then_inc(y_ps, 1)

            pe.wait_ge(idx_ready, 1)
            pe.wait_ge(acc_free, NT * (OUT0 + 2))
            first_half(0, 0, 0, True)
            first_half(1, 1, 0, False)
            second_half(0, 0, 0, True)
            with pe.Fori(1, NPAIR // 2) as i:
                first_half(i * 2, 0, i, False)
                second_half(i * 2 - 1, 1, i - 1, False)
                first_half(i * 2 + 1, 1, i, False)
                second_half(i * 2, 0, i, False)
            second_half(NPAIR - 1, 1, NPAIR // 2 - 1, False)

            pe.wait_ge(slots_ready, 1)
            n_most = pe.value_load(most_i[0:1, 0:1], min_val=0, max_val=T_TOK)
            with pe.If(n_most > CAP):
                pe.wait_ge(y_ev, NPAIR)
                pe.sem_inc(L_xt, 1)
                pe.sem_inc(L_y, 1)
                with pe.Fori(1, LEVELS) as lv:
                    pe.wait_ge(L_oh, lv)
                    find_rows().then_inc(L_ips, 1)
                    with pe.Fori(0, NPAIR) as p:
                        it = (lv - 1) * NPAIR + p
                        pe.wait_ge(L_xg, it * 16 + 16)
                        rows_T(0, 0, 16).then_inc(L_xt, 1)
                        pe.wait_ge(L_xe, it + 1)
                        pe.wait_ge(L_w, it * 96 + 96)
                        gate_up(0, 0, 0).then_inc(L_gu, 1)
                        pe.wait_ge(L_act, it + 1)
                        act_T().then_inc(L_at, 1)
                        pe.wait_ge(L_ae, it + 1)
                        pe.wait_ge(L_ye, it + 1)
                        down(0).then_inc(L_y, 1)

        @block.scalar
        def _(act):
            af = nc.scalar.activation
            steps = [0]

            def step(ins):
                ins.then_inc(act_step, 1)
                steps[0] += 1
                act.wait_ge(act_step, steps[0])

            roots = [0]
            squared = [0]

            def guess(n, R=P):
                roots[0] += 1
                act.wait_ge(ms_ready, roots[0])
                step(af(root[0:R, 0, 0:n], ms[0:R, 0:n], ACT.Ln))
                af(root[0:R, 1, 0:n], root[0:R, 0, 0:n], ACT.Exp, scale=-0.5).then_inc(root_ready, 1)

            ck = cache_swa_k.rearrange("o b w g d -> (o b w) (g d)")
            cv = cache_swa_v.rearrange("o b w g d -> (o b w) (g d)")
            act.dma_start(cache_k[:, :], ck).then_inc(kv_in, 16)
            act.dma_start(cache_v[:, :], cv).then_inc(kv_in, 16)
            cs = cache_ret_state.rearrange("o b (i h) k v -> (h k) (o b i) v", h=2)
            for i in range(2):
                act.dma_start(state_s[:, i, :], cs[:, i, :]).then_inc(kv_in, 16)

            n = 0
            for t in range(NT):
                R = rows_of(t)
                act.wait_ge(x_in[t], 16 if t < TAIL else 32)
                if t == 0:
                    act.wait_ge(ssq_clear, 1)
                else:
                    act.wait_ge(act_step, steps[0])
                step(af(rqk[0:R, 0:2, :].rearrange("p a n -> p (a n)"), x_sb[0:R, t, :], ACT.Square,
                        accum_out=ssq[0:R, t:t + 1]))
                for half in range(2):
                    n += 1
                    act.wait_ge(xt_part, n)
                    nc.scalar.copy(xT_hi[:, 4 * half:4 * half + 4, P * t:P * t + R],
                                   part[:, half, :, 0:R]).then_inc(xt_hi, 1)
            guess(NT)

            act.wait_ge(rstd_ready, 1)

            def evict(c, t, b):
                if c >= OUT0:
                    return
                R = rows_of(t)
                r1 = rstd1[0:R, t:t + 1]
                act.wait_ge(acc_done, NT * c + t + 1)
                if c == SKV:
                    af(sk[0:R, t, :], acc[0:R, t, 0:P], ACT.Copy, scale=r1)
                    af(sv[0:R, t, :], acc[0:R, t, P:2 * P], ACT.Copy, scale=r1).then_inc(acc_free, 1)
                    return
                dst = {SQ: sq[0:R, t].rearrange("p h g d -> p (h g d)"), RQK: rqk[0:R, t, :],
                       RV: rv[0:R, t, :], RG: gate[0:R, t, :]}[c]
                af(dst, acc[0:R, t, :], ACT.Copy, scale=r1).then_inc(acc_free, 1)

            def post(c, t, b):
                R = rows_of(t)
                act.wait_ge(acc_free, nth["evict", c, t])
                if c == RQK:
                    return
                if squared[0]:
                    act.wait_ge(raw_sq_used, squared[0])
                squared[0] += 1
                if c == RG:
                    af(h_sq[0:R, :], gate[0:R, t, :], ACT.Exp, scale=-1.0).then_inc(raw_sq, 1)
                elif c == SKV:
                    af(h_sq[0:R, 0:P], sk[0:R, t, :], ACT.Square).then_inc(raw_sq, 1)
                    guess(2, R)
                else:
                    af(h_sq[0:R, :], sq[0:R, t].rearrange("p h g d -> p (h g d)"), ACT.Square
                       ).then_inc(raw_sq, 1)
                    guess(QH, R)

            def meta_v(b):
                act.wait_ge(acc_free, NT)
                own = v_own[:, :, :].rearrange("p (t c) d -> p t c d", c=2)
                act.dma_start(v_shift[64:128, :, :], sv[0:64, 0:4, :]).then_inc(shift_in, 16)
                act.dma_start(v_shift[0:64, 1:4, :], sv[64:128, 0:3, :]).then_inc(shift_in, 16)
                act.dma_start(own[0:64, :, 0, :], sv[0:64, 0:4, :]).then_inc(shift_in, 16)
                act.dma_start(own[0:64, :, 1, :], sv[64:128, 0:4, :]).then_inc(shift_in, 16)

            def keys_out(b):
                act.wait_ge(posted, NT)
                for out_p, out_s, rows_, old in ((k_prompt, k_sample, sk, ck), (v_prompt, v_sample, sv, cv)):
                    op = out_p.rearrange("o b w g d -> (o b w) (g d)")
                    os = out_s.rearrange("o b w g d -> (o b w) (g d)")
                    act.dma_start(op, rows_[:, 3, :]).then_inc(kv_out, 16)
                    act.dma_start(os[DEC:, :], rows_[0:DEC, TAIL, :]).then_inc(kv_out, 16)
                    act.dma_start(os[0:WINDOW - DEC, :], old[DEC:, :]).then_inc(kv_out, 16)

            def kT(t, b):
                R = rows_of(t)
                act.wait_ge(k_ps, nth["kT", t])
                if t == TAIL:
                    nc.scalar.copy(skT[:, CACHE0:CACHE0 + P], side[:, b, P:2 * P])
                nc.scalar.copy(skT[:, P * t:P * t + R], side[:, b, 0:R]).then_inc(kT_ev, 1)

            def rT_(t, b):
                R = rows_of(t)
                act.wait_ge(r_ps, nth["rT", t])
                nc.scalar.copy(rT[:, :, P * t:P * t + R],
                               side[:, b, :].rearrange("p (j n) -> p j n", j=4)[:, :, 0:R]).then_inc(rT_ev, 1)

            def score(i, b):
                R = out_rows(UNITS[i][0])
                act.wait_ge(s_max, i + 1)
                for hl in range(2):
                    af(probs[0:R, b, hl, :], side[0:R, b, 256 * hl:256 * hl + KEYS], ACT.Exp,
                       scale=HD ** -0.5, bias=soft[0:R, b, 2 + hl:3 + hl], accum_out=soft[0:R, b, 4 + hl:5 + hl])
                af(soft[0:R, b, 8:10], soft[0:R, b, 6:8], ACT.Exp).then_inc(s_exp, 1)

            def probs_T(i, b):
                R = out_rows(UNITS[i][0])
                act.wait_ge(pT_ps, i + 1)
                nc.scalar.copy(probsT[:, b, 0, :, 0:R],
                               side[:, b, 0:2 * P].rearrange("p (j n) -> p j n", j=2)[:, :, 0:R])
                nc.scalar.copy(probsT[0:CH + NMETA, b, 1, :, 0:R],
                               side[0:CH + NMETA, b, 2 * P:].rearrange("p (j n) -> p j n", j=2)[:, :, 0:R]
                               ).then_inc(pT_ev, 1)

            def value(i, b):
                t, g, hh = UNITS[i]
                R = out_rows(t)
                act.wait_ge(o_ps, i + 1)
                if i == 0:
                    act.wait_ge(mix_clear, 1)
                nc.scalar.copy(mix_hi[:, 2 * g + hh, P * t:P * t + R], side[:, b, 0:R]).then_inc(o_hi, 1)

            def ret_out(m, b):
                R = out_rows(RUNITS[m][0])
                act.wait_ge(ro_ps, m + 1)
                af(squares[0:R, b, :], side[0:R, b, 2 * P:], ACT.Square).then_inc(ro_sq, 1)
                guess(2, R)

            def ret_T(m, b):
                t, par = RUNITS[m]
                R = out_rows(t)
                act.wait_ge(rm_part, m + 1)
                nc.scalar.copy(xT_hi[:, par:4:2, P * t:P * t + R], part_r[:, b, :, 0:R]).then_inc(rm_hi, 1)

            def states_out(b):
                act.wait_ge(st_new, len(st_nth))
                for st, out in ((state_s, ret_sample), (state_p, ret_prompt)):
                    dst = out.rearrange("o b (i h) k v -> (h k) (o b i) v", h=2)
                    for j in range(2):
                        act.dma_start(dst[:, j, :], st[:, j, :]).then_inc(st_out, 16)

            def square(n, t, b):
                R = out_rows(t)
                act.wait_ge(acc_free, nth["evict", OUT0 + n, t])
                act.wait_ge(ssq_clear, 2)
                if nth["square", n, t] > 1:
                    act.wait_ge(sq2, nth["square", n, t] - 1)
                af(xsq[0:R, :], x_sb[0:R, t, 512 * n:512 * n + 512], ACT.Square,
                   accum_out=ssq2[0:R, n, t:t + 1]).then_inc(sq2, 1)

            does = {"evict": evict, "post": post, "meta_v": meta_v, "kv_out": keys_out, "kT": kT, "rT": rT_,
                    "score": score, "pT": probs_T, "value": value, "ro": ret_out, "rm": ret_T,
                    "states_out": states_out, "square": square}
            for kind, *args in STEPS:
                if kind in does:
                    does[kind](*args)

            guess(NT)
            act.wait_ge(rstd2_rdy, 1)
            for t in range(NT):
                R = out_rows(t)
                b = t % 2
                if t >= 2:
                    act.wait_ge(hn_out[b], 16 * (t // 2))
                af(rows[0:R, b, :], x_sb[0:R, t, :], ACT.Copy, scale=rstd2[0:R, t:t + 1]).then_inc(hn_rows, 1)
                act.wait_ge(hn_rows, t + 1)
                act.dma_start(hn_d[P * t:P * t + R, :], rows[0:R, b, :]).then_inc(hn_out[b], 16)
            act.wait_ge(r_exp, 1)
            step(af(r4b[:, :, :], r4[:, :, :], ACT.Exp))
            act.sem_inc(r_expd, 1)
            act.wait_ge(r_exp, 2)
            af(small[:, 20:25], small[:, 25:30], ACT.Exp).then_inc(r_expd, 1)

            def pair_out(p, u, rnd, first):
                act.wait_ge(y_ps, p + 1)
                if not first:
                    act.wait_ge(y_out[u], rnd * 16)
                step_free(nc.scalar.copy(y_sb[:, u, :], acc[:, 2:4, :].rearrange("p b n -> p (b n)")), p)
                act.dma_start(y_pairs[bass.ds(p, 1)].rearrange("o r d -> (o r) d"), y_sb[:, u, :]
                              ).then_inc(y_out[u], 16)

            def step_free(ins, p):
                ins.then_inc(y_ev, 1)
                act.wait_ge(y_ev, p + 1)

            def pair_exp(p, u, first):
                act.wait_ge(gu_ps, p + 1)
                if not first:
                    act.wait_ge(e_act, p)
                af(glu[:, 0, :], acc[:, u, 0:FF], ACT.Exp, scale=-1.0).then_inc(e_exp, 1)

            pair_exp(0, 0, True)
            pair_exp(1, 1, False)
            pair_out(0, 0, 0, True)
            pair_exp(2, 0, False)
            pair_out(1, 1, 0, True)
            pair_exp(3, 1, False)
            with act.Fori(1, NPAIR // 2 - 1) as i:
                for u in range(2):
                    pair_out(i * 2 + u, u, i, False)
                    pair_exp(i * 2 + u + 2, u, False)
            pair_out(NPAIR - 2, 0, NPAIR // 2 - 1, False)
            pair_out(NPAIR - 1, 1, NPAIR // 2 - 1, False)

            act.wait_ge(slots_ready, 1)
            n_most = act.value_load(most_i[0:1, 0:1], min_val=0, max_val=T_TOK)
            with act.If(n_most > CAP):
                act.wait_ge(y_out[0], 8 * NPAIR)
                act.sem_inc(L_ye, 1)
                act.sem_inc(L_out, 16)
                with act.Fori(1, LEVELS) as lv:
                    with act.Fori(0, NPAIR) as p:
                        it = (lv - 1) * NPAIR + p
                        act.wait_ge(L_gu, it + 1)
                        af(glu[:, 0, :], acc[:, 0, 0:FF], ACT.Exp, scale=-1.0).then_inc(L_ex, 1)
                        act.wait_ge(L_y, it + 2)
                        act.wait_ge(L_out, it * 16 + 16)
                        nc.scalar.copy(y_sb[:, 0, :], acc[:, 2:4, :].rearrange("p b n -> p (b n)")).then_inc(L_ye, 1)
                        act.wait_ge(L_ye, it + 2)
                        act.dma_start(y_pairs[bass.ds(lv * NPAIR + p, 1)].rearrange("o r d -> (o r) d"),
                                      y_sb[:, 0, :]).then_inc(L_out, 16)

        @block.vector
        def _(dve):
            tt = nc.vector.tensor_tensor
            ts = nc.vector.tensor_scalar
            stt = nc.vector.scalar_tensor_tensor
            red = nc.vector.tensor_reduce
            steps = [0]

            def step(ins):
                ins.then_inc(dve_step, 1)
                steps[0] += 1
                dve.wait_ge(dve_step, steps[0])

            roots = [0]

            def newton(dst, n, R=P):
                roots[0] += 1
                dve.wait_ge(root_ready, roots[0])
                a = root[0:R, 2, 0:n]
                g = root[0:R, 1, 0:n]
                step(tt(a, g, g, ALU.mult))
                step(tt(a, a, ms[0:R, 0:n], ALU.mult))
                step(ts(a, a, -0.5, 1.5, ALU.mult, ALU.add))
                step(tt(dst, a, g, ALU.mult))

            def inv_root(dst, n, R=P):
                dve.sem_inc(ms_ready, 1)
                newton(dst, n, R)

            step(nc.vector.memset(ssq[:, :], 1.0))
            dve.sem_inc(ssq_clear, 1)
            step(nc.vector.memset(ssq2[:, :, :], 1.0))
            dve.sem_inc(ssq_clear, 1)
            dve.wait_ge(c_in, 32)
            n = 0
            for t in range(NT):
                R = rows_of(t)
                for half in range(2):
                    n += 1
                    dve.wait_ge(xt_ps, n)
                    if n > 2:
                        dve.wait_ge(xt_lo, n - 2)
                        dve.wait_ge(xt_hi, n - 2)
                    src = side[:, (n - 1) % 2, :].rearrange("p (j n) -> p j n", j=4)[:, :, 0:R]
                    tt(part[:, half, :, 0:R], src,
                       g1T[:, 4 * half:4 * half + 4].unsqueeze(2).to_broadcast([P, 4, R]), ALU.mult
                       ).then_inc(xt_part, 1)
                    dve.wait_ge(xt_hi, n)
                    dst = (slice(None), slice(4 * half, 4 * half + 4), slice(P * t, P * t + R))
                    tt(xT_lo[dst], part[:, half, :, 0:R], xT_hi[dst].bitcast(F32), ALU.subtract
                       ).then_inc(xt_lo, 1)
            dve.wait_ge(act_step, NT)
            step(ts(ms[:, 0:NT], ssq[:, 0:NT], 1.0 / D, EPS, ALU.mult, ALU.add))
            inv_root(rstd1[:, :], NT)
            dve.sem_inc(rstd_ready, 1)
            dve.wait_ge(g_in, 16 * 6)
            for a in range(2):
                g = qk_g[:, a:a + 1, :].to_broadcast([P, NT, HD])
                step(tt(rope_g[:, a, 0], cos_t, g, ALU.mult))
                h = HD // 2
                step(tt(rope_g[:, a, 1, :, 0:h], sin_t[:, :, 0:h], qk_g[:, a:a + 1, h:].to_broadcast([P, NT, h]),
                        ALU.mult))
                step(tt(rope_g[:, a, 1, :, h:], sin_t[:, :, h:], qk_g[:, a:a + 1, 0:h].to_broadcast([P, NT, h]),
                        ALU.mult))

            def rope(src, nh, R, cos, sin):
                h = HD // 2
                s = src.rearrange("p (n d) -> p n d", n=nh)
                a = h_a[0:R, 0:nh * HD].rearrange("p (n d) -> p n d", n=nh)
                b = h_b[0:R, 0:nh * HD].rearrange("p (n d) -> p n d", n=nh)
                step(tt(a, s, cos.unsqueeze(1).to_broadcast([R, nh, HD]), ALU.mult))
                step(tt(b[:, :, 0:h], s[:, :, h:], sin[:, 0:h].unsqueeze(1).to_broadcast([R, nh, h]), ALU.mult))
                step(tt(b[:, :, h:], s[:, :, 0:h], sin[:, h:].unsqueeze(1).to_broadcast([R, nh, h]), ALU.mult))
                step(tt(a, a, b, ALU.add))
                return a

            squared = [0]

            def post(c, t, b):
                R = rows_of(t)
                dve.wait_ge(acc_free, nth["evict", c, t])
                if c == RG:
                    squared[0] += 1
                    dve.wait_ge(raw_sq, squared[0])
                    step(ts(h_a[0:R, :], h_sq[0:R, :], 1.0, None, ALU.add))
                    dve.sem_inc(raw_sq_used, 1)
                    step(nc.vector.reciprocal(h_b[0:R, :], h_a[0:R, :]))
                    tt(gate[0:R, t, :], gate[0:R, t, :], h_b[0:R, :], ALU.mult).then_inc(posted, 1)
                    return
                if c == RQK:
                    raw = rqk[0:R, t, :]
                    a = rope(raw, 8, R, cos_t[0:R, t], sin_t[0:R, t])
                    tt(raw.rearrange("p (n d) -> p n d", n=8), a,
                       ret_scale[0:R, t // TAIL, :].unsqueeze(2).to_broadcast([R, 8, HD]), ALU.mult
                       ).then_inc(posted, 1)
                    return
                nh, kind = (2, 1) if c == SKV else (QH, 0)
                w = nh * HD
                squared[0] += 1
                dve.wait_ge(raw_sq, squared[0])
                step(red(ssq[0:R, 0:nh], h_sq[0:R, 0:w].rearrange("p (n d) -> p n d", n=nh), AX_X, ALU.add))
                dve.sem_inc(raw_sq_used, 1)
                step(ts(ms[0:R, 0:nh], ssq[0:R, 0:nh], 1.0 / HD, EPS, ALU.mult, ALU.add))
                raw = sk[0:R, t, :] if c == SKV else sq[0:R, t].rearrange("p h g d -> p (h g d)")
                dve.sem_inc(ms_ready, 1)
                a = rope(raw, nh, R, rope_g[0:R, kind, 0, t], rope_g[0:R, kind, 1, t])
                newton(rstd[0:R, 0:nh], nh, R)
                if c == SKV:
                    r = rstd[0:R, 0:nh].unsqueeze(2).to_broadcast([R, nh, HD])
                    tt(raw.rearrange("p (n d) -> p n d", n=2), a, r, ALU.mult).then_inc(posted, 1)
                    return
                for g in range(2):
                    l = tt(sq[0:R, t, :, g, :], a[:, 4 * g:4 * g + 4, :],
                           rstd[0:R, 4 * g:4 * g + 4].unsqueeze(2).to_broadcast([R, 4, HD]), ALU.mult)
                l.then_inc(posted, 1)

            def meta_v(b):
                dve.wait_ge(acc_free, NT)
                nc.vector.tensor_copy(v_own[64:64 + NMETA, :, :], sv[64:64 + NMETA, TAIL:TAIL + 1, :]
                                      .to_broadcast([NMETA, 8, P]))
                nc.vector.memset(v_shift[0:64, 0, :], 0.0).then_inc(vmeta, 1)

            def qT(t, b):
                R = rows_of(t)
                dve.wait_ge(q_ps, nth["qT", t])
                nc.vector.tensor_copy(sqT[:, :, P * t:P * t + R],
                                      side[:, b, :].rearrange("p (j n) -> p j n", j=4)[:, :, 0:R]
                                      ).then_inc(qT_ev, 1)

            def score(i, b):
                t, g, hh = UNITS[i]
                R = out_rows(t)
                if i == 0:
                    dve.wait_ge(q_ps, NT)
                    nc.vector.memset(mix_hi[:, :, T_TOK:].bitcast(F32), 0.0)
                    nc.vector.memset(mix_lo[:, :, T_TOK:].bitcast(F32), 0.0).then_inc(mix_clear, 1)
                dve.wait_ge(s_ps, i + 1)
                s2 = side[:, b, :].rearrange("p (h n) -> p h n", h=2)
                if t == 0:
                    nc.vector.memset(s2[0:64, :, 0:WINDOW], NEG)
                    step(nc.vector.memset(s2[64:128, :, 0:CH], NEG))
                sink = sinks[0:R, 4 * g + 2 * hh:4 * g + 2 * hh + 2]
                v = soft[0:R, b, :]
                step(red(v[:, 0:2], s2[0:R, :, 0:KEYS], AX_X, ALU.max))
                step(stt(out=v[:, 0:2], in0=v[:, 0:2], scalar=HD ** -0.5, in1=sink, op0=ALU.mult, op1=ALU.max))
                ts(v[:, 2:4], v[:, 0:2], -1.0, None, ALU.mult)
                tt(v[:, 6:8], sink, v[:, 0:2], ALU.subtract).then_inc(s_max, 1)

            def norm(i, b):
                R = out_rows(UNITS[i][0])
                v = soft[0:R, b, :]
                dve.wait_ge(s_exp, i + 1)
                step(tt(v[:, 10:12], v[:, 4:6], v[:, 8:10], ALU.add))
                step(nc.vector.reciprocal(v[:, 12:14], v[:, 10:12]))
                tt(probs[0:R, b], probs[0:R, b], v[:, 12:14].unsqueeze(2).to_broadcast([R, 2, KEYS]), ALU.mult
                   ).then_inc(s_prob, 1)

            def value(i, b):
                t, g, hh = UNITS[i]
                R = out_rows(t)
                dve.wait_ge(o_hi, i + 1)
                tok = slice(P * t, P * t + R)
                tt(mix_lo[:, 2 * g + hh, tok], side[:, b, 0:R], mix_hi[:, 2 * g + hh, tok].bitcast(F32),
                   ALU.subtract).then_inc(o_lo, 1)

            def ps_state(par, b):
                return side[64 * par:64 * par + 64, b, 0:2 * P].rearrange("p (i v) -> p i v", i=2)

            def meta_state(par, b):
                hs = slice(64 * par, 64 * par + 64)
                dve.wait_ge(st_ps, st_nth["meta_state", par])
                tt(state_p[hs], ps_state(par, b), decay[hs, 2, :].unsqueeze(2).to_broadcast([64, 2, RDV]),
                   ALU.mult).then_inc(st_new, 1)

            causal = const("causal")

            def ret_scores(m, b):
                R = out_rows(RUNITS[m][0])
                dve.wait_ge(ra_ps, m + 1)
                tt(ret_aT[0:R, b, :, 0:R], side[0:R, b, 0:2 * P].rearrange("p (j n) -> p j n", j=2)[:, :, 0:R],
                   causal[0:R, 0:R].unsqueeze(1).to_broadcast([R, 2, R]), ALU.mult).then_inc(ra_ev, 1)

            def ret_out(m, b):
                t, par = RUNITS[m]
                R = out_rows(t)
                hs = slice(64 * par, 64 * par + 64)
                state = state_s if t == TAIL else state_p
                dve.wait_ge(st_ps, st_nth["ro", m])
                dve.wait_ge(ro_sq, m + 1)
                tmp = h_b[hs, 0:2 * RDV].rearrange("p (i v) -> p i v", i=2)
                step(tt(tmp, ps_state(par, b), state[hs], ALU.add))
                tt(state[hs], tmp, decay[hs, t // TAIL, :].unsqueeze(2).to_broadcast([64, 2, RDV]), ALU.mult
                   ).then_inc(st_new, 1)
                step(red(ssq[0:R, 0:2], squares[0:R, b, :].rearrange("p (j n) -> p j n", j=2), AX_X, ALU.add))
                step(ts(ms[0:R, 0:2], ssq[0:R, 0:2], 1.0 / RDV, EPS, ALU.mult, ALU.add))
                dve.sem_inc(ms_ready, 1)

            def ret_norm(m, b):
                t, par = RUNITS[m]
                R = out_rows(t)
                dve.wait_ge(posted, nth["post", RG, t])
                a = h_a[0:R, 0:2 * P].rearrange("p (j n) -> p j n", j=2)
                g2 = gate[0:R, t, :].rearrange("p (j q n) -> p j q n", j=2, q=2)[:, :, par, :]
                step(tt(a, side[0:R, b, 2 * P:].rearrange("p (j n) -> p j n", j=2), g2, ALU.mult))
                newton(rstd[0:R, 0:2], 2, R)
                tt(o_rows[0:R, b], a, rstd[0:R, 0:2].unsqueeze(2).to_broadcast([R, 2, RDV]), ALU.mult
                   ).then_inc(ro_rows, 1)

            def ret_T(m, b):
                t, par = RUNITS[m]
                R = out_rows(t)
                dve.wait_ge(rm_ps, m + 1)
                tt(part_r[:, b, :, 0:R], side[:, b, 0:2 * P].rearrange("p (j n) -> p j n", j=2)[:, :, 0:R],
                   retgT[:, par:4:2].unsqueeze(2).to_broadcast([P, 2, R]), ALU.mult).then_inc(rm_part, 1)
                dve.wait_ge(rm_hi, m + 1)
                dst = (slice(None), slice(par, 4, 2), slice(P * t, P * t + R))
                tt(xT_lo[dst], part_r[:, b, :, 0:R], xT_hi[dst].bitcast(F32), ALU.subtract).then_inc(rm_lo, 1)

            def evict(c, t, b):
                if c < OUT0:
                    return
                R = out_rows(t)
                cols = slice(512 * (c - OUT0), 512 * (c - OUT0) + 512)
                dve.wait_ge(acc_done, NT * c + t + 1)
                tt(x_sb[0:R, t, cols], x_sb[0:R, t, cols], acc[0:R, t, :], ALU.add).then_inc(acc_free, 1)

            def hid_T(n, t, b):
                R = out_rows(t)
                dve.wait_ge(hT_ps, nth["hT", n, t])
                tt(hnT[:, b, :, 0:R], side[:, b, :].rearrange("p (j n) -> p j n", j=4)[:, :, 0:R],
                   g2_both[:, 1, 4 * n:4 * n + 4].unsqueeze(2).to_broadcast([P, 4, R]), ALU.mult
                   ).then_inc(hT_ev, 1)

            def logit(n, t, b):
                R = out_rows(t)
                if n == 0 and t == 0:
                    step(nc.vector.memset(logits[:, :, :], 0.0))
                dve.wait_ge(lg_ps, nth["logit", n, t])
                ps = side[0:R, b, 0:NG + NE]
                if n == 0:
                    nc.vector.tensor_copy(logits[0:R, t, :], ps).then_inc(lg_ev, 1)
                else:
                    tt(logits[0:R, t, :], logits[0:R, t, :], ps, ALU.add).then_inc(lg_ev, 1)

            does = {"evict": evict, "post": post, "meta_v": meta_v, "qT": qT, "score": score, "norm": norm,
                    "value": value, "meta_state": meta_state, "ra": ret_scores, "ro": ret_out,
                    "rn": ret_norm, "rm": ret_T, "hT": hid_T, "logit": logit}
            for kind, *args in STEPS:
                if kind in does:
                    does[kind](*args)

            dve.wait_ge(sq2, 2 * NT)
            step(tt(ms[:, 0:NT], ssq2[:, 0, :], ssq2[:, 1, :], ALU.add))
            step(ts(ms[:, 0:NT], ms[:, 0:NT], 1.0 / D, EPS, ALU.mult, ALU.add))
            inv_root(rstd2[:, :], NT)
            dve.sem_inc(rstd2_rdy, 1)
            dve.wait_ge(lg_ev, 2 * NT)
            step(tt(logits[:, :, :], logits[:, :, :], rstd2[:, :].unsqueeze(2).to_broadcast([P, NT, NG + NE]),
                    ALU.mult))

            gl = logits[:, :, 0:NG]
            col = lambda lo: small[:, lo:lo + NT]

            def wide(ap, n):
                return ap.unsqueeze(2).to_broadcast([P, NT, n])

            def first_of(oh_out, vals, top, n):
                c = cand[:, :, 0:n]
                step(tt(c, vals, wide(top, n), ALU.is_equal))
                step(ts(small[:, 100:100 + n], iota[:, 0:n], -OFF, None, ALU.add))
                step(tt(c, c, small[:, 100:100 + n].unsqueeze(1).to_broadcast([P, NT, n]), ALU.mult))
                step(red(col(120), c, AX_X, ALU.min))
                step(tt(oh_out, c, wide(col(120), n), ALU.is_equal))

            step(red(col(30), gl, AX_X, ALU.max))
            step(tt(r4[:, :, :], gl, wide(col(30), NG), ALU.subtract))
            dve.sem_inc(r_exp, 1)
            first_of(oh_g[:, :, :], gl, col(30), NG)
            e4 = logits[:, :, NG:].rearrange("p t (g e) -> p t g e", g=NG)
            for t in range(NT):
                step(tt(r32[:, t], e4[:, t], oh_g[:, t, :].unsqueeze(2).to_broadcast([P, NG, EPG]), ALU.mult))
            step(red(el[:, :, :], r32[:, :, :, :].rearrange("p t g e -> p t e g"), AX_X, ALU.add))
            step(red(col(35), el[:, :, :], AX_X, ALU.max))
            first_of(oh_e[:, 0], el[:, :, :], col(35), EPG)
            step(stt(out=el2[:, :, :], in0=oh_e[:, 0], scalar=NEG, in1=el[:, :, :], op0=ALU.mult, op1=ALU.add))
            step(red(col(40), el2[:, :, :], AX_X, ALU.max))
            first_of(oh_e[:, 1], el2[:, :, :], col(40), EPG)
            step(tt(col(25), col(40), col(35), ALU.subtract))
            dve.sem_inc(r_exp, 1)
            for k in range(2):
                for g in range(NG):
                    step(tt(oh[:, k, :, EPG * g:EPG * g + EPG], oh_e[:, k],
                            wide(oh_g[:, :, g], EPG), ALU.mult))
            step(tt(chosen[:, :, :], oh[:, 0], oh[:, 1], ALU.add))
            step(nc.vector.memset(chosen[DEC:, TAIL, :], 0.0))
            dve.sem_inc(m_ready, 1)
            dve.wait_ge(r_expd, 2)
            step(red(col(50), r4b[:, :, :], AX_X, ALU.add))
            step(ts(col(55), col(20), 1.0, None, ALU.add))
            step(tt(col(50), col(50), col(55), ALU.mult))
            step(nc.vector.reciprocal(w_k[:, 0, :], col(50)))
            step(tt(w_k[:, 1, :], w_k[:, 0, :], col(20), ALU.mult))
            for k in range(2):
                for t in range(NT):
                    o2 = oh[:, k, t, :].rearrange("p (a b) -> p a b", b=2)
                    j = k * NT + t
                    step(tt(pair_tok[:, j, :], o2[:, :, 0], o2[:, :, 1], ALU.add))
                    step(ts(pair_tok[:, j, :], pair_tok[:, j, :], const("token")[:, t:t + 1], None, ALU.mult))
            dve.wait_ge(rank_ps, 1)
            step(nc.vector.tensor_copy(rank[:, :, :], side3[:, 0:NE * NT].rearrange("p (t e) -> p t e", t=NT)))
            step(red(most[:, :], side3[:, NE * NT:NE * NT + NE], AX_X, ALU.max))
            step(nc.vector.tensor_copy(most_i[:, :], most[:, :]))
            e_row = const("expert_row0").unsqueeze(1).to_broadcast([P, NT, NE])
            p_row = const("pair_row0").unsqueeze(1).to_broadcast([P, NT, NE])

            def pick(dst, values):
                for k in range(2):
                    step(tt(tmp_k[:, k], oh[:, k], values, ALU.mult))
                step(red(dst, tmp_k[:, :, :, :].rearrange("p k t e -> p (k t) e"), AX_X, ALU.add))

            pick(rank_k[:, :], rank[:, :, :])
            pick(row_k[:, :], p_row)
            pick(slot_f[:, :], e_row)
            step(nc.vector.tensor_copy(slot_i[:, :], rank_k[:, :]))
            step(ts(slot_i[:, :], slot_i[:, :], CAP.bit_length() - 1, None, ALU.logical_shift_right))
            step(nc.vector.tensor_copy(lvl_a[:, :], slot_i[:, :]))
            step(tt(slot_f[:, :], slot_f[:, :], rank_k[:, :], ALU.add))
            step(stt(out=slot_f[:, :], in0=lvl_a[:, :], scalar=float((NE - 1) * CAP), in1=slot_f[:, :],
                     op0=ALU.mult, op1=ALU.add))
            step(nc.vector.tensor_copy(slot_i[:, :], slot_f[:, :]))
            step(tt(row_k[:, :], row_k[:, :], rank_k[:, :], ALU.add))
            step(nc.vector.memset(level0[:, :], 0.0))

            def rows_of_level(one):
                one(ts(lvl_a[:, :], rank_k[:, :], level0[:, 0:1], None, ALU.subtract))
                one(ts(lvl_b[:, :], lvl_a[:, :], float(CAP), 1000.0, ALU.is_ge, ALU.mult))
                one(ts(lvl_a[:, :], lvl_a[:, :], 0.0, 1000.0, ALU.is_lt, ALU.mult))
                one(tt(lvl_a[:, :], lvl_a[:, :], lvl_b[:, :], ALU.add))
                one(tt(lvl_a[:, :], lvl_a[:, :], row_k[:, :], ALU.add))
                one(ts(row_l[:, :], lvl_a[:, :], level0[:, 0:1], None, ALU.subtract))
                for j in range(2 * NT):
                    one(ts(row_oh[:, j, :], iota, row_l[:, j:j + 1], None, ALU.is_equal))

            rows_of_level(step)
            dve.sem_inc(oh_ready, 1)
            dve.wait_ge(idx_ps, 1)
            step(nc.vector.tensor_copy(idx[:, :], side3[:, 256:256 + NPAIR]))
            dve.sem_inc(slots_ready, 1)
            dve.sem_inc(idx_ready, 1)

            def rows_in(p, u, first):
                dve.wait_ge(xg_ps, p + 1)
                if not first:
                    dve.wait_ge(gu_ps, p - 1)
                tt(xgT[:, u], side[:, 0:2, :].rearrange("p b (j n) -> p (b j) n", j=4),
                   g2T.unsqueeze(2).to_broadcast([P, KD, P]), ALU.mult).then_inc(xg_ev, 1)

            def glu_steps(u, wait):
                ts(glu[:, 1, :], glu[:, 0, :], 1.0, None, ALU.add).then_inc(glu_step, 1)
                dve.wait_ge(glu_step, wait + 1)
                nc.vector.reciprocal(glu[:, 2, :], glu[:, 1, :]).then_inc(glu_step, 1)
                dve.wait_ge(glu_step, wait + 2)
                tt(glu[:, 1, :], glu[:, 2, :], acc[:, u, 0:FF], ALU.mult).then_inc(glu_step, 1)
                dve.wait_ge(glu_step, wait + 3)
                return tt(actv[:, :], glu[:, 1, :], acc[:, u, FF:2 * FF], ALU.mult)

            def act_in(p, u, first):
                dve.wait_ge(e_exp, p + 1)
                if not first:
                    dve.wait_ge(aT_ps, p)
                glu_steps(u, p * 3).then_inc(e_act, 1)

            def actT_in(p, first):
                dve.wait_ge(aT_ps, p + 1)
                if not first:
                    dve.wait_ge(y_ps, p)
                nc.vector.tensor_copy(actT[:, :, :], side3[:, 0:2 * P].rearrange("p (j n) -> p j n", j=2)
                                      ).then_inc(aT_ev, 1)

            rows_in(0, 0, True)
            rows_in(1, 1, True)
            act_in(0, 0, True)
            actT_in(0, True)
            with dve.Fori(1, NPAIR // 2) as i:
                rows_in(i * 2, 0, False)
                act_in(i * 2 - 1, 1, False)
                actT_in(i * 2 - 1, False)
                rows_in(i * 2 + 1, 1, False)
                act_in(i * 2, 0, False)
                actT_in(i * 2, False)
            act_in(NPAIR - 1, 1, False)
            actT_in(NPAIR - 1, False)

            n_most = dve.value_load(most_i[0:1, 0:1], min_val=0, max_val=T_TOK)
            with dve.If(n_most > CAP):
                with dve.Fori(1, LEVELS) as lv:
                    seen = [0]

                    def one(ins):
                        ins.then_inc(L_step, 1)
                        seen[0] += 1
                        dve.wait_ge(L_step, (lv - 1) * PER_LEVEL + seen[0])

                    one(ts(level0[:, :], level0[:, :], float(CAP), None, ALU.add))
                    rows_of_level(one)
                    assert seen[0] == PER_LEVEL
                    dve.sem_inc(L_oh, 1)
                    dve.wait_ge(L_ips, lv)
                    dve.wait_ge(L_xt, (lv - 1) * NPAIR + 1)
                    nc.vector.tensor_copy(idx[:, :], side3[:, 256:256 + NPAIR]).then_inc(L_idx, 1)
                    with dve.Fori(0, NPAIR) as p:
                        it = (lv - 1) * NPAIR + p
                        dve.wait_ge(L_xt, it + 2)
                        tt(xgT[:, 0], side[:, 0:2, :].rearrange("p b (j n) -> p (b j) n", j=4),
                           g2T.unsqueeze(2).to_broadcast([P, KD, P]), ALU.mult).then_inc(L_xe, 1)
                        dve.wait_ge(L_ex, it + 1)
                        glu_steps(0, (NPAIR + it) * 3).then_inc(L_act, 1)
                        dve.wait_ge(L_at, it + 1)
                        nc.vector.tensor_copy(actT[:, :, :], side3[:, 0:2 * P].rearrange("p (j n) -> p j n", j=2)
                                              ).then_inc(L_ae, 1)

            for t in range(NT):
                R = out_rows(t)
                dve.wait_ge(yg_in[t], 32)
                for k in range(2):
                    step(stt(out=x_sb[0:R, t, :], in0=y_tok[0:R, t, k, :], scalar=w_k[0:R, k, t:t + 1],
                             in1=x_sb[0:R, t, :], op0=ALU.mult, op1=ALU.add))
                dve.sem_inc(y_fin, 1)


_INS = ["x_prompt", "x_sample", "cache_ret_state", "cache_swa_k", "cache_swa_v", "meta_tokens", "norm1_g",
        "w_in", "q_norm_g", "k_norm_g", "ret_norm_g", "attn_sinks", "w_out", "norm2_g", "w_group",
        "w_gate", "w_up", "w_down"]
_OUTS = [(1, SEQ, D), (1, DEC, D), (1, 1, RH, RDK, RDV), (1, 1, WINDOW, 2, HD), (1, 1, WINDOW, 2, HD),
         (1, 1, RH, RDK, RDV), (1, 1, WINDOW, 2, HD), (1, 1, WINDOW, 2, HD)]


def kernel(**inputs):
    import numpy as _np
    import concourse.bacc as _bacc
    from concourse import mybir as _mybir
    from concourse.bass_utils import run_bass_kernel_spmd as _run

    nc = _bacc.Bacc("TRN2", target_bir_lowering=False, num_devices=1)
    table, _ = constants()
    arrays, args = {"in_consts_dram": table}, []
    args.append(nc.dram_tensor("in_consts_dram", table.shape, _mybir.dt.float32, kind="ExternalInput").ap())
    for name in _INS:
        a = _np.ascontiguousarray(inputs[name])
        if name == "norm2_g":
            a = _np.stack([a.reshape(P, KD), a.reshape(KD, P).T], 1)
        if name == "w_group":
            a = _np.concatenate([a[0], _np.asarray(inputs["w_expert"])[0]], 1).reshape(KD, P, NG + NE)
            a = _np.ascontiguousarray(a.transpose(1, 0, 2))
        if name == "ret_norm_g":
            a = _np.ascontiguousarray(a.reshape(RH, RDV).T)
        arrays[f"in_{name}_dram"] = a
        args.append(nc.dram_tensor(f"in_{name}_dram", a.shape, _mybir.dt.from_np(a.dtype), kind="ExternalInput").ap())
    for i, shape in enumerate(_OUTS):
        args.append(nc.dram_tensor(f"out_{i}_dram", shape, _mybir.dt.float32, kind="ExternalOutput").ap())
    stream_step(nc, *args)
    r = _run(nc, [arrays], core_ids=[0])
    return tuple(r.results[0][f"out_{i}_dram"] for i in range(len(_OUTS)))
```

```python
from contextlib import ExitStack

import numpy as np

import concourse.bass as bass
from concourse import mybir

ALU = mybir.AluOpType
ACT = mybir.ActivationFunctionType
F32 = mybir.dt.float32
F32R = mybir.dt.float32r
I32 = mybir.dt.int32
AX_X = mybir.AxisListType.X

P = 128
D = 1024
KD = D // P
SEQ, DEC, NMETA = 512, 64, 16
T_TOK = SEQ + DEC
T_ALL = T_TOK + NMETA
NT = 5
TAIL = 4
CH = 64
PAST = 512
RH, RDK, RDV = 4, 64, 128
QH, HD = 8, 64
WINDOW = 128
BAND = WINDOW + CH
KEYS = BAND + NMETA
CACHE0 = T_ALL
NG, EPG = 4, 8
NE = NG * EPG
NPAIR = NE // 2
FF = 256
SLOTS = 3
AHEAD = 4
CAP = 64
LEVELS = T_TOK // CAP
PER_LEVEL = 8
EPS = 1e-6
NEG = -1e30
OFF = 64.0

C_RQK, C_RV, C_RG, C_SQ, C_SKV = 0, 512, 1024, 1536, 2048
CHUNKS = [(C_SKV, 256), (C_SQ, 512), (C_RQK, 512), (C_RV, 512), (C_RG, 512)]
SKV, SQ, RQK, RV, RG = range(5)
RING = 4
OUT_K = [4, 5, 6, 7, 0, 1, 2, 3]


ORDER = [TAIL, 0, 1, 2, 3]
UNITS = [(t, g, hh) for t in ORDER for g in range(2) for hh in range(2)]
RUNITS = [(t, par) for t in ORDER for par in range(2)]
OUT0 = len(CHUNKS)

LONE = KD * OUT0 + 4


def plan():
    slots = KD * (len(CHUNKS) + 2)
    before = [[] for _ in range(slots)]
    after = [[] for _ in range(slots)]
    for c in range(len(CHUNKS) + 1):
        after[KD * c + KD - 1] += [("evict", c, t) for t in range(NT)]
    for c in (SKV, SQ):
        after[KD * c + KD] += [("sums", c, t) for t in range(NT)] + [("root", c)]
    for i, t in enumerate(ORDER):
        after[KD * SQ + i + 1].append(("post", SKV, t))
        after[KD * RQK + i + 1].append(("post", SQ, t))
        after[KD * RV + i].append(("post", RQK, t))
    for i, t in enumerate(ORDER):
        after[KD * SQ + i + 3].append(("kT", t))
        after[KD * RQK + i + 3].append(("qT", t))
    after[KD * SQ - 1].append(("meta_v",))
    after[KD * RQK - 1].append(("kv_out",))
    u0 = KD * RQK + 5
    for n in range(len(UNITS)):
        s = u0 + n
        before[s + 1].append(("norm", n))
        before[s + 2].insert(0, ("pT", n))
        after[s + 2].append(("value", n))
        after[s].append(("score", n))
    after[KD * OUT0 + 1] += [("post", RG, t) for t in ORDER]
    for i, t in enumerate(ORDER):
        after[KD * RG + i].append(("rT", t))
    for par in range(2):
        after[KD * RG + NT + par].append(("meta_state", par))
    tail = [[] for _ in range(len(RUNITS) + 3)]
    for m, (t, par) in enumerate(RUNITS):
        if m > 1:
            tail[m].append(("rn", m - 2))
        if m:
            tail[m].append(("ro", m - 1))
        tail[m].append(("ra", m))
        if m > 1:
            tail[m].append(("rm", m - 2))
    n = len(RUNITS)
    tail[n] += [("rn", n - 2), ("ro", n - 1), ("rm", n - 2)]
    tail[n + 1] += [("rn", n - 1), ("rm", n - 1)]
    lone = LONE
    first = lone - 2
    for s in range(first, lone):
        after[s] += tail[s - first]
    tail[-1].append(("states_out",))
    for t in range(NT):
        s = KD * (OUT0 + 1) + t
        after[s].append(("square", 0, t))
        after[s].append(("hT", 0, t))
        after[s + 1].append(("logit", 0, t))
    order = []
    for s in range(slots):
        if s == lone:
            for x in tail[lone - first:]:
                order += x
        order += before[s] + [("piece", s // KD, s % KD)] + after[s]
    order.append(("evict", OUT0 + 1, 0))
    for t in range(NT):
        if t + 1 < NT:
            order.append(("evict", OUT0 + 1, t + 1))
        order += [("square", 1, t), ("hT", 1, t)]
        if t:
            order.append(("logit", 1, t - 1))
    order.append(("logit", 1, NT - 1))
    free, held, steps = [0, 1, 2], {}, []
    last = {"kT": "kT", "qT": "qT", "rT": "rT", "meta_state": "meta_state", "score": "value", "ra": "rm",
            "hT": "logit"}
    unit = {"score": "u", "norm": "u", "pT": "u", "value": "u", "ra": "r", "ro": "r", "rn": "r", "rm": "r"}
    for x in order:
        kind, key = x[0], (unit.get(x[0], "h" if x[0] in ("hT", "logit") else x[0]),) + x[1:]
        if kind in last:
            held[key] = free.pop(0)
        bank = held.get(key)
        steps.append(x + (bank,))
        if kind in last.values() and key in held:
            free.append(held.pop(key))
    return steps


def rows_of(t):
    return P if t < TAIL else DEC + NMETA


def out_rows(t):
    return P if t < TAIL else DEC


def constants():
    p = np.arange(P)
    at, cols = {}, []

    def put(name, a):
        a = np.asarray(a, np.float32).reshape(P, -1)
        lo = sum(c.shape[1] for c in cols)
        at[name] = (lo, lo + a.shape[1])
        cols.append(a)

    put("ident", np.eye(P))
    put("causal", p[None, :] >= p[:, None])
    put("before", p[:, None] < p[None, :])
    put("ones", np.ones((P, P)))
    put("iota", np.tile(p, (P, 1)))
    pos = np.zeros((NT, P), np.float32)
    for t in range(TAIL):
        pos[t] = NMETA + P * t + p
    pos[TAIL, :DEC] = NMETA + PAST + np.arange(DEC)
    pos[TAIL, DEC:DEC + NMETA] = np.arange(NMETA)
    half = HD // 2
    inv = np.float32(10000.0) ** (-np.arange(half, dtype=np.float32) / np.float32(half))
    ang = pos[:, :, None] * inv
    cos, sin = np.cos(ang), np.sin(ang)
    put("cos", np.concatenate([cos, cos], -1).transpose(1, 0, 2))
    put("sin", np.concatenate([-sin, sin], -1).transpose(1, 0, 2))
    gamma = 1.0 - 2.0 ** (-5.0 - np.arange(RH))
    step = np.stack([p, np.where(p < DEC, p, p - DEC)], 0)[..., None] + 1.0
    q_scale = gamma ** step
    k_scale = gamma ** -step * RDK ** -0.5
    put("ret_scale", np.concatenate([q_scale, k_scale], -1).transpose(1, 0, 2))
    head = 2 * np.arange(2)[None, :] + (p[:, None] >= 64)
    put("decay", np.stack([gamma[head] ** n for n in (P, DEC, NMETA)], 1))
    tok = np.arange(NT)[None, :] * P + p[:, None]
    put("token", np.where(tok < T_TOK, tok, 0))
    put("expert_row0", np.tile(np.arange(NE) * CAP, (P, 1)))
    put("pair_row0", np.tile(np.arange(NE) % 2 * CAP, (P, 1)))
    return np.ascontiguousarray(np.concatenate(cols, 1)), at


def root_steps(eng, step, x, tmp):
    u, y, a = tmp[:, 0], tmp[:, 1], tmp[:, 2]
    step(eng.tensor_scalar(y.bitcast(I32), x.bitcast(I32), -0.5, float(0x5F1FFFF9), ALU.mult, ALU.add))
    step(eng.tensor_tensor(a, y, y, ALU.mult))
    step(eng.tensor_tensor(a, a, x, ALU.mult))
    step(eng.tensor_scalar(a, a, -0.703952253, 0.703952253 * 2.38924456, ALU.mult, ALU.add))
    step(eng.tensor_tensor(y, a, y, ALU.mult))
    step(eng.tensor_tensor(a, y, y, ALU.mult))
    step(eng.tensor_tensor(u, a, x, ALU.mult))
    step(eng.tensor_scalar(a, u, 0.375, -1.25, ALU.mult, ALU.add))
    step(eng.tensor_tensor(a, a, u, ALU.mult))
    step(eng.tensor_scalar(a, a, 1.875, None, ALU.add))
    step(eng.tensor_tensor(y, a, y, ALU.mult))
    return y


def turn(r, j):
    n = AHEAD + j
    return r * 6 + n, n % SLOTS, r * (6 // SLOTS) + n // SLOTS, n % 2, r * 3 + n // 2


def stream_step(nc, consts, x_prompt, x_sample, cache_ret_state, cache_swa_k, cache_swa_v,
                meta_tokens, norm1_g, w_in, q_norm_g, k_norm_g, ret_norm_g, attn_sinks, w_out,
                norm2_g, w_group, w_gate, w_up, w_down,
                y_prompt, y_sample, ret_prompt, k_prompt, v_prompt, ret_sample, k_sample,
                v_sample):
    _, at = constants()
    NCONST = consts.shape[1]

    hn_d = nc.dram_tensor("hn_d", [T_TOK, D], F32, kind="Internal").ap()
    y_d = nc.dram_tensor("y_d", [LEVELS * NE * CAP, D], F32, kind="Internal").ap()
    y_pairs = y_d.rearrange("(q r) d -> q r d", r=2 * CAP)

    w_in_v = w_in.rearrange("o (p k) n -> p (o k) n", p=P)
    w_out_v = w_out.rearrange("o (k p) n -> p (o k) n", p=P)
    gate_v = w_gate.rearrange("o e (p k) f -> (o e) p (k f)", p=P)
    up_v = w_up.rearrange("o e (p k) f -> (o e) p (k f)", p=P)
    down_v = w_down.rearrange("o e (p j) n -> (o e) p (j n)", p=P)

    with ExitStack() as ctx:
        def sb(name, shape, dt=F32):
            return ctx.enter_context(nc.sbuf_tensor(name, shape, dt))

        def sem(name):
            return ctx.enter_context(nc.semaphore(name))

        cst = sb("cst", [P, NCONST])

        def const(name, rows=P):
            return cst[0:rows, at[name][0]:at[name][1]]

        ident, iota, ones = const("ident"), const("iota"), const("ones")
        cos_t = const("cos").rearrange("p (t d) -> p t d", t=NT)
        sin_t = const("sin").rearrange("p (t d) -> p t d", t=NT)
        ret_scale = const("ret_scale").rearrange("p (a h) -> p a h", a=2)
        decay = const("decay").rearrange("p (a h) -> p a h", a=3)
        x_sb = sb("x_sb", [P, NT, D])
        g1T = sb("g1T", [P, KD])
        g2_both = sb("g2_both", [P, 2, KD])
        g2T = g2_both[:, 0, :]
        retgT = sb("retgT", [P, RH])
        qk_g = sb("qk_g", [P, 2, HD])
        sinks = sb("sinks", [P, QH])
        w_router = sb("w_router", [P, KD, NG + NE])
        small = sb("small", [P, 160])
        counting = sb("counting", [P, 2, P], F32R)
        soft = sb("soft", [P, 3, 16])
        ssq2 = sb("ssq2", [P, 2, NT])
        rstd2 = sb("rstd2", [P, NT])
        ms = sb("ms", [P, NT * QH])
        root = sb("root", [P, 3, NT * QH])
        ssq_qk = sb("ssq_qk", [P, NT * QH])
        rstd_qk = sb("rstd_qk", [P, NT * QH])
        ms_r = sb("ms_r", [P, 3, 2])
        root_r = sb("root_r", [P, 3, 3, 2])
        rstd1 = sb("rstd1", [P, NT])
        ssq = sb("ssq", [P, 8])

        attn = ExitStack()

        def sba(name, shape, dt=F32):
            return attn.enter_context(nc.sbuf_tensor(name, shape, dt))

        state_p = sba("state_p", [P, 2, RDV])
        state_s = sba("state_s", [P, 2, RDV])
        rope_g = sba("rope_g", [P, 2, 2, NT, HD])
        rqk = sba("rqk", [P, NT, 512])
        rv = sba("rv", [P, NT, 512])
        gate = sba("gate", [P, NT, 512])
        sk = sba("sk", [P, NT, P])
        sv = sba("sv", [P, NT, P])
        rT = sba("rT", [P, 4, T_ALL])
        sqT = sba("sqT", [P, 4, T_ALL])
        skT = sba("skT", [P, T_ALL + WINDOW])
        sig = [sqT[:, :, :].rearrange("p j n -> p (j n)")[:, 512 * t:512 * t + 512] for t in range(TAIL)]
        sig.append(skT[:, 0:512])
        cache_k = sba("cache_k", [P, P])
        cache_v = sba("cache_v", [P, P])
        v_shift = sba("v_shift", [P, 4, P])
        v_own = sba("v_own", [P, 8, P])
        h_a = sba("h_a", [P, 512])
        h_b = sba("h_b", [P, 512])
        squares = sba("squares", [P, 3, 256])
        h_sq = squares[:, :, :].rearrange("p a n -> p (a n)")[:, 0:512]
        probs = sba("probs", [P, 3, 2, KEYS])
        probsT = sba("probsT", [P, 3, 2, 2, P])
        ret_aT = sba("ret_aT", [P, 3, 2, P])
        o_rows = sba("o_rows", [P, 3, 2, P])
        part_r = sba("part_r", [P, 3, 2, P])
        part = rv[:, 0:2, :].rearrange("p a (j n) -> p a j n", j=4)
        mix_lo = sba("mix_lo", [P, 4, T_ALL], F32R)
        with nc.sbuf_tensor("sq", [P, NT, 4, 2, HD], F32) as sq:
            pass
        mix_hi = sba("mix_hi", [P, NT * 512], F32R)[:, 0:4 * T_ALL].rearrange("p (j n) -> p j n", j=4)
        xT_hi = sba("xT_hi", [P, KD, T_ALL], F32R)
        xT_lo = sba("xT_lo", [P, KD, T_ALL], F32R)
        w_raw = sba("w_raw", [P, RING, 512])
        w_hi = sba("w_hi", [P, RING, 512], F32R)
        w_lo = sba("w_lo", [P, RING, 512], F32R)
        attn.close()

        w_moe = sb("w_moe", [P, SLOTS, 2, 3, KD * FF])
        r4 = sb("r4", [P, NT, NG])
        r4b = sb("r4b", [P, NT, NG])
        oh_g = sb("oh_g", [P, NT, NG])
        logits = sb("logits", [P, NT, NG + NE])
        xgT = sb("xgT", [P, 2, KD, P])
        xg_flat = xgT[:, :, :, :].rearrange("p u k n -> p (u k n)")
        hnT = xg_flat[:, 0:12 * P].rearrange("p (b j n) -> p b j n", b=3, j=4)
        xsq = xg_flat[:, 12 * P:16 * P]
        rows = sb("rows", [P, 2, D])
        xg = rows
        y_sb = sb("y_sb", [P, 2, D])
        row_oh = y_sb[:, :, :].rearrange("p u n -> p (u n)")[:, 0:2 * NT * P].rearrange(
            "p (j n) -> p j n", j=2 * NT)
        glu = sb("glu", [P, 2, FF])
        glu_flat = glu[:, :, :].rearrange("p a n -> p (a n)")
        actv = sb("actv", [P, FF])
        actT = sb("actT", [P, 2, P])
        tmp_k = glu_flat[:, 0:2 * NT * NE].rearrange("p (k t e) -> p k t e", k=2, t=NT)
        r32 = glu_flat[:, 2 * NT * NE:3 * NT * NE].rearrange("p (t g e) -> p t g e", t=NT, g=NG)
        rank = actv[:, 0:NT * NE].rearrange("p (t e) -> p t e", t=NT)
        oh_e = actT[:, :, :].rearrange("p a n -> p (a n)")[:, 0:2 * NT * EPG].rearrange(
            "p (k t e) -> p k t e", k=2, t=NT)
        chosen = sb("chosen", [P, NT, NE], F32R)
        el = sb("el", [P, NT, EPG])
        el2 = sb("el2", [P, NT, EPG])
        cand = sb("cand", [P, NT, EPG])
        oh = sb("oh", [P, 2, NT, NE])
        rank_k = sb("rank_k", [P, 2 * NT])
        row_k = sb("row_k", [P, 2 * NT])
        row_l = sb("row_l", [P, 2 * NT])
        lvl_a = sb("lvl_a", [P, 2 * NT])
        lvl_b = sb("lvl_b", [P, 2 * NT])
        level0 = sb("level0", [P, 1])
        slot_f = sb("slot_f", [P, 2 * NT])
        slot_i = sb("slot_i", [P, 2 * NT], I32)
        pair_tok = sb("pair_tok", [P, 2 * NT, NPAIR])
        idx = sb("idx", [P, NPAIR], I32)
        idx_now = sb("idx_now", [P, 2, 1], I32)
        most = sb("most", [P, 1])
        most_i = sb("most_i", [P, 1], I32)
        w_k = sb("w_k", [P, 2, NT])
        y_tok = w_moe[:, 0].rearrange("p e m n -> p (e m n)")[:, 0:2 * NT * D].rearrange(
            "p (t k d) -> p t k d", t=NT, k=2)

        acc = ctx.enter_context(nc.psum_tensor("acc", [P, NT, 512], F32))
        side = ctx.enter_context(nc.psum_tensor("side", [P, 3, 512], F32))
        side3 = side[:, 2, :]

        c_in = sem("c_in")
        x_in = [sem(f"x_in{t}") for t in range(NT)]
        g_in = sem("g_in")
        kv_in = sem("kv_in")
        raw_in = [sem(f"raw_in{s}") for s in range(RING)]
        hi_done = sem("hi_done")
        split = sem("split")
        piece_used = sem("piece_used")
        xt_ps = sem("xt_ps")
        xt_part = sem("xt_part")
        xt_hi = sem("xt_hi")
        xt_lo = sem("xt_lo")
        pool_pass = sem("pool_pass")
        ssq_clear = sem("ssq_clear")
        acc_done = sem("acc_done")
        acc_free = sem("acc_free")
        ms_ready = sem("ms_ready")
        root_ready = sem("root_ready")
        root_step = sem("root_step")
        rstd_ready = sem("rstd_ready")
        act_step = sem("act_step")
        dve_step = sem("dve_step")
        raw_sq = sem("raw_sq")
        raw_sq_used = sem("raw_sq_used")
        posted = sem("posted")
        k_ps = sem("k_ps")
        q_ps = sem("q_ps")
        r_ps = sem("r_ps")
        mix_clear = sem("mix_clear")
        gate_z = sem("gate_z")
        gate_rows = sem("gate_rows")
        shift_in = sem("shift_in")
        vmeta = sem("vmeta")
        qT_ev = sem("qT_ev")
        kT_ev = sem("kT_ev")
        rT_ev = sem("rT_ev")
        s_ps = sem("s_ps")
        s_max = sem("s_max")
        s_exp = sem("s_exp")
        s_prob = sem("s_prob")
        pT_ps = sem("pT_ps")
        pT_ev = sem("pT_ev")
        o_ps = sem("o_ps")
        o_hi = sem("o_hi")
        o_lo = sem("o_lo")
        st_ps = sem("st_ps")
        st_new = sem("st_new")
        ra_ps = sem("ra_ps")
        ra_ev = sem("ra_ev")
        ro_part = sem("ro_part")
        ro_cross = sem("ro_cross")
        ro_ps = sem("ro_ps")
        ro_sq = sem("ro_sq")
        ro_rows = sem("ro_rows")
        rm_ps = sem("rm_ps")
        rm_part = sem("rm_part")
        rm_hi = sem("rm_hi")
        rm_lo = sem("rm_lo")
        x2_done = sem("x2_done")
        sq2 = sem("sq2")
        rstd2_rdy = sem("rstd2_rdy")
        hn_rows = sem("hn_rows")
        hn_out = [sem(f"hn_out{b}") for b in range(2)]
        hT_ps = sem("hT_ps")
        hT_ev = sem("hT_ev")
        lg_ps = sem("lg_ps")
        lg_ev = sem("lg_ev")
        r_exp = sem("r_exp")
        r_expd = sem("r_expd")
        m_ready = sem("m_ready")
        rank_ps = sem("rank_ps")
        oh_ready = sem("oh_ready")
        idx_ps = sem("idx_ps")
        idx_ready = sem("idx_ready")
        slots_ready = sem("slots_ready")
        gu_in = [sem(f"gu_in{s}") for s in range(SLOTS)]
        dn_in = [sem(f"dn_in{s}") for s in range(SLOTS)]
        idx_c = sem("idx_c")
        xg_in = [sem(f"xg_in{u}") for u in range(2)]
        xg_ps = sem("xg_ps")
        xg_ev = sem("xg_ev")
        gu_ps = sem("gu_ps")
        e_exp = sem("e_exp")
        e_act = sem("e_act")
        aT_ps = sem("aT_ps")
        aT_ev = sem("aT_ev")
        y_ps = sem("y_ps")
        y_ev = sem("y_ev")
        y_out = [sem(f"y_out{u}") for u in range(2)]
        L_idx = sem("L_idx")
        L_col = sem("L_col")
        L_w = sem("L_w")
        L_xg = sem("L_xg")
        L_xt = sem("L_xt")
        L_xe = sem("L_xe")
        L_gu = sem("L_gu")
        L_ex = sem("L_ex")
        L_act = sem("L_act")
        L_at = sem("L_at")
        L_ae = sem("L_ae")
        L_y = sem("L_y")
        L_ye = sem("L_ye")
        L_out = sem("L_out")
        L_step = sem("L_step")
        glu_step = sem("glu_step")
        L_oh = sem("L_oh")
        L_ips = sem("L_ips")
        yg_in = [sem(f"yg_in{t}") for t in range(NT)]
        y_fin = sem("y_fin")
        fin_out = sem("fin_out")
        st_out = sem("st_out")
        kv_out = sem("kv_out")

        STEPS = plan()
        nth = {}
        for kind in {x[0] for x in STEPS}:
            for i, x in enumerate(y for y in STEPS if y[0] == kind):
                nth[x[:-1]] = i + 1
        st_nth = {}
        for x in STEPS:
            if x[0] in ("meta_state", "ro"):
                st_nth[x[:-1]] = len(st_nth) + 1

        block = ctx.enter_context(nc.Block())

        @block.sync
        def _(sp):
            xp = x_prompt.rearrange("o (t p) d -> p (o t) d", p=P)
            for t in range(TAIL):
                sp.dma_start(x_sb[:, t, :], xp[:, t, :]).then_inc(x_in[t], 16)
                if t == 0:
                    sp.dma_start(cst[:, :], consts).then_inc(c_in, 16)
                    sp.dma_start(g1T[:, :], norm1_g.rearrange("o (p k) -> p (o k)", k=KD)).then_inc(c_in, 16)
            sp.dma_start(x_sb[0:DEC, TAIL, :], x_sample.rearrange("o s d -> (o s) d")).then_inc(x_in[TAIL], 16)
            sp.dma_start(x_sb[DEC:DEC + NMETA, TAIL, :], meta_tokens).then_inc(x_in[TAIL], 16)

            def load_piece(src, width, i, s, first):
                if not first:
                    sp.wait_ge(split, i - RING + 1)
                sp.dma_start(w_raw[:, s, 0:width], src).then_inc(raw_in[s], 16)

            for c, (col, width) in enumerate(CHUNKS):
                if c == 0:
                    for k in range(KD):
                        load_piece(w_in_v[:, k, col:col + width], width, k, k % RING, k < RING)
                    continue
                with sp.Fori(0, KD // RING) as r:
                    for s in range(RING):
                        k = r * RING + s
                        load_piece(w_in_v[:, bass.ds(k, 1), col:col + width].rearrange("p o n -> p (o n)"),
                                   width, k + KD * c, s, False)
            for n in range(2):
                for j, k in enumerate(OUT_K):
                    load_piece(w_out_v[:, k, n * 512:n * 512 + 512], 512, KD * (len(CHUNKS) + n) + j,
                               j % RING, False)

            sp.wait_ge(o_lo, len(UNITS))
            sp.wait_ge(o_hi, len(UNITS))
            sp.wait_ge(rm_lo, len(RUNITS))
            sp.wait_ge(rm_hi, len(RUNITS))
            sp.wait_ge(kv_out, 16 * 6)
            sp.wait_ge(st_out, 16 * 4)

            def load_pair(p, s, first):
                if not first:
                    sp.wait_ge(gu_ps, p - SLOTS + 1)
                for e in range(2):
                    for m, v in enumerate((gate_v, up_v)):
                        sp.dma_start(w_moe[:, s, e, m, :], v[bass.ds(p * 2 + e, 1)].rearrange("o p n -> p (o n)")
                                     ).then_inc(gu_in[s], 16)
                if not first:
                    sp.wait_ge(y_ps, p - SLOTS + 1)
                for e in range(2):
                    sp.dma_start(w_moe[:, s, e, 2, :], down_v[bass.ds(p * 2 + e, 1)].rearrange("o p n -> p (o n)")
                                 ).then_inc(dn_in[s], 16)

            for p in range(SLOTS):
                if p == 2:
                    sp.wait_ge(piece_used, KD * (OUT0 + 2))
                load_pair(p, p, True)
            load_pair(SLOTS, 0, False)
            with sp.Fori(0, (NPAIR - AHEAD) // 6) as r:
                for j in range(6):
                    p, s, _, _, _ = turn(r, j)
                    load_pair(p, s, False)

            sp.wait_ge(slots_ready, 1)
            n_most = sp.value_load(most_i[0:1, 0:1], min_val=0, max_val=T_TOK)
            with sp.If(n_most > CAP):
                sp.wait_ge(y_ps, NPAIR)
                with sp.Fori(1, LEVELS) as lv:
                    with sp.Fori(0, NPAIR) as p:
                        it = (lv - 1) * NPAIR + p
                        sp.wait_ge(L_y, it + 1)
                        for e in range(2):
                            for m, v in enumerate((gate_v, up_v, down_v)):
                                sp.dma_start(w_moe[:, 0, e, m, :],
                                             v[bass.ds(p * 2 + e, 1)].rearrange("o p n -> p (o n)")
                                             ).then_inc(L_w, 16)
            yp = y_prompt.rearrange("o (t p) d -> p (o t) d", p=P)
            ys = y_sample.rearrange("o s d -> (o s) d")
            for t in range(NT):
                sp.wait_ge(y_fin, t + 1)
                if t < TAIL:
                    sp.dma_start(yp[:, t, :], x_sb[:, t, :]).then_inc(fin_out, 16)
                else:
                    sp.dma_start(ys, x_sb[0:DEC, t, :]).then_inc(fin_out, 16)
            sp.wait_ge(fin_out, 16 * NT)

        @block.gpsimd
        def _(pool):
            rt = w_router[:, :, :]

            def alone():
                pool.sem_inc(pool_pass, 1)

            pool.dma_start(g2_both[:, :, :], norm2_g).then_inc(g_in, 16)
            pool.dma_start(retgT[:, :], ret_norm_g).then_inc(g_in, 16)
            pool.dma_start(qk_g[:, 0, :], q_norm_g.to_broadcast([P, HD])).then_inc(g_in, 16)
            pool.dma_start(qk_g[:, 1, :], k_norm_g.to_broadcast([P, HD])).then_inc(g_in, 16)
            pool.dma_start(sinks[:, :], attn_sinks.to_broadcast([P, QH])).then_inc(g_in, 16)
            pool.dma_start(w_router[:, :, :], w_group).then_inc(g_in, 16)

            def split_piece(i, s, width):
                pool.wait_ge(hi_done, i + 1)
                nc.gpsimd.tensor_tensor(w_lo[:, s, 0:width], w_raw[:, s, 0:width],
                                        w_hi[:, s, 0:width].bitcast(F32), ALU.subtract).then_inc(split, 1)

            for k in range(KD):
                split_piece(k, k % RING, CHUNKS[0][1])
            with pool.Fori(2, LONE // RING) as r:
                for s in range(RING):
                    split_piece(r * RING + s, s, 512)
            for n in range(LONE, LONE + RING - 1):
                split_piece(n, n % RING, 512)
            steps = [0]

            def step(ins):
                ins.then_inc(root_step, 1)
                steps[0] += 1
                pool.wait_ge(root_step, steps[0])

            for m, b in [x[1:] for x in STEPS if x[0] == "ro"]:
                R = out_rows(RUNITS[m][0])
                pool.wait_ge(ms_ready, m + 1)
                root_steps(nc.gpsimd, step, ms_r[0:R, b, :], root_r[0:R, b])
                pool.sem_inc(root_ready, 1)
            split_piece(LONE + RING - 1, RING - 1, 512)
            with pool.Fori(LONE // RING + 1, 2 * (OUT0 + 2)) as r:
                for s in range(RING):
                    split_piece(r * RING + s, s, 512)

            def gather(p, u, first):
                if not first:
                    pool.wait_ge(xg_ps, p - 1)
                    alone()
                nc.gpsimd.tensor_copy(idx_now[:, u, :], idx[:, bass.ds(p, 1)]).then_inc(idx_c, 1)
                pool.wait_ge(idx_c, p + 1)
                if not first:
                    alone()
                pool.indirect_dma_start(out=xg[:, u, :], out_offset=None, in_=hn_d,
                                        in_offset=bass.IndirectOffsetOnAxis(ap=idx_now[:, u, 0:1], axis=0)
                                        ).then_inc(xg_in[u], 16)

            pool.wait_ge(hn_out[0], 16 * 3)
            pool.wait_ge(hn_out[1], 16 * 2)
            pool.wait_ge(idx_ready, 1)
            for u in range(2):
                gather(u, u, True)
            with pool.Fori(1, NPAIR // 2) as i:
                for u in range(2):
                    gather(i * 2 + u, u, False)
            pool.wait_ge(slots_ready, 1)
            n_most = pool.value_load(most_i[0:1, 0:1], min_val=0, max_val=T_TOK)
            with pool.If(n_most > CAP):
                pool.wait_ge(xg_ps, NPAIR)
                with pool.Fori(1, LEVELS) as lv:
                    pool.wait_ge(L_idx, lv)
                    alone()
                    with pool.Fori(0, NPAIR) as p:
                        it = (lv - 1) * NPAIR + p
                        pool.wait_ge(L_xt, it + 1)
                        alone()
                        nc.gpsimd.tensor_copy(idx_now[:, 0, :], idx[:, bass.ds(p, 1)]).then_inc(L_col, 1)
                        pool.wait_ge(L_col, it + 1)
                        alone()
                        pool.indirect_dma_start(out=xg[:, 0, :], out_offset=None, in_=hn_d,
                                                in_offset=bass.IndirectOffsetOnAxis(ap=idx_now[:, 0, 0:1], axis=0)
                                                ).then_inc(L_xg, 16)

            def fetch(levels):
                for t in range(NT):
                    for k in range(2):
                        n = out_rows(t)
                        pool.indirect_dma_start(out=y_tok[0:n, t, k, :], out_offset=None,
                                                in_=y_d[0:levels * NE * CAP, :],
                                                in_offset=bass.IndirectOffsetOnAxis(
                                                    ap=slot_i[0:n, k * NT + t:k * NT + t + 1], axis=0)
                                                ).then_inc(yg_in[t], 16)

            for u in range(2):
                pool.wait_ge(y_out[u], 8 * NPAIR)
            pool.wait_ge(y_ps, NPAIR)
            with pool.If(n_most > CAP):
                pool.wait_ge(L_out, 16 * NPAIR * (LEVELS - 1) + 16)
                fetch(LEVELS)
            with pool.If(n_most <= CAP):
                fetch(1)

        @block.tensor
        def _(pe):
            mm = nc.tensor.matmul
            busy = {0: [], 1: [], 2: []}

            def take(b):
                for s, n in busy[b]:
                    pe.wait_ge(s, n)

            pe.wait_ge(c_in, 32)
            n = 0
            for t in range(NT):
                pe.wait_ge(x_in[t], 16 if t < TAIL else 32)
                R = rows_of(t)
                xv = x_sb[0:R, t, :].rearrange("p (q k) -> p k q", k=KD)
                for half in range(2):
                    b = n % 2
                    take(b)
                    for j in range(4):
                        l = nc.tensor.transpose(side[:, b, j * P:j * P + R], xv[:, 4 * half + j, :],
                                                ident[0:R, 0:R])
                    l.then_inc(xt_ps, 1)
                    n += 1
                    busy[b] = [(xt_part, n)]
            pe.wait_ge(xt_lo, 2 * NT)
            pe.wait_ge(xt_hi, 2 * NT)

            def piece(c, kk, b):
                n = KD * c + kk
                s = n % RING
                pe.wait_ge(split, n + 1)
                width = CHUNKS[c][1] if c < OUT0 else 512
                if c < OUT0:
                    a_hi, a_lo = xT_hi[:, kk, :], xT_lo[:, kk, :]
                elif kk < 4:
                    a_hi, a_lo = mix_hi[:, kk, :], mix_lo[:, kk, :]
                    if c == OUT0:
                        pe.wait_ge(mix_clear, 1)
                        pe.wait_ge(o_hi, len(UNITS) - 3 + kk)
                        pe.wait_ge(o_lo, len(UNITS) - 3 + kk)
                else:
                    a_hi, a_lo = xT_hi[:, kk - 4, :], xT_lo[:, kk - 4, :]
                    if c == OUT0 and kk == 4:
                        pe.wait_ge(rm_hi, len(RUNITS))
                        pe.wait_ge(rm_lo, len(RUNITS))
                for t in range(NT):
                    R = rows_of(t)
                    if kk == 0 and c > 0:
                        pe.wait_ge(acc_free, nth["evict", c - 1, t])
                    for j, (a, w) in enumerate(((a_hi, w_hi), (a_hi, w_lo), (a_lo, w_hi))):
                        l = mm(acc[0:R, t, 0:width], a[:, P * t:P * t + R], w[:, s, 0:width],
                               start=(kk == 0 and j == 0), stop=(kk == KD - 1 and j == 2))
                    if kk == KD - 1:
                        l.then_inc(acc_done, 1)
                    elif t == NT - 1:
                        l.then_inc(piece_used, 1)
                if kk == KD - 1:
                    pe.wait_ge(acc_done, NT * (c + 1))
                    pe.sem_inc(piece_used, 1)

            def kT(t, b):
                R = rows_of(t)
                take(b)
                pe.wait_ge(posted, nth["post", SKV, t])
                l = nc.tensor.transpose(side[:, b, 0:R], sk[0:R, t, :], ident[0:R, 0:R])
                if t == TAIL:
                    pe.wait_ge(kv_in, 16 * 4)
                    l = nc.tensor.transpose(side[:, b, P:2 * P], cache_k[:, :], ident)
                l.then_inc(k_ps, 1)
                busy[b] = [(kT_ev, nth["kT", t])]

            def qT(t, b):
                R = rows_of(t)
                take(b)
                pe.wait_ge(posted, nth["post", SQ, t])
                for h in range(4):
                    l = nc.tensor.transpose(side[:, b, h * P:h * P + R],
                                            sq[0:R, t, h, :, :].rearrange("p g d -> p (g d)"), ident[0:R, 0:R])
                l.then_inc(q_ps, 1)
                busy[b] = [(qT_ev, nth["qT", t])]

            def rT_(t, b):
                R = rows_of(t)
                take(b)
                pe.wait_ge(posted, nth["post", RQK, t])
                for j in range(4):
                    l = nc.tensor.transpose(side[:, b, j * P:j * P + R], rqk[0:R, t, j * P:j * P + P],
                                            ident[0:R, 0:R])
                l.then_inc(r_ps, 1)
                busy[b] = [(rT_ev, nth["rT", t])]

            def score(i, b):
                t, g, hh = UNITS[i]
                take(b)
                pe.wait_ge(qT_ev, nth["qT", t])
                pe.wait_ge(kT_ev, NT)
                gs = slice(64 * g, 64 * g + 64)
                keys = []
                for c2 in range(2 if t < TAIL else 1):
                    c = 2 * t + c2
                    if t == TAIL:
                        keys.append([(CACHE0, WINDOW, 0), (SEQ, CH, WINDOW), (T_TOK, NMETA, BAND)])
                    elif c < 2:
                        keys.append([(0, CH * (c + 1), WINDOW - CH * c), (T_TOK, NMETA, BAND)])
                    else:
                        keys.append([(CH * c - WINDOW, BAND, 0), (T_TOK, NMETA, BAND)])
                for hl in range(2):
                    for lots in zip(*keys):
                        for c2, (col, n, dst) in enumerate(lots):
                            c = 2 * t + c2
                            l = mm(side[64 * c2:64 * c2 + 64, b, 256 * hl + dst:256 * hl + dst + n],
                                   sqT[gs, 2 * hh + hl, CH * c:CH * c + CH], skT[gs, col:col + n],
                                   start=True, stop=True)
                l.then_inc(s_ps, 1)

            def probs_T(i, b):
                R = out_rows(UNITS[i][0])
                pe.wait_ge(s_prob, i + 1)
                for hl in range(2):
                    nc.tensor.transpose(side[:, b, hl * P:hl * P + R], probs[0:R, b, hl, 0:P], ident[0:R, 0:R])
                for hl in range(2):
                    l = nc.tensor.transpose(side[0:CH + NMETA, b, 2 * P + hl * P:2 * P + hl * P + R],
                                            probs[0:R, b, hl, P:KEYS], ident[0:R, 0:R])
                l.then_inc(pT_ps, 1)

            def value(i, b):
                t, g, hh = UNITS[i]
                if i == 0:
                    pe.wait_ge(shift_in, 16 * 4)
                    pe.wait_ge(vmeta, 1)
                pe.wait_ge(pT_ev, i + 1)
                n = CH + NMETA
                gc = slice(64 * g, 64 * g + 64)
                for c2 in range(2 if t < TAIL else 1):
                    if t == TAIL:
                        lots = [(cache_v[:, gc], 0, P), (sv[0:n, t, gc], 1, n)]
                    else:
                        before = v_shift[:, t, gc] if c2 else (sv[:, t - 1, gc] if t else None)
                        lots = [(before, 0, P)] if before is not None else []
                        lots.append((v_own[0:n, 2 * t + c2, gc], 1, n))
                    q = slice(64 * c2, 64 * c2 + 64)
                    for j, (v, blk, kn) in enumerate(lots):
                        for hl in range(2):
                            l = mm(side[64 * hl:64 * hl + 64, b, q], v, probsT[0:kn, b, blk, hl, q],
                                   start=(j == 0), stop=(j == len(lots) - 1))
                l.then_inc(o_ps, 1)
                busy[b] = [(o_hi, i + 1), (o_lo, i + 1)]

            def outer(lo, n, t, par, b):
                for hp in range(2):
                    h = 2 * hp + par
                    l = mm(side[64 * par:64 * par + 64, b, P * hp:P * hp + P],
                           rqk[lo:lo + n, t, 256 + 64 * h:256 + 64 * h + 64],
                           rv[lo:lo + n, t, P * h:P * h + P], start=True, stop=True)
                l.then_inc(st_ps, 1)

            def meta_state(par, b):
                take(b)
                pe.wait_ge(acc_free, nth["evict", RV, TAIL])
                pe.wait_ge(posted, nth["post", RQK, TAIL])
                outer(DEC, NMETA, TAIL, par, b)
                busy[b] = [(st_new, st_nth["meta_state", par])]

            def ret_scores(m, b):
                t, par = RUNITS[m]
                R = out_rows(t)
                hs, tok = slice(64 * par, 64 * par + 64), slice(P * t, P * t + R)
                take(b)
                pe.wait_ge(rT_ev, nth["rT", t])
                for hp in range(2):
                    l = mm(side[0:R, b, P * hp:P * hp + R], rT[hs, 2 + hp, tok], rT[hs, hp, tok],
                           start=True, stop=True)
                l.then_inc(ra_ps, 1)

            def ret_out(m, b):
                t, par = RUNITS[m]
                R = out_rows(t)
                state = state_s if t == TAIL else state_p
                hs, tok = slice(64 * par, 64 * par + 64), slice(P * t, P * t + R)
                pe.wait_ge(ra_ev, m + 1)
                outer(0, R, t, par, b)
                if t != TAIL:
                    pe.wait_ge(st_new, st_nth[("ro", m - 2) if t else ("meta_state", par)])
                for hp in range(2):
                    h = 2 * hp + par
                    out = side[0:R, b, 2 * P + P * hp:2 * P + P * hp + P]
                    l = mm(out, ret_aT[0:R, b, hp, 0:R], rv[0:R, t, P * h:P * h + P], start=True, stop=False)
                    if R < P:
                        l.then_inc(ro_part, 1)
                        pe.wait_ge(ro_part, 2 * m + hp + 1)
                    l = mm(out, rT[hs, hp, tok], state[hs, hp, :], start=False, stop=True)
                    if R < P and hp == 0:
                        l.then_inc(ro_cross, 1)
                        pe.wait_ge(ro_cross, m + 1)
                l.then_inc(ro_ps, 1)

            def ret_T(m, b):
                t, par = RUNITS[m]
                R = out_rows(t)
                pe.wait_ge(ro_rows, m + 1)
                pe.wait_ge(st_new, st_nth["ro", m])
                for hp in range(2):
                    l = nc.tensor.transpose(side[:, b, P * hp:P * hp + R], o_rows[0:R, b, hp, :],
                                            ident[0:R, 0:R])
                l.then_inc(rm_ps, 1)
                busy[b] = [(rm_part, m + 1)]

            def hid_T(n, t, b):
                R = out_rows(t)
                take(b)
                pe.wait_ge(acc_free, nth["evict", OUT0 + n, t])
                for j in range(4):
                    lo = 512 * n + P * j
                    l = nc.tensor.transpose(side[:, b, P * j:P * j + R], x_sb[0:R, t, lo:lo + P],
                                            ident[0:R, 0:R])
                l.then_inc(hT_ps, 1)

            def logit(n, t, b):
                R = out_rows(t)
                pe.wait_ge(hT_ev, nth["hT", n, t])
                for j in range(4):
                    l = mm(side[0:R, b, 0:NG + NE], hnT[:, b, j, 0:R], w_router[:, 4 * n + j, :],
                           start=(j == 0), stop=(j == 3))
                l.then_inc(lg_ps, 1)
                busy[b] = [(lg_ev, nth["logit", n, t])]

            does = {"piece": piece, "kT": kT, "qT": qT, "rT": rT_, "score": score, "pT": probs_T,
                    "value": value, "meta_state": meta_state, "ra": ret_scores, "ro": ret_out, "rm": ret_T,
                    "hT": hid_T, "logit": logit}
            for kind, *args in STEPS:
                if kind in does:
                    does[kind](*args)

            pe.wait_ge(m_ready, 1)
            for b in range(3):
                take(b)
            for t in range(NT):
                for t2 in range(t + 1):
                    mm(side3[:, NE * t:NE * t + NE], counting[:, 0 if t2 == t else 1, :], chosen[:, t2, :],
                       start=(t2 == 0), stop=(t2 == t))
            for t in range(NT):
                l = mm(side3[:, NE * NT:NE * NT + NE], counting[:, 1, :], chosen[:, t, :], start=(t == 0), stop=(t == NT - 1))
            l.then_inc(rank_ps, 1)
            pe.wait_ge(oh_ready, 1)

            def find_rows():
                for j in range(2 * NT):
                    l = mm(side3[:, 256:256 + NPAIR], row_oh[:, j, :], pair_tok[:, j, :], start=(j == 0),
                           stop=(j == 2 * NT - 1))
                return l

            find_rows().then_inc(idx_ps, 1)

            def rows_T(p, u, wait):
                pe.wait_ge(xg_in[u], wait)
                gv = xg[:, u, :].rearrange("p (q k) -> p k q", k=KD)
                for k in range(KD):
                    l = nc.tensor.transpose(side[:, k // 4, (k % 4) * P:(k % 4) * P + P], gv[:, k, :], ident)
                return l

            def gate_up(u, slot, xu):
                for k in range(KD):
                    for e in range(2):
                        l = mm(acc[64 * e:64 * e + 64, u, :].rearrange("p (m f) -> p m f", m=2),
                               xgT[:, xu, k, 64 * e:64 * e + 64], w_moe[:, slot, e, 0:2, k * FF:k * FF + FF],
                               start=(k == 0), stop=(k == KD - 1))
                return l

            def act_T():
                av = actv[:, :].rearrange("p (q j) -> p j q", j=2)
                for j in range(2):
                    l = nc.tensor.transpose(side3[:, P * j:P * j + P], av[:, j, :], ident)
                return l

            def down(slot):
                for n in range(2):
                    for j in range(2):
                        for e in range(2):
                            l = mm(acc[64 * e:64 * e + 64, 2 + n, :], actT[:, j, 64 * e:64 * e + 64],
                                   w_moe[:, slot, e, 2, j * D + n * 512:j * D + n * 512 + 512],
                                   start=(j == 0), stop=(j == 1))
                return l

            def first_half(p, slot, slot_uses, u, u_uses, first=False):
                if not first:
                    pe.wait_ge(xg_ev, p)
                rows_T(p, u, u_uses * 16 + 16).then_inc(xg_ps, 1)
                pe.wait_ge(xg_ev, p + 1)
                pe.wait_ge(gu_in[slot], slot_uses * 64 + 64)
                gate_up(u, slot, u).then_inc(gu_ps, 1)

            def second_half(p, slot, slot_uses, u, u_uses, first=False):
                pe.wait_ge(e_act, p + 1)
                act_T().then_inc(aT_ps, 1)
                pe.wait_ge(aT_ev, p + 1)
                pe.wait_ge(dn_in[slot], slot_uses * 32 + 32)
                if not first:
                    pe.wait_ge(y_ev, p)
                down(slot).then_inc(y_ps, 1)

            pe.wait_ge(idx_ready, 1)
            pe.wait_ge(acc_free, NT * (OUT0 + 2))
            first_half(*turn(0, -AHEAD), first=True)
            for j in range(1 - AHEAD, 0):
                first_half(*turn(0, j))
                second_half(*turn(0, j - 1), first=j == 1 - AHEAD)
            with pe.Fori(0, (NPAIR - AHEAD) // 6) as r:
                for j in range(6):
                    first_half(*turn(r, j))
                    second_half(*turn(r, j - 1))
            second_half(*turn(0, NPAIR - AHEAD - 1))

            pe.wait_ge(slots_ready, 1)
            n_most = pe.value_load(most_i[0:1, 0:1], min_val=0, max_val=T_TOK)
            with pe.If(n_most > CAP):
                pe.wait_ge(y_ev, NPAIR)
                pe.sem_inc(L_xt, 1)
                pe.sem_inc(L_y, 1)
                with pe.Fori(1, LEVELS) as lv:
                    pe.wait_ge(L_oh, lv)
                    find_rows().then_inc(L_ips, 1)
                    with pe.Fori(0, NPAIR) as p:
                        it = (lv - 1) * NPAIR + p
                        pe.wait_ge(L_xg, it * 16 + 16)
                        rows_T(0, 0, 16).then_inc(L_xt, 1)
                        pe.wait_ge(L_xe, it + 1)
                        pe.wait_ge(L_w, it * 96 + 96)
                        gate_up(0, 0, 0).then_inc(L_gu, 1)
                        pe.wait_ge(L_act, it + 1)
                        act_T().then_inc(L_at, 1)
                        pe.wait_ge(L_ae, it + 1)
                        pe.wait_ge(L_ye, it + 1)
                        down(0).then_inc(L_y, 1)

        @block.scalar
        def _(act):
            af = nc.scalar.activation
            steps = [0]

            def step(ins):
                ins.then_inc(act_step, 1)
                steps[0] += 1
                act.wait_ge(act_step, steps[0])

            squared = [0]

            ck = cache_swa_k.rearrange("o b w g d -> (o b w) (g d)")
            cv = cache_swa_v.rearrange("o b w g d -> (o b w) (g d)")
            act.dma_start(cache_k[:, :], ck).then_inc(kv_in, 16)
            act.dma_start(cache_v[:, :], cv).then_inc(kv_in, 16)
            cs = cache_ret_state.rearrange("o b (i h) k v -> (h k) (o b i) v", h=2)
            for i in range(2):
                act.dma_start(state_s[:, i, :], cs[:, i, :]).then_inc(kv_in, 16)

            n = 0
            for t in range(NT):
                R = rows_of(t)
                act.wait_ge(x_in[t], 16 if t < TAIL else 32)
                if t == 0:
                    act.wait_ge(ssq_clear, 1)
                else:
                    act.wait_ge(act_step, steps[0])
                step(af(rqk[0:R, 0:2, :].rearrange("p a n -> p (a n)"), x_sb[0:R, t, :], ACT.Square,
                        accum_out=ssq[0:R, t:t + 1]))
                for half in range(2):
                    n += 1
                    act.wait_ge(xt_part, n)
                    nc.scalar.copy(xT_hi[:, 4 * half:4 * half + 4, P * t:P * t + R],
                                   part[:, half, :, 0:R]).then_inc(xt_hi, 1)

            act.wait_ge(rstd_ready, 1)

            def evict(c, t, b):
                if c >= OUT0:
                    return
                R = rows_of(t)
                r1 = rstd1[0:R, t:t + 1]
                act.wait_ge(acc_done, NT * c + t + 1)
                if c == SKV:
                    af(sk[0:R, t, :], acc[0:R, t, 0:P], ACT.Copy, scale=r1)
                    af(sv[0:R, t, :], acc[0:R, t, P:2 * P], ACT.Copy, scale=r1).then_inc(acc_free, 1)
                    return
                dst = {SQ: sq[0:R, t].rearrange("p h g d -> p (h g d)"), RQK: rqk[0:R, t, :],
                       RV: rv[0:R, t, :], RG: gate[0:R, t, :]}[c]
                af(dst, acc[0:R, t, :], ACT.Copy, scale=r1).then_inc(acc_free, 1)

            def squares_of(c, t, b):
                R = rows_of(t)
                act.wait_ge(acc_free, nth["evict", c, t])
                if squared[0]:
                    act.wait_ge(raw_sq_used, squared[0])
                squared[0] += 1
                if c == SKV:
                    af(h_sq[0:R, 0:P], sk[0:R, t, :], ACT.Square).then_inc(raw_sq, 1)
                else:
                    af(h_sq[0:R, :], sq[0:R, t].rearrange("p h g d -> p (h g d)"), ACT.Square
                       ).then_inc(raw_sq, 1)

            def post(c, t, b):
                if c != RG:
                    return
                R = rows_of(t)
                act.wait_ge(acc_free, nth["evict", c, t])
                if t == ORDER[0]:
                    act.wait_ge(s_ps, len(UNITS))
                af(sig[t][0:R, :], gate[0:R, t, :], ACT.Sigmoid).then_inc(gate_z, 1)

            def high(n):
                if n >= KD * (OUT0 + 2):
                    return
                s, width = n % RING, CHUNKS[0][1] if n < KD else 512
                act.wait_ge(raw_in[s], 16 * (n // RING + 1))
                if n >= RING:
                    act.wait_ge(piece_used, n - RING + 1)
                nc.scalar.copy(w_hi[:, s, 0:width], w_raw[:, s, 0:width]).then_inc(hi_done, 1)

            def piece(c, kk, b):
                high(KD * c + kk + RING - 1)

            def meta_v(b):
                act.wait_ge(acc_free, NT)
                own = v_own[:, :, :].rearrange("p (t c) d -> p t c d", c=2)
                act.dma_start(v_shift[64:128, :, :], sv[0:64, 0:4, :]).then_inc(shift_in, 16)
                act.dma_start(v_shift[0:64, 1:4, :], sv[64:128, 0:3, :]).then_inc(shift_in, 16)
                act.dma_start(own[0:64, :, 0, :], sv[0:64, 0:4, :]).then_inc(shift_in, 16)
                act.dma_start(own[0:64, :, 1, :], sv[64:128, 0:4, :]).then_inc(shift_in, 16)

            def keys_out(b):
                act.wait_ge(posted, NT)
                for out_p, out_s, rows_, old in ((k_prompt, k_sample, sk, ck), (v_prompt, v_sample, sv, cv)):
                    op = out_p.rearrange("o b w g d -> (o b w) (g d)")
                    os = out_s.rearrange("o b w g d -> (o b w) (g d)")
                    act.dma_start(op, rows_[:, 3, :]).then_inc(kv_out, 16)
                    act.dma_start(os[DEC:, :], rows_[0:DEC, TAIL, :]).then_inc(kv_out, 16)
                    act.dma_start(os[0:WINDOW - DEC, :], old[DEC:, :]).then_inc(kv_out, 16)

            def kT(t, b):
                R = rows_of(t)
                act.wait_ge(k_ps, nth["kT", t])
                if t == TAIL:
                    nc.scalar.copy(skT[:, CACHE0:CACHE0 + P], side[:, b, P:2 * P])
                nc.scalar.copy(skT[:, P * t:P * t + R], side[:, b, 0:R]).then_inc(kT_ev, 1)

            def rT_(t, b):
                R = rows_of(t)
                act.wait_ge(r_ps, nth["rT", t])
                nc.scalar.copy(rT[:, :, P * t:P * t + R],
                               side[:, b, :].rearrange("p (j n) -> p j n", j=4)[:, :, 0:R]).then_inc(rT_ev, 1)

            def score(i, b):
                R = out_rows(UNITS[i][0])
                act.wait_ge(s_max, i + 1)
                for hl in range(2):
                    af(probs[0:R, b, hl, :], side[0:R, b, 256 * hl:256 * hl + KEYS], ACT.Exp,
                       scale=HD ** -0.5, bias=soft[0:R, b, 2 + hl:3 + hl], accum_out=soft[0:R, b, 4 + hl:5 + hl])
                af(soft[0:R, b, 8:10], soft[0:R, b, 6:8], ACT.Exp).then_inc(s_exp, 1)

            def probs_T(i, b):
                R = out_rows(UNITS[i][0])
                act.wait_ge(pT_ps, i + 1)
                nc.scalar.copy(probsT[:, b, 0, :, 0:R],
                               side[:, b, 0:2 * P].rearrange("p (j n) -> p j n", j=2)[:, :, 0:R])
                nc.scalar.copy(probsT[0:CH + NMETA, b, 1, :, 0:R],
                               side[0:CH + NMETA, b, 2 * P:].rearrange("p (j n) -> p j n", j=2)[:, :, 0:R]
                               ).then_inc(pT_ev, 1)

            def value(i, b):
                t, g, hh = UNITS[i]
                R = out_rows(t)
                act.wait_ge(o_ps, i + 1)
                if i == 0:
                    act.wait_ge(mix_clear, 1)
                nc.scalar.copy(mix_hi[:, 2 * g + hh, P * t:P * t + R], side[:, b, 0:R]).then_inc(o_hi, 1)

            def ret_out(m, b):
                R = out_rows(RUNITS[m][0])
                act.wait_ge(ro_ps, m + 1)
                af(squares[0:R, b, :], side[0:R, b, 2 * P:], ACT.Square).then_inc(ro_sq, 1)

            def ret_T(m, b):
                t, par = RUNITS[m]
                R = out_rows(t)
                act.wait_ge(rm_part, m + 1)
                nc.scalar.copy(xT_hi[:, par:4:2, P * t:P * t + R], part_r[:, b, :, 0:R]).then_inc(rm_hi, 1)

            def states_out(b):
                act.wait_ge(st_new, len(st_nth))
                for st, out in ((state_s, ret_sample), (state_p, ret_prompt)):
                    dst = out.rearrange("o b (i h) k v -> (h k) (o b i) v", h=2)
                    for j in range(2):
                        act.dma_start(dst[:, j, :], st[:, j, :]).then_inc(st_out, 16)

            def square(n, t, b):
                R = out_rows(t)
                act.wait_ge(acc_free, nth["evict", OUT0 + n, t])
                act.wait_ge(ssq_clear, 2)
                if nth["square", n, t] > 1:
                    act.wait_ge(sq2, nth["square", n, t] - 1)
                af(xsq[0:R, :], x_sb[0:R, t, 512 * n:512 * n + 512], ACT.Square,
                   accum_out=ssq2[0:R, n, t:t + 1]).then_inc(sq2, 1)

            for n in range(RING - 1):
                high(n)
            does = {"piece": piece, "evict": evict, "sums": squares_of, "post": post, "meta_v": meta_v,
                    "kv_out": keys_out, "kT": kT, "rT": rT_,
                    "score": score, "pT": probs_T, "value": value, "ro": ret_out, "rm": ret_T,
                    "states_out": states_out, "square": square}
            for kind, *args in STEPS:
                if kind in does:
                    does[kind](*args)

            act.wait_ge(rstd2_rdy, 1)
            for t in range(NT):
                R = out_rows(t)
                b = t % 2
                if t >= 2:
                    act.wait_ge(hn_out[b], 16 * (t // 2))
                af(rows[0:R, b, :], x_sb[0:R, t, :], ACT.Copy, scale=rstd2[0:R, t:t + 1]).then_inc(hn_rows, 1)
                act.wait_ge(hn_rows, t + 1)
                act.dma_start(hn_d[P * t:P * t + R, :], rows[0:R, b, :]).then_inc(hn_out[b], 16)
            act.wait_ge(r_exp, 1)
            step(af(r4b[:, :, :], r4[:, :, :], ACT.Exp))
            act.sem_inc(r_expd, 1)
            act.wait_ge(r_exp, 2)
            af(small[:, 20:25], small[:, 25:30], ACT.Exp).then_inc(r_expd, 1)

            def pair_out(p, u, rnd, first):
                act.wait_ge(y_ps, p + 1)
                if not first:
                    act.wait_ge(y_out[u], rnd * 16)
                step_free(nc.scalar.copy(y_sb[:, u, :], acc[:, 2:4, :].rearrange("p b n -> p (b n)")), p)
                act.dma_start(y_pairs[bass.ds(p, 1)].rearrange("o r d -> (o r) d"), y_sb[:, u, :]
                              ).then_inc(y_out[u], 16)

            def step_free(ins, p):
                ins.then_inc(y_ev, 1)
                act.wait_ge(y_ev, p + 1)

            def pair_exp(p, u, first):
                act.wait_ge(gu_ps, p + 1)
                if not first:
                    act.wait_ge(e_act, p)
                af(glu[:, 0, :], acc[:, u, 0:FF], ACT.Sigmoid).then_inc(e_exp, 1)

            pair_exp(0, 0, True)
            pair_exp(1, 1, False)
            pair_out(0, 0, 0, True)
            pair_exp(2, 0, False)
            pair_out(1, 1, 0, True)
            pair_exp(3, 1, False)
            with act.Fori(1, NPAIR // 2 - 1) as i:
                for u in range(2):
                    pair_out(i * 2 + u, u, i, False)
                    pair_exp(i * 2 + u + 2, u, False)
            pair_out(NPAIR - 2, 0, NPAIR // 2 - 1, False)
            pair_out(NPAIR - 1, 1, NPAIR // 2 - 1, False)

            act.wait_ge(slots_ready, 1)
            n_most = act.value_load(most_i[0:1, 0:1], min_val=0, max_val=T_TOK)
            with act.If(n_most > CAP):
                act.wait_ge(y_out[0], 8 * NPAIR)
                act.sem_inc(L_ye, 1)
                act.sem_inc(L_out, 16)
                with act.Fori(1, LEVELS) as lv:
                    with act.Fori(0, NPAIR) as p:
                        it = (lv - 1) * NPAIR + p
                        act.wait_ge(L_gu, it + 1)
                        af(glu[:, 0, :], acc[:, 0, 0:FF], ACT.Sigmoid).then_inc(L_ex, 1)
                        act.wait_ge(L_y, it + 2)
                        act.wait_ge(L_out, it * 16 + 16)
                        nc.scalar.copy(y_sb[:, 0, :], acc[:, 2:4, :].rearrange("p b n -> p (b n)")).then_inc(L_ye, 1)
                        act.wait_ge(L_ye, it + 2)
                        act.dma_start(y_pairs[bass.ds(lv * NPAIR + p, 1)].rearrange("o r d -> (o r) d"),
                                      y_sb[:, 0, :]).then_inc(L_out, 16)

        @block.vector
        def _(dve):
            tt = nc.vector.tensor_tensor
            ts = nc.vector.tensor_scalar
            stt = nc.vector.scalar_tensor_tensor
            red = nc.vector.tensor_reduce
            steps = [0]

            def step(ins):
                ins.then_inc(dve_step, 1)
                steps[0] += 1
                dve.wait_ge(dve_step, steps[0])

            def inv_root(n, R=P):
                return root_steps(nc.vector, step, ms[0:R, 0:n], root[0:R, :, 0:n])

            step(nc.vector.memset(ssq[:, :], 1.0))
            dve.sem_inc(ssq_clear, 1)
            step(nc.vector.memset(ssq_qk[:, :], 1.0))
            step(nc.vector.memset(ssq2[:, :, :], 1.0))
            dve.sem_inc(ssq_clear, 1)
            dve.wait_ge(c_in, 32)
            n = 0
            for t in range(NT):
                R = rows_of(t)
                for half in range(2):
                    n += 1
                    dve.wait_ge(xt_ps, n)
                    if n > 2:
                        dve.wait_ge(xt_lo, n - 2)
                        dve.wait_ge(xt_hi, n - 2)
                    src = side[:, (n - 1) % 2, :].rearrange("p (j n) -> p j n", j=4)[:, :, 0:R]
                    tt(part[:, half, :, 0:R], src,
                       g1T[:, 4 * half:4 * half + 4].unsqueeze(2).to_broadcast([P, 4, R]), ALU.mult
                       ).then_inc(xt_part, 1)
                    dve.wait_ge(xt_hi, n)
                    dst = (slice(None), slice(4 * half, 4 * half + 4), slice(P * t, P * t + R))
                    tt(xT_lo[dst], part[:, half, :, 0:R], xT_hi[dst].bitcast(F32), ALU.subtract
                       ).then_inc(xt_lo, 1)
            dve.wait_ge(act_step, NT)
            step(ts(ms[:, 0:NT], ssq[:, 0:NT], 1.0 / D, EPS, ALU.mult, ALU.add))
            step(nc.vector.tensor_copy(rstd1[:, :], inv_root(NT)))
            dve.sem_inc(rstd_ready, 1)
            lo = at["before"][0]
            step(nc.vector.tensor_copy(counting[:, :, :].rearrange("p a n -> p (a n)"), cst[:, lo:lo + 2 * P]))
            step(ts(small[:, 100:108], iota[:, 0:8], -OFF, None, ALU.add))
            dve.wait_ge(g_in, 16 * 6)
            for a in range(2):
                g = qk_g[:, a:a + 1, :].to_broadcast([P, NT, HD])
                step(tt(rope_g[:, a, 0], cos_t, g, ALU.mult))
                h = HD // 2
                step(tt(rope_g[:, a, 1, :, 0:h], sin_t[:, :, 0:h], qk_g[:, a:a + 1, h:].to_broadcast([P, NT, h]),
                        ALU.mult))
                step(tt(rope_g[:, a, 1, :, h:], sin_t[:, :, h:], qk_g[:, a:a + 1, 0:h].to_broadcast([P, NT, h]),
                        ALU.mult))

            def rope(src, nh, R, cos, sin):
                h = HD // 2
                s = src.rearrange("p (n d) -> p n d", n=nh)
                a = h_a[0:R, 0:nh * HD].rearrange("p (n d) -> p n d", n=nh)
                b = h_b[0:R, 0:nh * HD].rearrange("p (n d) -> p n d", n=nh)
                step(tt(a, s, cos.unsqueeze(1).to_broadcast([R, nh, HD]), ALU.mult))
                step(tt(b[:, :, 0:h], s[:, :, h:], sin[:, 0:h].unsqueeze(1).to_broadcast([R, nh, h]), ALU.mult))
                step(tt(b[:, :, h:], s[:, :, 0:h], sin[:, h:].unsqueeze(1).to_broadcast([R, nh, h]), ALU.mult))
                step(tt(a, a, b, ALU.add))
                return a

            squared = [0]

            def sums(c, t, b):
                R, nh = rows_of(t), 2 if c == SKV else QH
                squared[0] += 1
                dve.wait_ge(raw_sq, squared[0])
                step(red(ssq_qk[0:R, nh * t:nh * t + nh],
                         h_sq[0:R, 0:nh * HD].rearrange("p (n d) -> p n d", n=nh), AX_X, ALU.add))
                dve.sem_inc(raw_sq_used, 1)

            def factors(c, b):
                n = NT * (2 if c == SKV else QH)
                step(ts(ms[:, 0:n], ssq_qk[:, 0:n], 1.0 / HD, EPS, ALU.mult, ALU.add))
                step(nc.vector.tensor_copy(rstd_qk[:, 0:n], inv_root(n)))

            posts = [0]

            def post(c, t, b):
                R = rows_of(t)
                if posts[0]:
                    dve.wait_ge(posted, posts[0])
                posts[0] += 1
                dve.wait_ge(acc_free, nth["evict", c, t])
                if c == RG:
                    dve.wait_ge(gate_z, ORDER.index(t) + 1)
                    tt(gate[0:R, t, :], gate[0:R, t, :], sig[t][0:R, :], ALU.mult).then_inc(posted, 1)
                    return
                if c == RQK:
                    raw = rqk[0:R, t, :]
                    a = rope(raw, 8, R, cos_t[0:R, t], sin_t[0:R, t])
                    tt(raw.rearrange("p (n d) -> p n d", n=8), a,
                       ret_scale[0:R, t // TAIL, :].unsqueeze(2).to_broadcast([R, 8, HD]), ALU.mult
                       ).then_inc(posted, 1)
                    return
                nh, kind = (2, 1) if c == SKV else (QH, 0)
                factor = rstd_qk[0:R, nh * t:nh * t + nh]
                raw = sk[0:R, t, :] if c == SKV else sq[0:R, t].rearrange("p h g d -> p (h g d)")
                a = rope(raw, nh, R, rope_g[0:R, kind, 0, t], rope_g[0:R, kind, 1, t])
                if c == SKV:
                    r = factor.unsqueeze(2).to_broadcast([R, nh, HD])
                    tt(raw.rearrange("p (n d) -> p n d", n=2), a, r, ALU.mult).then_inc(posted, 1)
                    return
                for g in range(2):
                    l = tt(sq[0:R, t, :, g, :], a[:, 4 * g:4 * g + 4, :],
                           factor[:, 4 * g:4 * g + 4].unsqueeze(2).to_broadcast([R, 4, HD]), ALU.mult)
                l.then_inc(posted, 1)

            def meta_v(b):
                dve.wait_ge(acc_free, NT)
                nc.vector.tensor_copy(v_own[64:64 + NMETA, :, :], sv[64:64 + NMETA, TAIL:TAIL + 1, :]
                                      .to_broadcast([NMETA, 8, P]))
                nc.vector.memset(v_shift[0:64, 0, :], 0.0).then_inc(vmeta, 1)

            def qT(t, b):
                R = rows_of(t)
                dve.wait_ge(q_ps, nth["qT", t])
                nc.vector.tensor_copy(sqT[:, :, P * t:P * t + R],
                                      side[:, b, :].rearrange("p (j n) -> p j n", j=4)[:, :, 0:R]
                                      ).then_inc(qT_ev, 1)

            def score(i, b):
                t, g, hh = UNITS[i]
                R = out_rows(t)
                dve.wait_ge(s_ps, i + 1)
                s2 = side[:, b, :].rearrange("p (h n) -> p h n", h=2)
                if t == 0:
                    nc.vector.memset(s2[0:64, :, 0:WINDOW], NEG)
                    step(nc.vector.memset(s2[64:128, :, 0:CH], NEG))
                sink = sinks[0:R, 4 * g + 2 * hh:4 * g + 2 * hh + 2]
                v = soft[0:R, b, :]
                step(red(v[:, 0:2], s2[0:R, :, 0:KEYS], AX_X, ALU.max))
                step(stt(out=v[:, 0:2], in0=v[:, 0:2], scalar=HD ** -0.5, in1=sink, op0=ALU.mult, op1=ALU.max))
                ts(v[:, 2:4], v[:, 0:2], -1.0, None, ALU.mult)
                tt(v[:, 6:8], sink, v[:, 0:2], ALU.subtract).then_inc(s_max, 1)

            def norm(i, b):
                R = out_rows(UNITS[i][0])
                v = soft[0:R, b, :]
                dve.wait_ge(s_exp, i + 1)
                step(tt(v[:, 10:12], v[:, 4:6], v[:, 8:10], ALU.add))
                step(nc.vector.reciprocal(v[:, 12:14], v[:, 10:12]))
                tt(probs[0:R, b], probs[0:R, b], v[:, 12:14].unsqueeze(2).to_broadcast([R, 2, KEYS]), ALU.mult
                   ).then_inc(s_prob, 1)

            def value(i, b):
                t, g, hh = UNITS[i]
                R = out_rows(t)
                if i == 0:
                    dve.wait_ge(q_ps, NT)
                    nc.vector.memset(mix_hi[:, :, T_TOK:].bitcast(F32), 0.0)
                    nc.vector.memset(mix_lo[:, :, T_TOK:].bitcast(F32), 0.0).then_inc(mix_clear, 1)
                dve.wait_ge(o_hi, i + 1)
                tok = slice(P * t, P * t + R)
                tt(mix_lo[:, 2 * g + hh, tok], side[:, b, 0:R], mix_hi[:, 2 * g + hh, tok].bitcast(F32),
                   ALU.subtract).then_inc(o_lo, 1)

            def ps_state(par, b):
                return side[64 * par:64 * par + 64, b, 0:2 * P].rearrange("p (i v) -> p i v", i=2)

            def meta_state(par, b):
                hs = slice(64 * par, 64 * par + 64)
                dve.wait_ge(st_ps, st_nth["meta_state", par])
                tt(state_p[hs], ps_state(par, b), decay[hs, 2, :].unsqueeze(2).to_broadcast([64, 2, RDV]),
                   ALU.mult).then_inc(st_new, 1)

            causal = const("causal")

            def ret_scores(m, b):
                R = out_rows(RUNITS[m][0])
                dve.wait_ge(ra_ps, m + 1)
                tt(ret_aT[0:R, b, :, 0:R], side[0:R, b, 0:2 * P].rearrange("p (j n) -> p j n", j=2)[:, :, 0:R],
                   causal[0:R, 0:R].unsqueeze(1).to_broadcast([R, 2, R]), ALU.mult).then_inc(ra_ev, 1)

            def ret_out(m, b):
                t, par = RUNITS[m]
                R = out_rows(t)
                hs = slice(64 * par, 64 * par + 64)
                state = state_s if t == TAIL else state_p
                dve.wait_ge(st_ps, st_nth["ro", m])
                dve.wait_ge(ro_sq, m + 1)
                tmp = h_b[hs, 0:2 * RDV].rearrange("p (i v) -> p i v", i=2)
                step(tt(tmp, ps_state(par, b), state[hs], ALU.add))
                tt(state[hs], tmp, decay[hs, t // TAIL, :].unsqueeze(2).to_broadcast([64, 2, RDV]), ALU.mult
                   ).then_inc(st_new, 1)
                step(red(ssq[0:R, 0:2], squares[0:R, b, :].rearrange("p (j n) -> p j n", j=2), AX_X, ALU.add))
                ts(ms_r[0:R, b, :], ssq[0:R, 0:2], 1.0 / RDV, EPS, ALU.mult, ALU.add).then_inc(ms_ready, 1)

            def ret_norm(m, b):
                t, par = RUNITS[m]
                R = out_rows(t)
                dve.wait_ge(posted, nth["post", RG, t])
                a = h_a[0:R, 0:2 * P].rearrange("p (j n) -> p j n", j=2)
                g2 = gate[0:R, t, :].rearrange("p (j q n) -> p j q n", j=2, q=2)[:, :, par, :]
                step(tt(a, side[0:R, b, 2 * P:].rearrange("p (j n) -> p j n", j=2), g2, ALU.mult))
                dve.wait_ge(root_ready, m + 1)
                tt(o_rows[0:R, b], a, root_r[0:R, b, 1].unsqueeze(2).to_broadcast([R, 2, RDV]), ALU.mult
                   ).then_inc(ro_rows, 1)

            def ret_T(m, b):
                t, par = RUNITS[m]
                R = out_rows(t)
                dve.wait_ge(rm_ps, m + 1)
                tt(part_r[:, b, :, 0:R], side[:, b, 0:2 * P].rearrange("p (j n) -> p j n", j=2)[:, :, 0:R],
                   retgT[:, par:4:2].unsqueeze(2).to_broadcast([P, 2, R]), ALU.mult).then_inc(rm_part, 1)
                dve.wait_ge(rm_hi, m + 1)
                dst = (slice(None), slice(par, 4, 2), slice(P * t, P * t + R))
                tt(xT_lo[dst], part_r[:, b, :, 0:R], xT_hi[dst].bitcast(F32), ALU.subtract).then_inc(rm_lo, 1)

            def evict(c, t, b):
                if c < OUT0:
                    return
                R = out_rows(t)
                cols = slice(512 * (c - OUT0), 512 * (c - OUT0) + 512)
                dve.wait_ge(acc_done, NT * c + t + 1)
                tt(x_sb[0:R, t, cols], x_sb[0:R, t, cols], acc[0:R, t, :], ALU.add).then_inc(acc_free, 1)

            def hid_T(n, t, b):
                R = out_rows(t)
                dve.wait_ge(hT_ps, nth["hT", n, t])
                tt(hnT[:, b, :, 0:R], side[:, b, :].rearrange("p (j n) -> p j n", j=4)[:, :, 0:R],
                   g2_both[:, 1, 4 * n:4 * n + 4].unsqueeze(2).to_broadcast([P, 4, R]), ALU.mult
                   ).then_inc(hT_ev, 1)

            def logit(n, t, b):
                R = out_rows(t)
                if n == 0 and t == 0:
                    step(nc.vector.memset(logits[:, :, :], 0.0))
                dve.wait_ge(lg_ps, nth["logit", n, t])
                ps = side[0:R, b, 0:NG + NE]
                if n == 0:
                    nc.vector.tensor_copy(logits[0:R, t, :], ps).then_inc(lg_ev, 1)
                else:
                    tt(logits[0:R, t, :], logits[0:R, t, :], ps, ALU.add).then_inc(lg_ev, 1)

            does = {"evict": evict, "sums": sums, "root": factors, "post": post, "meta_v": meta_v, "qT": qT, "score": score, "norm": norm,
                    "value": value, "meta_state": meta_state, "ra": ret_scores, "ro": ret_out,
                    "rn": ret_norm, "rm": ret_T, "hT": hid_T, "logit": logit}
            for kind, *args in STEPS:
                if kind in does:
                    does[kind](*args)

            dve.wait_ge(sq2, 2 * NT)
            step(tt(ms[:, 0:NT], ssq2[:, 0, :], ssq2[:, 1, :], ALU.add))
            step(ts(ms[:, 0:NT], ms[:, 0:NT], 1.0 / D, EPS, ALU.mult, ALU.add))
            step(nc.vector.tensor_copy(rstd2[:, :], inv_root(NT)))
            dve.sem_inc(rstd2_rdy, 1)
            dve.wait_ge(lg_ev, 2 * NT)
            step(tt(logits[:, :, :], logits[:, :, :], rstd2[:, :].unsqueeze(2).to_broadcast([P, NT, NG + NE]),
                    ALU.mult))

            gl = logits[:, :, 0:NG]
            col = lambda lo: small[:, lo:lo + NT]

            def wide(ap, n):
                return ap.unsqueeze(2).to_broadcast([P, NT, n])

            def first_of(oh_out, vals, top, n):
                c = cand[:, :, 0:n]
                step(tt(c, vals, wide(top, n), ALU.is_equal))
                step(tt(c, c, small[:, 100:100 + n].unsqueeze(1).to_broadcast([P, NT, n]), ALU.mult))
                step(red(col(120), c, AX_X, ALU.min))
                step(tt(oh_out, c, wide(col(120), n), ALU.is_equal))

            step(red(col(30), gl, AX_X, ALU.max))
            step(tt(r4[:, :, :], gl, wide(col(30), NG), ALU.subtract))
            dve.sem_inc(r_exp, 1)
            first_of(oh_g[:, :, :], gl, col(30), NG)
            e4 = logits[:, :, NG:].rearrange("p t (g e) -> p t g e", g=NG)
            step(tt(r32[:, :, :, :], e4, oh_g[:, :, :].unsqueeze(3).to_broadcast([P, NT, NG, EPG]), ALU.mult))
            step(red(el[:, :, :], r32[:, :, :, :].rearrange("p t g e -> p t e g"), AX_X, ALU.add))
            step(red(col(35), el[:, :, :], AX_X, ALU.max))
            first_of(oh_e[:, 0], el[:, :, :], col(35), EPG)
            step(stt(out=el2[:, :, :], in0=oh_e[:, 0], scalar=NEG, in1=el[:, :, :], op0=ALU.mult, op1=ALU.add))
            step(red(col(40), el2[:, :, :], AX_X, ALU.max))
            first_of(oh_e[:, 1], el2[:, :, :], col(40), EPG)
            step(tt(col(25), col(40), col(35), ALU.subtract))
            dve.sem_inc(r_exp, 1)
            for k in range(2):
                step(tt(oh[:, k].rearrange("p t (g e) -> p t g e", g=NG),
                        oh_e[:, k].unsqueeze(2).to_broadcast([P, NT, NG, EPG]),
                        oh_g[:, :, :].unsqueeze(3).to_broadcast([P, NT, NG, EPG]), ALU.mult))
            step(tt(chosen[:, :, :], oh[:, 0], oh[:, 1], ALU.add))
            step(nc.vector.memset(chosen[DEC:, TAIL, :].bitcast(F32), 0.0))
            dve.sem_inc(m_ready, 1)
            o2 = oh[:, :, :, :].rearrange("p k t (a b) -> p (k t) a b", b=2)
            step(tt(tmp_k[:, 0].rearrange("p t e -> p (t e)").rearrange("p (j a) -> p j a", a=NPAIR),
                    o2[:, :, :, 0], o2[:, :, :, 1], ALU.add))
            step(tt(pair_tok[:, :, :].rearrange("p (k t) a -> p k t a", k=2),
                    tmp_k[:, 0].rearrange("p t e -> p (t e)").rearrange("p (k t a) -> p k t a", k=2, t=NT),
                    const("token").unsqueeze(1).unsqueeze(3).to_broadcast([P, 2, NT, NPAIR]), ALU.mult))

            def pick(dst, values):
                step(tt(tmp_k[:, :, :, :], oh[:, :, :, :], values, ALU.mult))
                step(red(dst, tmp_k[:, :, :, :].rearrange("p k t e -> p (k t) e"), AX_X, ALU.add))

            def each(table):
                return const(table).unsqueeze(1).unsqueeze(1).to_broadcast([P, 2, NT, NE])

            pick(row_k[:, :], each("pair_row0"))
            pick(slot_f[:, :], each("expert_row0"))
            dve.wait_ge(rank_ps, 1)
            step(nc.vector.tensor_copy(rank[:, :, :], side3[:, 0:NE * NT].rearrange("p (t e) -> p t e", t=NT)))
            step(red(most[:, :], side3[:, NE * NT:NE * NT + NE], AX_X, ALU.max))
            step(nc.vector.tensor_copy(most_i[:, :], most[:, :]))
            pick(rank_k[:, :], rank[:, :, :].unsqueeze(1).to_broadcast([P, 2, NT, NE]))
            step(nc.vector.tensor_copy(slot_i[:, :], rank_k[:, :]))
            step(ts(slot_i[:, :], slot_i[:, :], CAP.bit_length() - 1, None, ALU.logical_shift_right))
            step(nc.vector.tensor_copy(lvl_a[:, :], slot_i[:, :]))
            step(tt(slot_f[:, :], slot_f[:, :], rank_k[:, :], ALU.add))
            step(stt(out=slot_f[:, :], in0=lvl_a[:, :], scalar=float((NE - 1) * CAP), in1=slot_f[:, :],
                     op0=ALU.mult, op1=ALU.add))
            step(nc.vector.tensor_copy(slot_i[:, :], slot_f[:, :]))
            step(tt(row_k[:, :], row_k[:, :], rank_k[:, :], ALU.add))
            step(nc.vector.memset(level0[:, :], 0.0))

            def rows_of_level(one):
                one(ts(lvl_a[:, :], rank_k[:, :], level0[:, 0:1], None, ALU.subtract))
                one(ts(lvl_b[:, :], lvl_a[:, :], float(CAP), 1000.0, ALU.is_ge, ALU.mult))
                one(ts(lvl_a[:, :], lvl_a[:, :], 0.0, 1000.0, ALU.is_lt, ALU.mult))
                one(tt(lvl_a[:, :], lvl_a[:, :], lvl_b[:, :], ALU.add))
                one(tt(lvl_a[:, :], lvl_a[:, :], row_k[:, :], ALU.add))
                one(ts(row_l[:, :], lvl_a[:, :], level0[:, 0:1], None, ALU.subtract))
                one(tt(row_oh[:, :, :], iota.unsqueeze(1).to_broadcast([P, 2 * NT, P]),
                       row_l[:, :].unsqueeze(2).to_broadcast([P, 2 * NT, P]), ALU.is_equal))

            rows_of_level(step)
            dve.sem_inc(oh_ready, 1)
            dve.wait_ge(r_expd, 2)
            step(red(col(50), r4b[:, :, :], AX_X, ALU.add))
            step(ts(col(55), col(20), 1.0, None, ALU.add))
            step(tt(col(50), col(50), col(55), ALU.mult))
            step(nc.vector.reciprocal(w_k[:, 0, :], col(50)))
            step(tt(w_k[:, 1, :], w_k[:, 0, :], col(20), ALU.mult))
            dve.wait_ge(idx_ps, 1)
            step(nc.vector.tensor_copy(idx[:, :], side3[:, 256:256 + NPAIR]))
            dve.sem_inc(slots_ready, 1)
            dve.sem_inc(idx_ready, 1)

            def rows_in(p, u, first):
                dve.wait_ge(xg_ps, p + 1)
                if not first:
                    dve.wait_ge(gu_ps, p - 1)
                tt(xgT[:, u], side[:, 0:2, :].rearrange("p b (j n) -> p (b j) n", j=4),
                   g2T.unsqueeze(2).to_broadcast([P, KD, P]), ALU.mult).then_inc(xg_ev, 1)

            def glu_steps(u, wait):
                tt(glu[:, 1, :], glu[:, 0, :], acc[:, u, 0:FF], ALU.mult).then_inc(glu_step, 1)
                dve.wait_ge(glu_step, wait + 1)
                return tt(actv[:, :], glu[:, 1, :], acc[:, u, FF:2 * FF], ALU.mult)

            def act_in(p, u, first):
                dve.wait_ge(e_exp, p + 1)
                if not first:
                    dve.wait_ge(aT_ps, p)
                glu_steps(u, p).then_inc(e_act, 1)

            def actT_in(p, first):
                dve.wait_ge(aT_ps, p + 1)
                if not first:
                    dve.wait_ge(y_ps, p)
                nc.vector.tensor_copy(actT[:, :, :], side3[:, 0:2 * P].rearrange("p (j n) -> p j n", j=2)
                                      ).then_inc(aT_ev, 1)

            rows_in(0, 0, True)
            rows_in(1, 1, True)
            act_in(0, 0, True)
            actT_in(0, True)
            with dve.Fori(1, NPAIR // 2) as i:
                rows_in(i * 2, 0, False)
                act_in(i * 2 - 1, 1, False)
                actT_in(i * 2 - 1, False)
                rows_in(i * 2 + 1, 1, False)
                act_in(i * 2, 0, False)
                actT_in(i * 2, False)
            act_in(NPAIR - 1, 1, False)
            actT_in(NPAIR - 1, False)

            n_most = dve.value_load(most_i[0:1, 0:1], min_val=0, max_val=T_TOK)
            with dve.If(n_most > CAP):
                for u in range(2):
                    dve.wait_ge(y_out[u], 8 * NPAIR)
                with dve.Fori(1, LEVELS) as lv:
                    dve.wait_ge(L_out, (lv - 1) * 16 * NPAIR + 16)
                    seen = [0]

                    def one(ins):
                        ins.then_inc(L_step, 1)
                        seen[0] += 1
                        dve.wait_ge(L_step, (lv - 1) * PER_LEVEL + seen[0])

                    one(ts(level0[:, :], level0[:, :], float(CAP), None, ALU.add))
                    rows_of_level(one)
                    assert seen[0] == PER_LEVEL
                    dve.sem_inc(L_oh, 1)
                    dve.wait_ge(L_ips, lv)
                    dve.wait_ge(L_xt, (lv - 1) * NPAIR + 1)
                    nc.vector.tensor_copy(idx[:, :], side3[:, 256:256 + NPAIR]).then_inc(L_idx, 1)
                    with dve.Fori(0, NPAIR) as p:
                        it = (lv - 1) * NPAIR + p
                        dve.wait_ge(L_xt, it + 2)
                        tt(xgT[:, 0], side[:, 0:2, :].rearrange("p b (j n) -> p (b j) n", j=4),
                           g2T.unsqueeze(2).to_broadcast([P, KD, P]), ALU.mult).then_inc(L_xe, 1)
                        dve.wait_ge(L_ex, it + 1)
                        glu_steps(0, NPAIR + it).then_inc(L_act, 1)
                        dve.wait_ge(L_at, it + 1)
                        nc.vector.tensor_copy(actT[:, :, :], side3[:, 0:2 * P].rearrange("p (j n) -> p j n", j=2)
                                              ).then_inc(L_ae, 1)

            for t in range(NT):
                R = out_rows(t)
                dve.wait_ge(yg_in[t], 32)
                for k in range(2):
                    step(stt(out=x_sb[0:R, t, :], in0=y_tok[0:R, t, k, :], scalar=w_k[0:R, k, t:t + 1],
                             in1=x_sb[0:R, t, :], op0=ALU.mult, op1=ALU.add))
                dve.sem_inc(y_fin, 1)


_INS = ["x_prompt", "x_sample", "cache_ret_state", "cache_swa_k", "cache_swa_v", "meta_tokens", "norm1_g",
        "w_in", "q_norm_g", "k_norm_g", "ret_norm_g", "attn_sinks", "w_out", "norm2_g", "w_group",
        "w_gate", "w_up", "w_down"]
_OUTS = [(1, SEQ, D), (1, DEC, D), (1, 1, RH, RDK, RDV), (1, 1, WINDOW, 2, HD), (1, 1, WINDOW, 2, HD),
         (1, 1, RH, RDK, RDV), (1, 1, WINDOW, 2, HD), (1, 1, WINDOW, 2, HD)]


def kernel(**inputs):
    import numpy as _np
    import concourse.bacc as _bacc
    from concourse import mybir as _mybir
    from concourse.bass_utils import run_bass_kernel_spmd as _run

    nc = _bacc.Bacc("TRN2", target_bir_lowering=False, num_devices=1)
    table, _ = constants()
    arrays, args = {"in_consts_dram": table}, []
    args.append(nc.dram_tensor("in_consts_dram", table.shape, _mybir.dt.float32, kind="ExternalInput").ap())
    for name in _INS:
        a = _np.ascontiguousarray(inputs[name])
        if name == "norm2_g":
            a = _np.stack([a.reshape(P, KD), a.reshape(KD, P).T], 1)
        if name == "w_group":
            a = _np.concatenate([a[0], _np.asarray(inputs["w_expert"])[0]], 1).reshape(KD, P, NG + NE)
            a = _np.ascontiguousarray(a.transpose(1, 0, 2))
        if name == "ret_norm_g":
            a = _np.ascontiguousarray(a.reshape(RH, RDV).T)
        arrays[f"in_{name}_dram"] = a
        args.append(nc.dram_tensor(f"in_{name}_dram", a.shape, _mybir.dt.from_np(a.dtype), kind="ExternalInput").ap())
    for i, shape in enumerate(_OUTS):
        args.append(nc.dram_tensor(f"out_{i}_dram", shape, _mybir.dt.float32, kind="ExternalOutput").ap())
    stream_step(nc, *args)
    r = _run(nc, [arrays], core_ids=[0])
    return tuple(r.results[0][f"out_{i}_dram"] for i in range(len(_OUTS)))
```
